# Optimizing a Trainium2 kernel written in Bass

```python
import math
import jax, jax.numpy as jnp
from jax import lax
import numpy as np

D_MODEL = 1024
BATCH = 1
SEQ = 512
DEPTH = 1
DEC_BATCH = 8
DEC_SEQ = 8
PAST_LEN = 4096
PAGE_SIZE = 128

N_META = 16
EPS = 1e-6
GLA_HEADS = 4
GLA_DK = 64
GLA_DV = 128
GLA_KW = GLA_HEADS * GLA_DK
GLA_VW = GLA_HEADS * GLA_DV
GLA_RANK = 16
GLA_TAU = 16.0
GLA_CHUNK = 16
SSD_HEADS = 8
SSD_HEADDIM = 64
SSD_INNER = SSD_HEADS * SSD_HEADDIM
SSD_GROUPS = 2
SSD_REP = SSD_HEADS // SSD_GROUPS
SSD_DSTATE = 128
SSD_CONV = 4
SSD_CHUNK = 64
CONV_DIM = SSD_INNER + 2 * SSD_GROUPS * SSD_DSTATE
MIX_WIDTH = GLA_VW + SSD_INNER
PEER_HEADS = 8
PEER_NKEYS = 128
PEER_EXPERTS = PEER_NKEYS * PEER_NKEYS
PEER_QDIM = 128
PEER_TOPK = 16
PEER_BLOCK = 256
IN_SPLITS = (GLA_KW, GLA_KW, GLA_VW, GLA_VW, GLA_RANK, SSD_INNER, CONV_DIM, SSD_HEADS)
IN_WIDTH = GLA_KW + GLA_KW + GLA_VW + GLA_VW + GLA_RANK + SSD_INNER + CONV_DIM + SSD_HEADS

kernel_name = 'hymba_gla_ssd_peer_decoder_step'

def rmsnorm(x, w):
    xf = x.astype(jnp.float32)
    y = xf * lax.rsqrt(jnp.mean(xf * xf, axis=-1, keepdims=True) + EPS)
    return (y * w.astype(jnp.float32)).astype(x.dtype)

def segments(seq_len, split):
    return [(0, split), (split, seq_len)] if split > 0 else [(0, seq_len)]

def gla_segment(q, k, v, gk, s0):
    bsz, seg_len = q.shape[0], q.shape[1]
    c = math.gcd(seg_len, GLA_CHUNK)
    n = seg_len // c
    q, k, v, gk = (t.reshape((bsz, n, c) + t.shape[2:]) for t in (q, k, v, gk))
    b = jnp.cumsum(gk, axis=2)
    causal = jnp.tril(jnp.ones((c, c), dtype=bool))[None, None, :, :, None, None]
    decay = jnp.exp(jnp.where(causal, b[:, :, :, None] - b[:, :, None], -jnp.inf))
    attn = jnp.sum(q[:, :, :, None] * decay * k[:, :, None], axis=-1)
    o_intra = jnp.einsum('bntsh,bnshe->bnthe', attn, v)
    b_last = b[:, :, -1]
    s_local = jnp.einsum('bnshd,bnshe->bnhde', k * jnp.exp(b_last[:, :, None] - b), v)

    def step(s, inp):
        bl, sl = inp
        return jnp.exp(bl)[..., None] * s + sl, s

    s_fin, s_start = lax.scan(step, s0, (jnp.moveaxis(b_last, 1, 0), jnp.moveaxis(s_local, 1, 0)))
    s_start = jnp.moveaxis(s_start, 0, 1)
    o_inter = jnp.einsum('bnthd,bnhde->bnthe', q * jnp.exp(b), s_start)
    o = (o_intra + o_inter).reshape((bsz, seg_len) + o_intra.shape[3:])
    return o, s_fin

def ssd_segment(x, dt, a, bm, cm, h0):
    bsz, seg_len = x.shape[0], x.shape[1]
    c = math.gcd(seg_len, SSD_CHUNK)
    n = seg_len // c
    x, dt, bm, cm = (t.reshape((bsz, n, c) + t.shape[2:]) for t in (x, dt, bm, cm))
    cum = jnp.cumsum(dt * a, axis=2)
    causal = jnp.tril(jnp.ones((c, c), dtype=bool))[None, None, :, :, None, None]
    lmat = jnp.exp(jnp.where(causal, cum[:, :, :, None] - cum[:, :, None], -jnp.inf))
    cb = jnp.einsum('bntgk,bnsgk->bntsg', cm, bm)
    m = cb[..., None] * lmat * dt[:, :, None]
    y_intra = jnp.einsum('bntsgr,bnsgrp->bntgrp', m, x)
    cum_last = cum[:, :, -1]
    xw = x * (jnp.exp(cum_last[:, :, None] - cum) * dt)[..., None]
    s_local = jnp.einsum('bnsgk,bnsgrp->bngrpk', bm, xw)

    def step(h, inp):
        cl, sl = inp
        return jnp.exp(cl)[..., None, None] * h + sl, h

    h_fin, h_start = lax.scan(step, h0, (jnp.moveaxis(cum_last, 1, 0), jnp.moveaxis(s_local, 1, 0)))
    h_start = jnp.moveaxis(h_start, 0, 1)
    y_inter = jnp.einsum('bntgk,bngrpk->bntgrp', cm, h_start) * jnp.exp(cum)[..., None]
    y = (y_intra + y_inter).reshape((bsz, seg_len) + y_intra.shape[3:])
    return y, h_fin

def causal_conv(xbc, buf, w, b):
    seq_len = xbc.shape[1]
    full = jnp.concatenate([buf.astype(xbc.dtype), xbc], axis=1)
    out = b + full[:, 0:seq_len] * w[0]
    for i in range(1, SSD_CONV):
        out = out + full[:, i:i + seq_len] * w[i]
    return out, full[:, -(SSD_CONV - 1):]

def token_mixers(xn, s_gla, s_ssm, s_conv, split, w_in, w_gk2, b_gk2, gla_norm_w,
                 conv_w, conv_b, dt_bias, a_log, d_skip, ssd_norm_w, w_out):
    f32 = jnp.float32
    bsz, seq_len, _ = xn.shape
    dtype = xn.dtype
    offs = np.cumsum(IN_SPLITS)[:-1].tolist()
    q, k, v, g, f_lr, z, xbc, dt_raw = jnp.split(xn @ w_in, offs, axis=-1)
    segs = segments(seq_len, split)
    q = (q.astype(f32) * GLA_DK ** -0.5).reshape(bsz, seq_len, GLA_HEADS, GLA_DK)
    k = k.astype(f32).reshape(bsz, seq_len, GLA_HEADS, GLA_DK)
    v = v.astype(f32).reshape(bsz, seq_len, GLA_HEADS, GLA_DV)
    gk = (jax.nn.log_sigmoid((f_lr @ w_gk2 + b_gk2).astype(f32)) / GLA_TAU).reshape(bsz, seq_len, GLA_HEADS, GLA_DK)
    s = s_gla.astype(f32)
    outs = []
    for lo, hi in segs:
        o, s = gla_segment(q[:, lo:hi], k[:, lo:hi], v[:, lo:hi], gk[:, lo:hi], s)
        outs.append(o)
    o = jnp.concatenate(outs, axis=1)
    o_gla = (rmsnorm(o, gla_norm_w) * jax.nn.silu(g.astype(f32)).reshape(bsz, seq_len, GLA_HEADS, GLA_DV)).reshape(bsz, seq_len, GLA_VW)
    xbc_c, new_conv = causal_conv(xbc, s_conv, conv_w, conv_b)
    xbc_c = jax.nn.silu(xbc_c.astype(f32))
    xs, bm, cm = jnp.split(xbc_c, [SSD_INNER, SSD_INNER + SSD_GROUPS * SSD_DSTATE], axis=-1)
    xs = xs.reshape(bsz, seq_len, SSD_GROUPS, SSD_REP, SSD_HEADDIM)
    bm = bm.reshape(bsz, seq_len, SSD_GROUPS, SSD_DSTATE)
    cm = cm.reshape(bsz, seq_len, SSD_GROUPS, SSD_DSTATE)
    dt = jax.nn.softplus(dt_raw.astype(f32) + dt_bias.astype(f32)).reshape(bsz, seq_len, SSD_GROUPS, SSD_REP)
    a = -jnp.exp(a_log.astype(f32)).reshape(SSD_GROUPS, SSD_REP)
    h = s_ssm.astype(f32).reshape(bsz, SSD_GROUPS, SSD_REP, SSD_HEADDIM, SSD_DSTATE)
    ys = []
    for lo, hi in segs:
        y, h = ssd_segment(xs[:, lo:hi], dt[:, lo:hi], a, bm[:, lo:hi], cm[:, lo:hi], h)
        ys.append(y)
    y = jnp.concatenate(ys, axis=1) + d_skip.astype(f32).reshape(SSD_GROUPS, SSD_REP)[..., None] * xs
    y = rmsnorm(y.reshape(bsz, seq_len, SSD_INNER) * jax.nn.silu(z.astype(f32)), ssd_norm_w)
    mix = jnp.concatenate([o_gla, y], axis=-1).astype(dtype)
    out = mix @ w_out
    new_ssm = h.reshape(bsz, SSD_HEADS, SSD_HEADDIM, SSD_DSTATE)
    return out, s.astype(s_gla.dtype), new_ssm.astype(s_ssm.dtype), new_conv.astype(s_conv.dtype)

def peer(xn, w_q, sub_k1, sub_k2, u, v):
    shape = xn.shape
    t = xn.reshape(-1, D_MODEL)
    n_tok = t.shape[0]
    q = (t @ w_q).astype(jnp.float32).reshape(n_tok, PEER_HEADS, 2, PEER_QDIM // 2)
    s1 = jnp.einsum('thd,kd->thk', q[:, :, 0], sub_k1.astype(jnp.float32))
    s2 = jnp.einsum('thd,kd->thk', q[:, :, 1], sub_k2.astype(jnp.float32))
    v1, i1 = lax.top_k(s1, PEER_TOPK)
    v2, i2 = lax.top_k(s2, PEER_TOPK)
    cand = (v1[..., :, None] + v2[..., None, :]).reshape(n_tok, PEER_HEADS, PEER_TOPK * PEER_TOPK)
    sc, ci = lax.top_k(cand, PEER_TOPK)
    e = (jnp.take_along_axis(i1, ci // PEER_TOPK, axis=-1) * PEER_NKEYS
         + jnp.take_along_axis(i2, ci % PEER_TOPK, axis=-1))
    gate = jax.nn.softmax(sc, axis=-1)
    e = e.reshape(n_tok, PEER_HEADS * PEER_TOPK)
    gate = gate.reshape(n_tok, PEER_HEADS * PEER_TOPK).astype(xn.dtype)
    pad = (-n_tok) % PEER_BLOCK
    tp = jnp.pad(t, ((0, pad), (0, 0))).reshape(-1, PEER_BLOCK, D_MODEL)
    ep = jnp.pad(e, ((0, pad), (0, 0))).reshape(-1, PEER_BLOCK, PEER_HEADS * PEER_TOPK)
    gp = jnp.pad(gate, ((0, pad), (0, 0))).reshape(-1, PEER_BLOCK, PEER_HEADS * PEER_TOPK)

    def blk(args):
        tb, eb, gb = args
        hid = jnp.einsum('tkd,td->tk', u[eb], tb)
        return jnp.einsum('tk,tkd->td', gb * jax.nn.gelu(hid), v[eb])

    out = lax.map(blk, (tp, ep, gp))
    return out.reshape(-1, D_MODEL)[:n_tok].reshape(shape)

def setup_inputs(seed: int = 0) -> dict:
    key = jax.random.key(seed)
    ks = jax.random.split(key, 32)
    f32 = jnp.float32

    def nrm(i, shape, s):
        return jax.random.normal(ks[i], shape, f32) * s

    dt0 = jnp.exp(jax.random.uniform(ks[10], (DEPTH, SSD_HEADS), f32, math.log(1e-3), math.log(1e-1)))
    return {
        'x_prompt': nrm(0, (BATCH, SEQ, D_MODEL), 1.0),
        'x_sample': nrm(1, (DEC_BATCH, DEC_SEQ, D_MODEL), 1.0),
        'state_gla': nrm(2, (DEPTH, DEC_BATCH, GLA_HEADS, GLA_DK, GLA_DV), 0.5),
        'state_ssm': nrm(3, (DEPTH, DEC_BATCH, SSD_HEADS, SSD_HEADDIM, SSD_DSTATE), 0.5),
        'state_conv': nrm(4, (DEPTH, DEC_BATCH, SSD_CONV - 1, CONV_DIM), 1.0),
        'meta_tokens': nrm(5, (N_META, D_MODEL), 1.0),
        'norm1_w': 1.0 + nrm(6, (DEPTH, D_MODEL), 0.02),
        'w_in': nrm(7, (DEPTH, D_MODEL, IN_WIDTH), D_MODEL ** -0.5),
        'w_gk2': nrm(8, (DEPTH, GLA_RANK, GLA_KW), GLA_RANK ** -0.5),
        'b_gk2': nrm(9, (DEPTH, GLA_KW), 0.01) + 1.0,
        'gla_norm_w': 1.0 + nrm(11, (DEPTH, GLA_DV), 0.02),
        'conv_w': nrm(12, (DEPTH, SSD_CONV, CONV_DIM), 0.5),
        'conv_b': nrm(13, (DEPTH, CONV_DIM), 0.01),
        'dt_bias': dt0 + jnp.log(-jnp.expm1(-dt0)),
        'a_log': jnp.log(jax.random.uniform(ks[14], (DEPTH, SSD_HEADS), f32, 1.0, 16.0)),
        'd_skip': 1.0 + nrm(15, (DEPTH, SSD_HEADS), 0.01),
        'ssd_norm_w': 1.0 + nrm(16, (DEPTH, SSD_INNER), 0.02),
        'w_out': nrm(17, (DEPTH, MIX_WIDTH, D_MODEL), MIX_WIDTH ** -0.5),
        'norm2_w': 1.0 + nrm(18, (DEPTH, D_MODEL), 0.02),
        'peer_wq': nrm(19, (DEPTH, D_MODEL, PEER_HEADS * PEER_QDIM), D_MODEL ** -0.5),
        'peer_k1': nrm(20, (DEPTH, PEER_NKEYS, PEER_QDIM // 2), (PEER_QDIM // 2) ** -0.5),
        'peer_k2': nrm(21, (DEPTH, PEER_NKEYS, PEER_QDIM // 2), (PEER_QDIM // 2) ** -0.5),
        'peer_u': nrm(22, (DEPTH, PEER_EXPERTS, D_MODEL), D_MODEL ** -0.5),
        'peer_v': nrm(23, (DEPTH, PEER_EXPERTS, D_MODEL), (PEER_HEADS * PEER_TOPK) ** -0.5),
        'final_norm_w': 1.0 + nrm(24, (D_MODEL,), 0.02),
    }

def reference(x_prompt, x_sample, state_gla, state_ssm, state_conv, meta_tokens, norm1_w, w_in,
              w_gk2, b_gk2, gla_norm_w, conv_w, conv_b, dt_bias, a_log, d_skip, ssd_norm_w, w_out,
              norm2_w, peer_wq, peer_k1, peer_k2, peer_u, peer_v, final_norm_w):
    dtype = x_prompt.dtype
    bp = x_prompt.shape[0]
    hp = jnp.concatenate([jnp.broadcast_to(meta_tokens[None].astype(dtype), (bp, N_META, D_MODEL)), x_prompt], axis=1)
    hs = x_sample
    gp = jnp.zeros((bp, GLA_HEADS, GLA_DK, GLA_DV), dtype)
    sp = jnp.zeros((bp, SSD_HEADS, SSD_HEADDIM, SSD_DSTATE), dtype)
    cp = jnp.zeros((bp, SSD_CONV - 1, CONV_DIM), dtype)

    def layer(h, sg, ss, sc, split, l):
        m, sg, ss, sc = token_mixers(rmsnorm(h, norm1_w[l]), sg, ss, sc, split, w_in[l], w_gk2[l], b_gk2[l],
                                     gla_norm_w[l], conv_w[l], conv_b[l], dt_bias[l], a_log[l], d_skip[l],
                                     ssd_norm_w[l], w_out[l])
        h = h + m
        h = h + peer(rmsnorm(h, norm2_w[l]), peer_wq[l], peer_k1[l], peer_k2[l], peer_u[l], peer_v[l])
        return h, sg, ss, sc

    gla_p, ssm_p, conv_p, gla_s, ssm_s, conv_s = [], [], [], [], [], []
    for l in range(DEPTH):
        hp, g1, s1, c1 = layer(hp, gp, sp, cp, N_META, l)
        hs, g2, s2, c2 = layer(hs, state_gla[l], state_ssm[l], state_conv[l], 0, l)
        gla_p.append(g1); ssm_p.append(s1); conv_p.append(c1)
        gla_s.append(g2); ssm_s.append(s2); conv_s.append(c2)
    y_prompt = rmsnorm(hp, final_norm_w)[:, N_META:]
    y_sample = rmsnorm(hs, final_norm_w)
    return (y_prompt, y_sample, jnp.stack(gla_p), jnp.stack(ssm_p), jnp.stack(conv_p),
            jnp.stack(gla_s), jnp.stack(ssm_s), jnp.stack(conv_s))


_drawn_inputs = setup_inputs


def setup_inputs(seed=0):
    import zlib

    import numpy as np

    out = dict(_drawn_inputs(seed))
    spreads = {}
    factors = {'b_gk2': 64.0,
     'gla_norm_w': 23.224,
     'conv_b': 2.945,
     'd_skip': 64.0,
     'ssd_norm_w': 14.642,
     'norm2_w': 28.099,
     'final_norm_w': 8.118,
     'w_gk2': 8.0}
    for name, (base, spread) in spreads.items():
        noise = np.random.default_rng([zlib.crc32(name.encode()), seed]).standard_normal(out[name].shape)
        drawn = base * np.exp(spread * noise) if base else spread * noise
        out[name] = __import__('jax').numpy.asarray(drawn.astype(out[name].dtype))
    for name, factor in factors.items():
        out[name] = (out[name] * factor).astype(out[name].dtype)
    return out
```

```python
from contextlib import ExitStack

import numpy as np
import concourse.bass as bass
from concourse import mybir

F32 = mybir.dt.float32
U32 = mybir.dt.uint32
ALU = mybir.AluOpType
ACT = mybir.ActivationFunctionType
AX = mybir.AxisListType

P = 128
D = 1024
KT = D // P
META, SEQ = 16, 512
NPROMPT = META + SEQ
NSEQ, SLEN = 8, 8
T = NPROMPT + NSEQ * SLEN
HALF = T // 2
TILES = 5
EPS = 1e-6
GH, DK, DV = 4, 64, 128
NP = GH // 2
RANK = 16
C = 16
SH, HD, DS, SG = 8, 64, 128, 2
CONV, CONVD = 4, 1024
CT = CONVD // P
PH, NK, QD, TOPK = 8, 128, 128, 16
XPW = (CONV - 1) + NPROMPT
XPS = CONV - 1 + SLEN
XP = XPW + NSEQ * XPS
N_FEAT = 20
N_PROJ = N_FEAT + KT + PH
GRP = 8
NGRP = NK // GRP
TB = 16
NBLK = T // TB
SEGS = 1 + NSEQ
CHUNKS = (TILES - 1) * (P // C) + SEGS
PROMPT_CHUNKS = NPROMPT // C


def rows(i):
    return P if i < TILES - 1 else T - P * (TILES - 1)


def cols(i):
    return slice(P * i, P * i + rows(i))


def seg_cols(r):
    return (0, META) if r == 0 else (META + SLEN * (r - 1), META + SLEN * r)


CONST_PARTS = [("ident", P), ("ones", P), ("incl_a", P), ("incl_b", P), ("suf_a", P), ("suf_b", P),
               ("tincl_a", P), ("tsuf_a", P), ("neg_a", P), ("neg_b", P), ("col_a", P // C), ("col_b", SEGS),
               ("head2", 2), ("iota", NK), ("iota16", TOPK)]


def offsets(parts):
    out, at = {}, 0
    for name, n in parts:
        out[name] = (at, at + n)
        at += n
    return out, at


CONST_AT, CONST_N = offsets(CONST_PARTS)
PARAM_PARTS = [("norm1", KT), ("norm2", KT), ("final", KT), ("gla_w", 1), ("ssd_w", 4), ("conv_w", CT * CONV),
               ("conv_b", CT), ("dskip", 4), ("a_log", SH)]
PARAM_AT, PARAM_N = offsets(PARAM_PARTS)


def constants():
    r = np.arange(P)
    seg_b = np.where(r < META, 0, 1 + (r - META) // SLEN)
    chunk_a = r // C
    le, gt = r[:, None] <= r[None, :], r[:, None] > r[None, :]
    same_a, same_b = chunk_a[:, None] == chunk_a[None, :], seg_b[:, None] == seg_b[None, :]
    parts = {
        "ident": np.eye(P), "ones": np.ones((P, P)),
        "incl_a": le & same_a, "incl_b": le & same_b, "suf_a": gt & same_a, "suf_b": gt & same_b,
        "tincl_a": le, "tsuf_a": gt,
        "neg_a": np.where(le, 0.0, -1e30), "neg_b": np.where(le & same_b, 0.0, -1e30),
        "col_a": chunk_a[:, None] == np.arange(P // C)[None, :],
        "col_b": seg_b[:, None] == np.arange(SEGS)[None, :],
        "head2": (r // DK)[:, None] == np.arange(2)[None, :],
        "iota": np.tile(np.arange(NK), (P, 1)), "iota16": np.tile(np.arange(TOPK), (P, 1)),
    }
    return np.concatenate([np.asarray(parts[n], np.float32) for n, _ in CONST_PARTS], axis=1)


def bc(ap, axis, n):
    ap = ap.unsqueeze(axis)
    shape = list(ap.shape)
    shape[axis] = n
    return ap.broadcast_to(shape)


def build(nc, d, o):
    base = ExitStack()
    with base:
        def sem(name):
            return base.enter_context(nc.semaphore(name))

        def sb(stack, name, shape, dt=F32):
            return stack.enter_context(nc.sbuf_tensor(name, shape, dt))

        gates_dram = nc.dram_tensor("gates_scratch", (NGRP, P, T, GRP), F32, kind="Internal").ap()

        h = sb(base, "h", [P, KT, T])
        xn = sb(base, "xn", [P, KT, T])
        ring = sb(base, "ring", [P, 4, D])
        cst = sb(base, "cst", [P, CONST_N])
        prm = sb(base, "prm", [P, PARAM_N])
        sq = sb(base, "sq", [P, 2, T])
        stat = sb(base, "stat", [P, 8, TILES])
        gstat = sb(base, "gstat", [P, 2, TILES * GH])

        def cc(name, r=P):
            a, b = CONST_AT[name]
            return cst[0:r, a:b]

        def pp(name):
            a, b = PARAM_AT[name]
            return prm[:, a:b]

        ident, ones = cc("ident"), cc("ones")
        bank = [base.enter_context(nc.psum_tensor(f"bank{n}", [P, 512], F32)) for n in range(8)]

        mix_stack = ExitStack()
        mix = sb(mix_stack, "mix", [P, 8, T])
        sg = sb(mix_stack, "sg", [P, 4, T])
        sz = sb(mix_stack, "sz", [P, 4, T])
        row = sb(mix_stack, "row", [1, GH * DK + SH])
        small = sb(mix_stack, "small", [P, KT, RANK + SH])
        wgk = sb(mix_stack, "wgk", [RANK, GH * DK])
        fl = sb(mix_stack, "fl", [RANK, T])
        dt = sb(mix_stack, "dt", [P, 4, TILES * SH])
        dta = sb(mix_stack, "dta", [P, TILES, SH])
        na = sb(mix_stack, "na", [P, SH])

        gla = ExitStack()
        qT = sb(gla, "qT", [P, NP, T])
        kT = sb(gla, "kT", [P, NP, T])
        bT = sb(gla, "bT", [P, NP, T])
        eb = sb(gla, "eb", [P, NP, T])
        qb = sb(gla, "qb", [P, NP, T])
        V = sb(gla, "V", [P, TILES, GH * DV])
        khat = sb(gla, "khat", [P, TILES, GH * DK])
        gk = sb(gla, "gk", [P, TILES, GH * DK])
        tmp = sb(gla, "tmp", [P, 2, TILES, GH * DK])
        E = sb(gla, "E", [P, 2, P // C * C * C])
        MT = sb(gla, "MT", [P, TILES, GH * P])
        tmpf = tmp[:, :, :, :].rearrange("p a b c -> p (a b c)")
        khm = [sb(gla, "khm", [P, SEGS, GH * DK])[:, :, :],
               tmpf[:, 0:SEGS * GH * DK].rearrange("p (c n) -> p c n", c=SEGS)]
        S = sb(gla, "S", [P, 2, NP, DV])
        Ssm = sb(gla, "Ssm", [P, NSEQ, NP, DV])
        gla.close()
        Ef = E[:, :, :].rearrange("p a b -> p (a b)")
        wv_sb = Ef[:, 0:KT * GH * DV].rearrange("p (k n) -> p k n", k=KT)
        gsq = Ef[:, 0:GH * T].rearrange("p (h t) -> p h t", h=GH)

        ssd = ExitStack()
        xp = sb(ssd, "xp", [P, CT, XP])
        xc = sb(ssd, "xc", [P, CT, T])
        xtok = sb(ssd, "xtok", [P, TILES, SH * HD])
        btok = sb(ssd, "btok", [P, TILES, SG * DS])
        ecb = sb(ssd, "ecb", [P, SH, P])
        L = sb(ssd, "L", [P, SH, P])
        Ct = sb(ssd, "Ct", [P, SH, P])
        Xd = sb(ssd, "Xd", [P, SH * HD])
        XW = sb(ssd, "XW", [P, SH * HD])
        XWm = sb(ssd, "XWm", [P, 2, SH * HD])
        cum = sb(ssd, "cum", [P, 3, SH])
        H = sb(ssd, "H", [P, 2, SH * HD])
        Hsm = sb(ssd, "Hsm", [P, NSEQ, SH * HD])
        ssd.close()
        mix_stack.close()

        rt = ExitStack()
        e1T = sb(rt, "e1T", [P, T])
        e2T = sb(rt, "e2T", [P, T])
        gT = sb(rt, "gT", [P, T])
        oneA = sb(rt, "oneA", [P, 2, TB, NK])
        oneB = sb(rt, "oneB", [P, 2, TB, NK])
        stage = sb(rt, "stage", [P, 2, NGRP, TB, GRP])
        rt2 = ExitStack()
        qh = sb(rt2, "qh", [P, PH, T])
        keys = sb(rt2, "keys", [P, NK])
        s12 = sb(rt2, "s12", [P, 2 * PH, NK])
        rep = sb(rt2, "rep", [P, 2, 2 * NK])
        v16 = sb(rt2, "v16", [P, 3, PH, TOPK])
        i16 = sb(rt2, "i16", [P, 3, PH, TOPK], U32)
        j16 = sb(rt2, "j16", [P, 2, PH, TOPK], U32)
        f16 = sb(rt2, "f16", [P, 4, PH, TOPK])
        cand = sb(rt2, "cand", [P, TOPK * TOPK])
        pick = sb(rt2, "pick", [P, PH, TOPK, TOPK])
        e12 = sb(rt2, "e12", [P, 3, PH, TOPK])
        den = sb(rt2, "den", [P, 2, PH])
        rt2.close()
        rt.close()

        ex = ExitStack()
        vbuf = sb(ex, "vbuf", [P, 2, GRP, D])
        G = sb(ex, "G", [P, 2, T, GRP])
        W = sb(ex, "W", [P, 2, GRP, T])
        ex.close()

        x_loaded, const_loaded, small_loaded, wv_loaded, sgla_loaded = map(
            sem, ["x_loaded", "const_loaded", "small_loaded", "wv_loaded", "sgla_loaded"])
        hist_loaded, hsm_loaded, keys_loaded = map(sem, ["hist_loaded", "hsm_loaded", "keys_loaded"])
        w_loaded = [sem(f"w_loaded{s}") for s in range(4)]
        u_loaded = [sem(f"u_loaded{s}") for s in range(4)]
        v_loaded = [sem(f"v_loaded{s}") for s in range(2)]
        g_loaded = [sem(f"g_loaded{s}") for s in range(2)]
        stored = sem("stored")
        proj_done, proj_act, proj_dve = map(sem, ["proj_done", "proj_act", "proj_dve"])
        sq_ready, sq_used, sum_done, var_ready, root_ready, rstd_ready, bc_done, normed = (
            [sem(f"{n}{m}") for m in range(4)] for n in
            ["sq_ready", "sq_used", "sum_done", "var_ready", "root_ready", "rstd_ready", "bc_done", "normed"])
        fl_done, fl_copied, dtl_done, dtl_copied, dt_step, dt_ready, a_exp = map(
            sem, ["fl_done", "fl_copied", "dtl_done", "dtl_copied", "dt_step", "dt_ready", "a_exp"])
        gk_done, gk_copied, gk_step, gk_ready, v_done, v_copied = map(
            sem, ["gk_done", "gk_copied", "gk_step", "gk_ready", "v_done", "v_copied"])
        b_done, b_copied, eb_ready, suf_done, suf_exp, ktok_done, khat_ready, qb_ready = map(
            sem, ["b_done", "b_copied", "eb_ready", "suf_done", "suf_exp", "ktok_done", "khat_ready", "qb_ready"])
        e_arg, e_exp, e_q, e_k, attn_used, attn_done, mt_ready, khm_ready = map(
            sem, ["e_arg", "e_exp", "e_q", "e_k", "attn_used", "attn_done", "mt_ready", "khm_ready"])
        s_zero, local_done, s_updated, inter_done, o_done, o_copied = map(
            sem, ["s_zero", "local_done", "s_updated", "inter_done", "o_done", "o_copied"])
        gsq_ready, gsum_done, gvar_ready, groot_ready, grstd_ready, gbc_done, g_normed, g_mixed = map(
            sem, ["gsq_ready", "gsum_done", "gvar_ready", "groot_ready", "grstd_ready", "gbc_done", "g_normed", "g_mixed"])
        xp_zero, conv_done, xc_ready, tr_done, tr_copied = map(
            sem, ["xp_zero", "conv_done", "xc_ready", "tr_done", "tr_copied"])
        pre_done, ecb_ready, wx_ready, ncum_ready, z_ready, l_exp, m_ready, ct_ready, xw_ready = map(
            sem, ["pre_done", "ecb_ready", "wx_ready", "ncum_ready", "z_ready", "l_exp", "m_ready", "ct_ready", "xw_ready"])
        y_done, y_copied, hloc_done, h_updated, xwm_ready, yz_ready = map(
            sem, ["y_done", "y_copied", "hloc_done", "h_updated", "xwm_ready", "yz_ready"])
        score_done, score_copied, top_sorted, sm_arg, sm_exp, pick_in, pick_mul, e_ready, e_turned, e_copied = map(
            sem, ["score_done", "score_copied", "top_sorted", "sm_arg", "sm_exp", "pick_in", "pick_mul", "e_ready", "e_turned", "e_copied"])
        one_hot_ready, gate_done, gate_copied = map(
            sem, ["one_hot_ready", "gate_done", "gate_copied"])
        gate_stored = [sem(f"gate_stored{x}") for x in range(2)]
        hid_done, gelu_ready, w_ready, v_used, acc_done, acc_added = map(
            sem, ["hid_done", "gelu_ready", "w_ready", "v_used", "acc_done", "acc_added"])
        chain, achain = sem("chain"), sem("achain")

        def proj_dst_is_dve(n):
            return N_FEAT <= n < N_FEAT + KT

        def wait_gates_stored(eng):
            eng.wait_ge(gate_stored[0], 16 * (NBLK - NBLK // 2))
            eng.wait_ge(gate_stored[1], 16 * (NBLK // 2))

        def xtok3(i):
            return xtok[0:rows(i), i, :].rearrange("p (h q) -> p h q", h=SH)

        def attn_matrix(dve, i):
            r, nch = rows(i), rows(i) // C
            dve.wait_ge(attn_used, 2 * i + 2)
            dve.tensor_tensor(MT[0:r, i, :].rearrange("p (h c t) -> p h c t", h=GH, t=C)[:, :, 0:nch, :],
                              bc(bank[i % 2][0:r, 0:GH * C].rearrange("p (h t) -> p h t", h=GH), 2, nch),
                              bc(cc("incl_a" if i < 4 else "incl_b", r)[:, 0:r].rearrange("p (c t) -> p c t", t=C), 1, GH),
                              ALU.mult).then_inc(mt_ready, 1)

        def wait_proj_evacuated(eng, n):
            m = n - 2
            if m < 0:
                return
            if proj_dst_is_dve(m):
                eng.wait_ge(proj_dve, m - N_FEAT + 1)
            else:
                eng.wait_ge(proj_act, m + 1 - (KT if m >= N_FEAT + KT else 0))

        norm_src = [(h, KT), (mix, 4), (h, KT), (h, KT)]
        norm_par = ["norm1", "ssd_w", "norm2", "final"]

        block = base.enter_context(nc.Block())

        @block.sync
        def _(sp):
            for k in range(KT):
                sp.dma_start(h[:, k, :], d["xT"][:, k, :]).then_inc(x_loaded, 16)
            sp.dma_start(cst[:, :], d["const"]).then_inc(const_loaded, 16)
            sp.dma_start(prm[:, :], d["param"]).then_inc(const_loaded, 16)
            sp.dma_start(row[:, :], d["rows"]).then_inc(small_loaded, 16)
            sp.dma_start(small[:, :, :], d["wsmall"]).then_inc(small_loaded, 16)
            sp.dma_start(wgk[:, :], d["w_gk2"]).then_inc(small_loaded, 16)
            sp.dma_start(wv_sb, d["wv"]).then_inc(wv_loaded, 16)

            def load_w(n):
                if n >= 4:
                    sp.wait_ge(proj_done, n - 3)
                sp.dma_start(ring[:, n % 4, :], d["wproj"][n]).then_inc(w_loaded[n % 4], 16)

            for n in range(12):
                load_w(n)
            sp.dma_start(Ssm[:, :, :, :], d["s_gla"]).then_inc(sgla_loaded, 16)
            for n in range(12, N_FEAT):
                if n == 12:
                    sp.wait_ge(s_updated, PROMPT_CHUNKS)
                    sp.dma_start(o["gla_p"], S[:, PROMPT_CHUNKS % 2, :, :]).then_inc(stored, 16)
                    sp.wait_ge(s_updated, CHUNKS)
                    sp.dma_start(o["gla_s"], Ssm[:, :, :, :]).then_inc(stored, 16)
                    sp.wait_ge(stored, 32)
                    sp.wait_ge(g_mixed, 4)
                    for f in range(CT):
                        sp.dma_start(xp[:, f, XPW:XP].rearrange("p (b t) -> p b t", b=NSEQ)[:, :, 0:CONV - 1],
                                     d["s_conv"][:, f, :, :]).then_inc(hist_loaded, 16)
                    sp.dma_start(Hsm[:, :, :], d["s_ssm"]).then_inc(hsm_loaded, 16)
                load_w(n)
            for n in range(N_FEAT, N_FEAT + 4):
                load_w(n)
            sp.wait_ge(proj_act, N_FEAT)
            sp.wait_ge(hist_loaded, 16 * CT)
            sp.dma_start(o["conv_p"], xp[:, :, XPW - (CONV - 1):XPW]).then_inc(stored, 16)
            for f in range(CT):
                sp.dma_start(o["conv_s"][:, f, :, :],
                             xp[:, f, XPW:XP].rearrange("p (b t) -> p b t", b=NSEQ)[:, :, SLEN:XPS]).then_inc(stored, 16)
            sp.wait_ge(h_updated, TILES)
            sp.dma_start(o["ssm_p"], H[:, TILES % 2, :]).then_inc(stored, 16)
            sp.wait_ge(h_updated, TILES + NSEQ)
            sp.dma_start(o["ssm_s"], Hsm[:, :, :]).then_inc(stored, 16)
            sp.wait_ge(stored, 16 * (2 + 1 + CT + 2))
            for n in range(N_FEAT + 4, N_PROJ):
                load_w(n)
                if n == N_FEAT + KT + 4:
                    sp.wait_ge(proj_done, N_FEAT + KT)
                    sp.dma_start(keys[:, :], d["keys"]).then_inc(keys_loaded, 16)
            with sp.Fori(0, NBLK // 2) as pair:
                b = pair * 2
                for x in range(2):
                    sp.wait_ge(gate_copied, (b + x + 1) * (TB // 4))
                    sp.dma_start(gates_dram[:, :, bass.ds((b + x) * TB, TB), :].rearrange("g p t j -> p g (t j)"),
                                 stage[:, x, :, :, :].rearrange("p g t j -> p g (t j)")).then_inc(gate_stored[x], 16)
            sp.wait_ge(gate_copied, NBLK * (TB // 4))
            sp.dma_start(gates_dram[:, :, T - TB:T, :].rearrange("g p t j -> p g (t j)"),
                         stage[:, (NBLK - 1) % 2, :, :, :].rearrange("p g t j -> p g (t j)")).then_inc(gate_stored[0], 16)
            wait_gates_stored(sp)

            def load_group(g, x, first=False):
                if not first:
                    sp.wait_ge(w_ready, (g - 1) * GRP)
                sp.dma_start(G[:, x, :, :], gates_dram[bass.ds(g, 1), :, :, :].rearrange("a p t j -> p (a t) j")
                             ).then_inc(g_loaded[x], 16)
                for j in range(GRP):
                    if j == 4:
                        if not first:
                            sp.wait_ge(acc_done, (g - 1) * KT)
                        sp.dma_start(vbuf[:, x, :, :], d["v"][:, bass.ds(g, 1), :, :].rearrange("p a j n -> p (a j) n")
                                     ).then_inc(v_loaded[x], 16)
                    if not (first and g == 0 and j < 4):
                        sp.wait_ge(hid_done, g * GRP + j - 3)
                    sp.dma_start(ring[:, j % 4, :], d["u"][bass.ds(g * GRP + j, 1), :, :].rearrange("a p n -> p (a n)")
                                 ).then_inc(u_loaded[j % 4], 16)

            load_group(0, 0, first=True)
            load_group(1, 1, first=True)
            with sp.Fori(1, NGRP // 2) as pair:
                g = pair * 2
                load_group(g, 0)
                load_group(g + 1, 1)
            for k in range(KT):
                sp.wait_ge(normed[3], k + 1)
                sp.dma_start(o["yT"][:, k, :], xn[:, k, :]).then_inc(stored, 16)
            sp.wait_ge(stored, 16 * (2 + 1 + CT + 2 + KT))

        @block.tensor
        def _(pe):
            def norm(m):
                _, n = norm_src[m]
                for k in range(n):
                    pe.wait_ge(sq_ready[m], k + 1)
                    for i in range(TILES):
                        mm = pe.matmul(bank[4][0:rows(i), i:i + 1], sq[:, k % 2, cols(i)], ones[:, 0:1],
                                       start=(k == 0 and i == 0), stop=(k == n - 1), skip_group_check=True)
                    mm.then_inc(sq_used[m], 1)
                pe.wait_ge(rstd_ready[m], 1)
                for i in range(TILES):
                    out = bank[6][:, cols(i)] if i < 4 else bank[7][:, 0:rows(i)]
                    mm = pe.matmul(out, stat[0:rows(i), 2 * m + 1, i:i + 1].broadcast_to([rows(i), P]),
                                   ident[0:rows(i), 0:rows(i)], start=True, stop=True)
                mm.then_inc(bc_done[m], 1)

            def project(n, src, src_ready=None):
                pe.wait_ge(w_loaded[n % 4], 16 * (n // 4 + 1))
                wait_proj_evacuated(pe, n)
                for x in range(2):
                    for k in range(KT):
                        mm = pe.matmul(bank[2 * (n % 2) + x][:, 0:HALF], ring[:, n % 4, k * P:(k + 1) * P],
                                       src[:, k, x * HALF:(x + 1) * HALF], start=(k == 0), stop=(k == KT - 1))
                mm.then_inc(proj_done, 1)

            pe.wait_ge(const_loaded, 32)
            norm(0)
            pe.wait_ge(normed[0], KT)
            pe.wait_ge(small_loaded, 48)
            for x in range(2):
                for k in range(KT):
                    mm = pe.matmul(bank[x][0:RANK, 0:HALF], small[:, k, 0:RANK], xn[:, k, x * HALF:(x + 1) * HALF],
                                   start=(k == 0), stop=(k == KT - 1))
            mm.then_inc(fl_done, 1)
            for i in range(TILES):
                out = bank[5][0:rows(i), SH * i:SH * i + SH]
                for k in range(KT):
                    pe.matmul(out, xn[:, k, cols(i)], small[:, k, RANK:RANK + SH], start=(k == 0), stop=False)
                mm = pe.matmul(out, ones[0:1, 0:rows(i)], row[0:1, GH * DK:GH * DK + SH], start=False, stop=True)
            mm.then_inc(dtl_done, 1)
            pe.wait_ge(fl_copied, 2)
            for i in range(TILES):
                out = bank[6 + i % 2][0:rows(i), 0:GH * DK]
                if i >= 2:
                    pe.wait_ge(gk_copied, i - 1)
                pe.matmul(out, fl[:, cols(i)], wgk[:, :], start=True, stop=False)
                pe.matmul(out, ones[0:1, 0:rows(i)], row[0:1, 0:GH * DK], start=False, stop=True).then_inc(gk_done, 1)
            pe.wait_ge(wv_loaded, 16)
            for i in range(TILES):
                if i >= 2:
                    pe.wait_ge(v_copied, i - 1)
                for k in range(KT):
                    mm = pe.matmul(bank[2 + i % 2][0:rows(i), :], xn[:, k, cols(i)], wv_sb[:, k, :],
                                   start=(k == 0), stop=(k == KT - 1))
                mm.then_inc(v_done, 1)
            pe.wait_ge(gk_ready, 1)
            pe.wait_ge(dtl_copied, 1)
            for p in range(NP):
                for i in range(TILES):
                    out = bank[4 + p][:, cols(i)] if i < 4 else bank[6][:, p * P:p * P + rows(i)]
                    mm = pe.matmul(out, gk[0:rows(i), i, p * P:(p + 1) * P],
                                   cc("incl_a" if i < 4 else "incl_b", rows(i))[:, 0:rows(i)], start=True, stop=True)
            mm.then_inc(b_done, 1)
            for i in range(TILES):
                out = [bank[7][:, 0:256], bank[7][:, 256:512], bank[0][:, 0:256], bank[0][:, 256:512],
                       bank[1][0:rows(4), 0:256]][i]
                mm = pe.matmul(out, cc("suf_a" if i < 4 else "suf_b", rows(i))[:, 0:rows(i)], gk[0:rows(i), i, :],
                               start=True, stop=True)
            mm.then_inc(suf_done, 1)
            pe.wait_ge(v_copied, TILES)
            pe.wait_ge(suf_exp, 3)
            for n in range(4):
                project(n, xn)
            pe.wait_ge(b_copied, 4)
            pe.wait_ge(proj_act, 4)
            for i in range(TILES):
                for p in range(NP):
                    mm = pe.transpose(bank[4 + i // 2][0:rows(i), (i % 2) * 256 + p * P:(i % 2) * 256 + (p + 1) * P],
                                      kT[:, p, cols(i)], ident)
            mm.then_inc(ktok_done, 1)
            for n in range(4, 12):
                project(n, xn)
            pe.wait_ge(proj_act, 12)
            for i in range(TILES):
                if i >= 2:
                    pe.wait_ge(mt_ready, i - 1)
                for p in range(NP):
                    u = 2 * i + p
                    pe.wait_ge(e_k, u + 1)
                    src = E[:, u % 2, 0:rows(i) * C].rearrange("p (t n) -> p t n", t=C)
                    for t in range(C):
                        out = bank[i % 2][0:rows(i), p * 2 * C + t:p * 2 * C + C + t + 1:C]
                        mm = pe.matmul(out, src[:, t, :], cc("head2"), start=True, stop=True)
                    mm.then_inc(attn_used, 1)
            pe.wait_ge(khat_ready, 1)
            n = 0
            for i in range(TILES):
                r = rows(i)
                ob = [bank[(2, 6)[i % 2] + x] for x in range(2)]
                pe.wait_ge(mt_ready, i + 1)
                pe.wait_ge(khm_ready, i + 1)
                if i >= 2:
                    pe.wait_ge(o_copied, i - 1)
                for hh in range(GH):
                    pe.matmul(ob[hh % 2][:, hh // 2 * P:hh // 2 * P + r], V[0:r, i, hh * DV:(hh + 1) * DV], MT[0:r, i, hh * P:hh * P + r],
                              start=(hh < 2), stop=True, skip_group_check=True)
                for c in range(P // C if i < 4 else SEGS):
                    a, b = (c * C, c * C + C) if i < 4 else seg_cols(c)
                    if n >= 2:
                        pe.wait_ge(s_updated, n - 1)
                    for hh in range(GH):
                        q = (hh % 2) * DK
                        mm = pe.matmul(bank[4 + n % 2][q:q + DK, (hh // 2) * P:(hh // 2) * P + DV],
                                       khm[i % 2][0:r, c, hh * DK:(hh + 1) * DK], V[0:r, i, hh * DV:(hh + 1) * DV],
                                       start=True, stop=True)
                    mm.then_inc(local_done, 1)
                    sample = i == 4 and c > 0
                    if sample:
                        pe.wait_ge(sgla_loaded, 16)
                    elif n == 0:
                        pe.wait_ge(s_zero, 1)
                    else:
                        pe.wait_ge(s_updated, n)
                    for hh in range(GH):
                        q = (hh % 2) * DK
                        src = Ssm[q:q + DK, c - 1, hh // 2, :] if sample else S[q:q + DK, n % 2, hh // 2, :]
                        mm = pe.matmul(ob[hh % 2][:, hh // 2 * P + a:hh // 2 * P + b], src, qb[q:q + DK, hh // 2, P * i + a:P * i + b],
                                       start=False, stop=True, skip_group_check=True)
                    mm.then_inc(inter_done, 1)
                    n += 1
            pe.wait_ge(gsq_ready, 1)
            pe.wait_ge(s_updated, CHUNKS)
            for i in range(TILES):
                for hh in range(GH):
                    mm = pe.matmul(bank[4][0:rows(i), i * GH + hh:i * GH + hh + 1], gsq[:, hh, cols(i)], ones[:, 0:1],
                                   start=True, stop=True)
            mm.then_inc(gsum_done, 1)
            pe.wait_ge(grstd_ready, 1)
            for hh in range(GH):
                for i in range(TILES):
                    out = bank[hh][:, cols(i)] if i < 4 else bank[5][:, hh * P:hh * P + rows(i)]
                    mm = pe.matmul(out, gstat[0:rows(i), 1, i * GH + hh:i * GH + hh + 1].broadcast_to([rows(i), P]),
                                   ident[0:rows(i), 0:rows(i)], start=True, stop=True)
            mm.then_inc(gbc_done, 1)
            pe.wait_ge(g_normed, 8)
            for n in range(12, N_FEAT):
                project(n, xn)
            pe.wait_ge(proj_act, N_FEAT)
            pe.wait_ge(xc_ready, 6)
            for i in range(TILES):
                if i >= 2:
                    pe.wait_ge(tr_copied, 2 * (i - 1))
                for f in range(6):
                    out = bank[4 + i % 2][0:rows(i), f * P:(f + 1) * P] if f < 4 else \
                        bank[6 + i % 2][0:rows(i), (f - 4) * P:(f - 3) * P]
                    mm = pe.transpose(out, xc[:, f, cols(i)], ident)
                mm.then_inc(tr_done, 1)
            pe.wait_ge(xc_ready, CT)
            pe.wait_ge(dt_ready, 1)
            pe.wait_ge(tr_copied, 2 * TILES)
            for i in range(TILES):
                r = rows(i)
                incl = cc("tincl_a" if i < 4 else "incl_b", r)[:, 0:r]
                suf = cc("tsuf_a" if i < 4 else "suf_b", r)[:, 0:r]
                if i >= 1:
                    pe.wait_ge(z_ready, i)
                    pe.wait_ge(ecb_ready, i)
                    pe.wait_ge(wx_ready, i)
                    pe.wait_ge(ncum_ready, i)
                    pe.wait_ge(m_ready, i)
                for hh in range(SH):
                    pe.matmul(bank[hh // 4][:, (hh % 4) * P:(hh % 4) * P + r],
                              dta[0:r, i, hh:hh + 1].broadcast_to([r, P]), incl, start=True, stop=True)
                pe.matmul(bank[3][0:r, 0:SH], incl, dta[0:r, i, :], start=True, stop=True)
                pe.matmul(bank[3][0:r, SH:2 * SH], suf, dta[0:r, i, :], start=True, stop=True)
                for g in range(SG):
                    mm = pe.matmul(bank[2][0:r, g * P:g * P + r], xc[:, 4 + g, cols(i)], xc[:, 6 + g, cols(i)],
                                   start=True, stop=True)
                mm.then_inc(pre_done, 1)
                pe.wait_ge(m_ready, i + 1)
                pe.wait_ge(ct_ready, i + 1)
                pe.wait_ge(xw_ready, i + 1)
                if i >= 1:
                    pe.wait_ge(y_copied, i)
                    pe.wait_ge(h_updated, i)
                else:
                    pe.wait_ge(s_zero, 2)
                if i == 4:
                    pe.wait_ge(hsm_loaded, 16)
                for hh in range(SH):
                    q = (hh % 2) * HD
                    out = bank[4][q:q + HD, (hh // 2) * P:(hh // 2) * P + r]
                    pe.matmul(out, Xd[0:r, hh * HD:(hh + 1) * HD], L[0:r, hh, 0:r], start=True, stop=(i == 4))
                    if i < 4:
                        mm = pe.matmul(out, H[:, i % 2, hh * HD:(hh + 1) * HD], Ct[:, hh, :], start=False, stop=True)
                    else:
                        for c in range(SEGS):
                            a, b = seg_cols(c)
                            src = H[:, i % 2, hh * HD:(hh + 1) * HD] if c == 0 else Hsm[:, c - 1, hh * HD:(hh + 1) * HD]
                            mm = pe.matmul(out[:, a:b], src, Ct[:, hh, a:b], start=False, stop=True,
                                           skip_group_check=True)
                mm.then_inc(y_done, 1)
                for c in range(1 if i < 4 else SEGS):
                    if i == 4:
                        pe.wait_ge(xwm_ready, c + 1)
                        if c >= 1:
                            pe.wait_ge(h_updated, i + c)
                    src = XW[0:r, :] if i < 4 else XWm[0:r, c % 2, :]
                    for g in range(SG):
                        mm = pe.matmul(bank[5][:, g * 256:(g + 1) * 256], btok[0:r, i, g * DS:(g + 1) * DS],
                                       src[:, g * 256:(g + 1) * 256], start=True, stop=True)
                    mm.then_inc(hloc_done, 1)
            pe.wait_ge(h_updated, TILES + NSEQ)
            norm(1)
            pe.wait_ge(normed[1], 4)
            for n in range(N_FEAT, N_FEAT + KT):
                project(n, mix)
            norm(2)
            pe.wait_ge(normed[2], KT)
            for n in range(N_FEAT + KT, N_PROJ):
                project(n, xn)
            pe.wait_ge(proj_act, N_PROJ - KT)
            pe.wait_ge(keys_loaded, 16)

            def turn_picks(i):
                pe.wait_ge(e_ready, i + 1)
                if i >= 1:
                    pe.wait_ge(e_copied, i)
                for x in range(3):
                    mm = pe.transpose(bank[0][:, x * P:x * P + rows(i)], e12[0:rows(i), x, :, :].rearrange("p h k -> p (h k)"),
                                      ident[0:rows(i), 0:rows(i)])
                mm.then_inc(e_turned, 1)

            for i in range(TILES):
                if i >= 1:
                    pe.wait_ge(score_copied, 4 * i)
                for half in range(2):
                    for hh in range(PH):
                        q = half * 64
                        mm = pe.matmul(bank[4 + 2 * half + hh // 4][0:rows(i), (hh % 4) * NK:(hh % 4 + 1) * NK],
                                       qh[q:q + 64, hh, cols(i)], keys[q:q + 64, :], start=True, stop=True)
                mm.then_inc(score_done, 1)
                if i >= 1:
                    turn_picks(i - 1)
            turn_picks(TILES - 1)
            pe.wait_ge(e_copied, TILES)

            def gate_block(b, x, first=False):
                pe.wait_ge(one_hot_ready, b + 1)
                for q in range(TB // 4):
                    if not first or q >= 4:
                        pe.wait_ge(gate_copied, b * (TB // 4) + q - 3)
                    for t in range(4):
                        mm = pe.matmul(bank[q % 4][:, t * NK:(t + 1) * NK], oneA[:, x, 4 * q + t, :],
                                       oneB[:, x, 4 * q + t, :], start=True, stop=True)
                    mm.then_inc(gate_done, 1)

            gate_block(0, 0, first=True)
            with pe.Fori(0, NBLK // 2) as pair:
                b = pair * 2 + 1
                gate_block(b, 1)
                gate_block(b + 1, 0)

            pe.wait_ge(gate_copied, NBLK * (TB // 4))

            def hidden(g, j, first=False):
                x = j % 2
                pe.wait_ge(u_loaded[j % 4], 16 * (2 * g + j // 4 + 1))
                if not first:
                    pe.wait_ge(gelu_ready, g * GRP + j - 1)
                for y in range(2):
                    for k in range(KT):
                        mm = pe.matmul(bank[2 * x + y][:, 0:HALF], ring[:, j % 4, k * P:(k + 1) * P],
                                       xn[:, k, y * HALF:(y + 1) * HALF], start=(k == 0), stop=(k == KT - 1))
                mm.then_inc(hid_done, 1)

            def second(g, par, k, first=False):
                x = k % 2
                if k == 0:
                    pe.wait_ge(v_loaded[par], 16 * (g // 2 + 1) if isinstance(g, int) else 8 * (g - par) + 16)
                    pe.wait_ge(w_ready, (g + 1) * GRP)
                if not (first and k < 2):
                    pe.wait_ge(acc_added, g * KT + k - 1)
                for y in range(2):
                    for j in range(GRP):
                        mm = pe.matmul(bank[4 + 2 * x + y][:, 0:HALF], vbuf[:, par, j, k * P:(k + 1) * P],
                                       W[:, par, j, y * HALF:(y + 1) * HALF], start=(j == 0), stop=(j == GRP - 1))
                mm.then_inc(acc_done, 1)

            for j in range(GRP):
                hidden(0, j, first=(j < 2))
            hidden(1, 0)
            second(0, 0, 0, first=True)
            for j in range(1, GRP):
                hidden(1, j)
                second(0, 0, j, first=True)
            with pe.Fori(1, NGRP // 2) as pair:
                g = pair * 2
                for y in range(2):
                    for j in range(GRP):
                        hidden(g + y, j)
                        second(g + (y - 1), 1 - y, j)
            for k in range(KT):
                second(NGRP - 1, 1, k)
            norm(3)

        @block.scalar
        def _(act):
            linked = [0]

            def link(ins):
                linked[0] += 1
                ins.then_inc(achain, 1)
                act.wait_ge(achain, linked[0])

            def norm(m):
                src, n = norm_src[m]
                off = 4 if m == 1 else 0
                for k in range(n):
                    if k >= 2:
                        act.wait_ge(sq_used[m], k - 1)
                    act.activation(sq[:, k % 2, :], src[:, off + k, :], ACT.Square).then_inc(sq_ready[m], 1)
                act.wait_ge(var_ready[m], 1)
                act.activation(stat[:, 2 * m, 0:TILES], stat[:, 2 * m, 0:TILES], ACT.Sqrt).then_inc(root_ready[m], 1)

            def from_pair(n, dst, func=ACT.Copy, scale=1.0):
                act.wait_ge(proj_done, n + 1)
                for x in range(2):
                    ins = act.activation(dst[:, x * HALF:(x + 1) * HALF], bank[2 * (n % 2) + x][:, 0:HALF], func, scale=scale)
                ins.then_inc(proj_act, 1)

            act.wait_ge(x_loaded, 16 * KT)
            norm(0)
            act.wait_ge(const_loaded, 32)
            act.activation(na[:, :], pp("a_log"), ACT.Exp).then_inc(a_exp, 1)
            act.wait_ge(fl_done, 1)
            for x in range(2):
                act.activation(fl[:, x * HALF:(x + 1) * HALF], bank[x][0:RANK, 0:HALF], ACT.Copy).then_inc(fl_copied, 1)
            act.wait_ge(dtl_copied, 1)
            link(act.activation(dt[:, 1, :], dt[:, 0, :], ACT.Abs))
            act.activation(dt[:, 1, :], dt[:, 1, :], ACT.Exp, scale=-1.0).then_inc(dt_step, 1)
            act.wait_ge(dt_step, 2)
            act.activation(dt[:, 3, :], dt[:, 2, :], ACT.Ln).then_inc(dt_step, 1)
            act.wait_ge(gk_copied, TILES)
            link(act.activation(tmp[:, 0, :, :], gk[:, :, :], ACT.Abs))
            act.activation(tmp[:, 0, :, :], tmp[:, 0, :, :], ACT.Exp, scale=-1.0).then_inc(gk_step, 1)
            act.wait_ge(gk_step, 3)
            act.activation(tmp[:, 1, :, :], tmp[:, 1, :, :], ACT.Ln).then_inc(gk_step, 1)
            for i in range(TILES):
                act.wait_ge(v_done, i + 1)
                act.activation(V[0:rows(i), i, :], bank[2 + i % 2][0:rows(i), :], ACT.Copy).then_inc(v_copied, 1)
            act.wait_ge(b_done, 1)
            for p in range(NP):
                act.activation(bT[:, p, 0:512], bank[4 + p][:, :], ACT.Copy).then_inc(b_copied, 1)
                act.activation(bT[:, p, 512:T], bank[6][:, p * P:p * P + rows(4)], ACT.Copy).then_inc(b_copied, 1)
            act.wait_ge(b_copied, 4)
            act.activation(eb[:, :, :], bT[:, :, :], ACT.Exp).then_inc(eb_ready, 1)
            act.wait_ge(suf_done, 1)
            act.activation(khat[:, 0:2, :], bank[7][:, :].rearrange("p (a b) -> p a b", a=2), ACT.Exp).then_inc(suf_exp, 1)
            act.activation(khat[:, 2:4, :], bank[0][:, :].rearrange("p (a b) -> p a b", a=2), ACT.Exp).then_inc(suf_exp, 1)
            act.activation(khat[0:rows(4), 4, :], bank[1][0:rows(4), 0:256], ACT.Exp).then_inc(suf_exp, 1)
            for n in range(4):
                from_pair(n, (qT if n < 2 else kT)[:, n % 2, :], scale=(DK ** -0.5 if n < 2 else 1.0))

            def decay(u):
                act.wait_ge(e_arg, u + 1)
                e = E[:, u % 2, 0:rows(u // 2) * C]
                act.activation(e, e, ACT.Exp).then_inc(e_exp, 1)

            for n in range(4, 12):
                from_pair(n, (sg if n < 8 else sz)[:, n % 4, :], ACT.Silu)
            for u in range(2 * TILES):
                decay(u)
            n = 0
            for i in range(TILES):
                n += P // C if i < 4 else SEGS
                act.wait_ge(inter_done, n)
                for x in range(2):
                    src = bank[(2, 6)[i % 2] + x][:, 0:2 * P].rearrange("p (h t) -> p h t", h=2)[:, :, 0:rows(i)]
                    ins = act.activation(mix[:, x:GH:2, cols(i)], src, ACT.Copy)
                ins.then_inc(o_copied, 1)
            act.wait_ge(o_copied, TILES)
            act.activation(gsq, mix[:, 0:GH, :], ACT.Square).then_inc(gsq_ready, 1)
            act.wait_ge(gvar_ready, 1)
            act.activation(gstat[:, 0, :], gstat[:, 0, :], ACT.Sqrt).then_inc(groot_ready, 1)
            act.wait_ge(g_mixed, 4)
            act.wait_ge(xp_zero, 1)
            act.wait_ge(stored, 32)
            for f in range(CT):
                n = 12 + f
                act.wait_ge(proj_done, n + 1)
                b0, b1 = bank[2 * (n % 2)], bank[2 * (n % 2) + 1]
                act.activation(xp[:, f, 3:3 + HALF], b0[:, 0:HALF], ACT.Copy)
                act.activation(xp[:, f, 3 + HALF:XPW], b1[:, 0:NPROMPT - HALF], ACT.Copy)
                act.activation(xp[:, f, XPW:XP].rearrange("p (b t) -> p b t", b=NSEQ)[:, :, CONV - 1:XPS],
                               b1[:, NPROMPT - HALF:HALF].rearrange("p (b t) -> p b t", b=NSEQ), ACT.Copy
                               ).then_inc(proj_act, 1)
            for f in range(CT):
                act.wait_ge(conv_done, f + 1)
                act.activation(xc[:, f, :], xc[:, f, :], ACT.Silu).then_inc(xc_ready, 1)
            for i in range(TILES):
                act.wait_ge(tr_done, i + 1)
                act.activation(xtok[0:rows(i), i, :], bank[4 + i % 2][0:rows(i), :], ACT.Copy).then_inc(tr_copied, 1)
                act.activation(btok[0:rows(i), i, :], bank[6 + i % 2][0:rows(i), 0:256], ACT.Copy).then_inc(tr_copied, 1)
            for i in range(TILES):
                r = rows(i)
                act.wait_ge(z_ready, i + 1)
                act.wait_ge(ncum_ready, i + 1)
                if i >= 1:
                    act.wait_ge(ct_ready, i)
                    act.wait_ge(h_updated, i)
                    act.wait_ge(xw_ready, i)
                for g in range(2):
                    ins = act.activation(ecb[:, 4 * g:4 * g + 4, 0:r],
                                         bank[g][:, :].rearrange("p (h t) -> p h t", h=4)[:, :, 0:r], ACT.Exp)
                ins.then_inc(ecb_ready, 1)
                act.activation(cum[0:r, 1, :], bank[3][0:r, SH:2 * SH], ACT.Exp).then_inc(wx_ready, 1)
                for hh in range(SH):
                    ins = act.activation(L[0:r, hh, 0:r], L[0:r, hh, 0:r], ACT.Exp, bias=cum[0:r, 0, hh:hh + 1])
                ins.then_inc(l_exp, 1)
            act.wait_ge(yz_ready, 4)
            norm(1)
            act.wait_ge(proj_dve, KT)
            norm(2)
            for n in range(N_FEAT + KT, N_PROJ):
                from_pair(n, qh[:, n - N_FEAT - KT, :])

            def copy_picks(i):
                act.wait_ge(e_turned, i + 1)
                for x, dst in enumerate((e1T, e2T, gT)):
                    ins = act.activation(dst[:, cols(i)], bank[0][:, x * P:x * P + rows(i)], ACT.Copy)
                ins.then_inc(e_copied, 1)

            for i in range(TILES):
                r = rows(i)
                act.wait_ge(score_done, i + 1)
                if i >= 1:
                    act.wait_ge(top_sorted, i)
                for x in range(4):
                    act.activation(s12[0:r, 4 * x:4 * x + 4, :], bank[4 + x][0:r, :].rearrange("p (h k) -> p h k", h=4),
                                   ACT.Copy).then_inc(score_copied, 1)
                if i >= 1:
                    copy_picks(i - 1)
                act.wait_ge(sm_arg, i + 1)
                act.activation(e12[0:r, 2, :, :], e12[0:r, 2, :, :], ACT.Exp).then_inc(sm_exp, 1)
            copy_picks(TILES - 1)

            def gates_out(b, x, first=False):
                if not first:
                    act.wait_ge(gate_stored[x], 8 * (b - x))
                for q in range(TB // 4):
                    act.wait_ge(gate_done, b * (TB // 4) + q + 1)
                    act.activation(stage[:, x, :, 4 * q:4 * q + 4, :].rearrange("p g t j -> p t g j"),
                                   bank[q % 4][:, :].rearrange("p (t g j) -> p t g j", t=4, j=GRP), ACT.Copy
                                   ).then_inc(gate_copied, 1)

            gates_out(0, 0, first=True)
            gates_out(1, 1, first=True)
            with act.Fori(1, NBLK // 2) as pair:
                b = pair * 2
                gates_out(b, 0)
                gates_out(b + 1, 1)
            gates_out(NBLK - 1, 0)

            def gelu(g, par, j, first=False):
                act.wait_ge(hid_done, g * GRP + j + 1)
                if not first:
                    if j == 0:
                        act.wait_ge(acc_done, (g - 1) * KT)
                for y in range(2):
                    ins = act.activation(W[:, par, j, y * HALF:(y + 1) * HALF], bank[2 * (j % 2) + y][:, 0:HALF],
                                         ACT.Gelu_apprx_tanh)
                ins.then_inc(gelu_ready, 1)

            wait_gates_stored(act)
            for g in range(2):
                for j in range(GRP):
                    gelu(g, g, j, first=True)
            with act.Fori(1, NGRP // 2) as pair:
                g = pair * 2
                for y in range(2):
                    for j in range(GRP):
                        gelu(g + y, y, j)
            act.wait_ge(acc_added, NGRP * KT)
            norm(3)

        @block.vector
        def _(dve):
            linked = [0]

            def link(ins):
                linked[0] += 1
                ins.then_inc(chain, 1)
                dve.wait_ge(chain, linked[0])

            def norm(m):
                src, n = norm_src[m]
                off = 4 if m == 1 else 0
                dst = mix if m == 1 else xn
                link(dve.memset(stat[:, 2 * m, 0:TILES], 1.0))
                dve.wait_ge(sq_used[m], n)
                s = 1.0 / (n * P)
                dve.tensor_scalar(stat[:, 2 * m, 0:4], bank[4][:, 0:4], s, EPS, ALU.mult, ALU.add)
                dve.tensor_scalar(stat[0:rows(4), 2 * m, 4:5], bank[4][0:rows(4), 4:5], s, EPS, ALU.mult, ALU.add
                                  ).then_inc(var_ready[m], 1)
                dve.wait_ge(root_ready[m], 1)
                dve.reciprocal(stat[:, 2 * m + 1, 0:TILES], stat[:, 2 * m, 0:TILES]).then_inc(rstd_ready[m], 1)
                dve.wait_ge(bc_done[m], 1)
                w = pp(norm_par[m])
                for k in range(n):
                    dve.scalar_tensor_tensor(dst[:, off + k, 0:512], src[:, off + k, 0:512], w[:, k:k + 1], bank[6][:, :],
                                             ALU.mult, ALU.mult)
                    dve.scalar_tensor_tensor(dst[:, off + k, 512:T], src[:, off + k, 512:T], w[:, k:k + 1],
                                             bank[7][:, 0:T - 512], ALU.mult, ALU.mult).then_inc(normed[m], 1)

            dve.wait_ge(x_loaded, 16 * KT)
            dve.wait_ge(const_loaded, 32)
            dve.memset(S[:, 0, :, :], 0.0).then_inc(s_zero, 1)
            dve.memset(gk[:, TILES - 1, :], 0.0)
            link(dve.memset(dt[:, 0, :], 0.0))
            norm(0)
            dve.wait_ge(a_exp, 1)
            link(dve.tensor_scalar(na[:, :], na[:, :], -1.0, None, ALU.mult))
            dve.wait_ge(dtl_done, 1)
            dve.tensor_copy(dt[:, 0, 0:4 * SH], bank[5][:, 0:4 * SH])
            dve.tensor_copy(dt[0:rows(4), 0, 4 * SH:5 * SH], bank[5][0:rows(4), 4 * SH:5 * SH]).then_inc(dtl_copied, 1)
            dve.wait_ge(dt_step, 1)
            dve.tensor_scalar(dt[:, 2, :], dt[:, 1, :], 1.0, None, ALU.add).then_inc(dt_step, 1)
            dve.wait_ge(dt_step, 3)
            link(dve.scalar_tensor_tensor(dt[:, 1, :], dt[:, 2, :], -1.0, dt[:, 1, :], ALU.add, ALU.subtract))
            link(dve.tensor_tensor(dt[:, 3, :], dt[:, 3, :], dt[:, 1, :], ALU.subtract))
            link(dve.scalar_tensor_tensor(dt[:, 0, :], dt[:, 0, :], 0.0, dt[:, 3, :], ALU.max, ALU.add))
            dve.tensor_tensor(dta[:, :, :], dt[:, 0, :].rearrange("p (i h) -> p i h", h=SH), bc(na[:, :], 1, TILES),
                              ALU.mult).then_inc(dt_ready, 1)
            for i in range(TILES):
                dve.wait_ge(gk_done, i + 1)
                dve.tensor_copy(gk[0:rows(i), i, :], bank[6 + i % 2][0:rows(i), 0:GH * DK]).then_inc(gk_copied, 1)
            dve.wait_ge(gk_step, 1)
            dve.tensor_scalar(tmp[:, 1, :, :], tmp[:, 0, :, :], 1.0, None, ALU.add).then_inc(gk_step, 1)
            dve.wait_ge(gk_step, 2)
            dve.scalar_tensor_tensor(tmp[:, 0, :, :], tmp[:, 1, :, :], -1.0, tmp[:, 0, :, :], ALU.add, ALU.subtract
                                     ).then_inc(gk_step, 1)
            dve.wait_ge(gk_step, 4)
            link(dve.tensor_tensor(tmp[:, 1, :, :], tmp[:, 0, :, :], tmp[:, 1, :, :], ALU.subtract))
            link(dve.scalar_tensor_tensor(tmp[:, 1, :, :], gk[:, :, :], 0.0, tmp[:, 1, :, :], ALU.min, ALU.add))
            dve.tensor_scalar(gk[:, :, :], tmp[:, 1, :, :], 1.0 / 16.0, None, ALU.mult).then_inc(gk_ready, 1)
            dve.wait_ge(proj_act, 4)
            dve.wait_ge(eb_ready, 1)
            dve.tensor_tensor(qb[:, :, :], qT[:, :, :], eb[:, :, :], ALU.mult).then_inc(qb_ready, 1)

            def mult_k(u):
                i, p = u // 2, u % 2
                e = E[:, u % 2, 0:rows(i) * C].rearrange("p (t c s) -> p t c s", t=C, s=C)
                dve.wait_ge(e_q, u + 1)
                dve.tensor_tensor(e, e, bc(kT[:, p, cols(i)].rearrange("p (c s) -> p c s", s=C), 1, C), ALU.mult
                                  ).then_inc(e_k, 1)

            for u in range(2 * TILES):
                i, p = u // 2, u % 2
                e = E[:, u % 2, 0:rows(i) * C].rearrange("p (t c s) -> p t c s", t=C, s=C)
                target = bc(bT[:, p, cols(i)].rearrange("p (c t) -> p t c", t=C), 3, C)
                source = bc(bT[:, p, cols(i)].rearrange("p (c s) -> p c s", s=C), 1, C)
                if u >= 2:
                    dve.wait_ge(attn_used, u - 1)
                if u == 0:
                    dve.wait_ge(v_copied, TILES)
                link(dve.tensor_tensor(e, target, source, ALU.subtract))
                ef = E[:, u % 2, 0:rows(i) * C]
                dve.tensor_scalar(ef, ef, 0.0, None, ALU.min).then_inc(e_arg, 1)
                if u == 0:
                    dve.wait_ge(ktok_done, 1)
                    dve.wait_ge(suf_exp, 3)
                    for q in range(2):
                        dve.tensor_tensor(khat[:, 2 * q:2 * q + 2, :], khat[:, 2 * q:2 * q + 2, :],
                                          bank[4 + q][:, :].rearrange("p (a b) -> p a b", a=2), ALU.mult)
                    dve.tensor_tensor(khat[0:rows(4), 4, :], khat[0:rows(4), 4, :], bank[6][0:rows(4), 0:256], ALU.mult
                                      ).then_inc(khat_ready, 1)
                if u >= 1:
                    mult_k(u - 1)
                if u >= 3 and u % 2 == 1:
                    attn_matrix(dve, u // 2 - 1)
            mult_k(2 * TILES - 1)
            attn_matrix(dve, TILES - 1)
            n = 0
            for i in range(TILES):
                for c in range(P // C if i < 4 else SEGS):
                    a, b = (c * C, c * C + C) if i < 4 else seg_cols(c)
                    last = P * i + b - 1
                    sample = i == 4 and c > 0
                    dve.wait_ge(local_done, n + 1)
                    if sample:
                        dve.wait_ge(inter_done, n + 1)
                    elif n >= 1:
                        dve.wait_ge(inter_done, n)
                        dve.wait_ge(s_updated, n)
                    for p in range(NP):
                        src = Ssm[:, c - 1, p, :] if sample else S[:, n % 2, p, :]
                        dst = Ssm[:, c - 1, p, :] if sample else S[:, (n + 1) % 2, p, :]
                        ins = dve.scalar_tensor_tensor(dst, src, eb[:, p, last:last + 1], bank[4 + n % 2][:, p * P:p * P + DV],
                                                       ALU.mult, ALU.add)
                    ins.then_inc(s_updated, 1)
                    n += 1
            link(dve.memset(gstat[:, 0, :], 1.0))
            dve.wait_ge(gsum_done, 1)
            dve.tensor_scalar(gstat[:, 0, 0:4 * GH], bank[4][:, 0:4 * GH], 1.0 / DV, EPS, ALU.mult, ALU.add)
            dve.tensor_scalar(gstat[0:rows(4), 0, 4 * GH:], bank[4][0:rows(4), 4 * GH:5 * GH], 1.0 / DV, EPS, ALU.mult,
                              ALU.add).then_inc(gvar_ready, 1)
            dve.wait_ge(groot_ready, 1)
            dve.reciprocal(gstat[:, 1, :], gstat[:, 0, :]).then_inc(grstd_ready, 1)
            dve.wait_ge(gbc_done, 1)
            for hh in range(GH):
                dve.scalar_tensor_tensor(mix[:, hh, 0:512], mix[:, hh, 0:512], pp("gla_w"), bank[hh][:, :], ALU.mult,
                                         ALU.mult).then_inc(g_normed, 1)
                dve.scalar_tensor_tensor(mix[:, hh, 512:T], mix[:, hh, 512:T], pp("gla_w"), bank[5][:, hh * P:hh * P + rows(4)],
                                         ALU.mult, ALU.mult).then_inc(g_normed, 1)
                dve.wait_ge(g_normed, 2 * hh + 2)
                dve.tensor_tensor(mix[:, hh, :], mix[:, hh, :], sg[:, hh, :], ALU.mult).then_inc(g_mixed, 1)
            dve.wait_ge(stored, 32)
            dve.memset(xp[:, :, 0:CONV - 1], 0.0).then_inc(xp_zero, 1)
            dve.memset(H[:, 0, :], 0.0).then_inc(s_zero, 1)
            dve.wait_ge(hist_loaded, 16 * CT)
            w, cb = pp("conv_w"), pp("conv_b")
            for f in range(CT):
                dve.wait_ge(proj_act, 12 + f + 1)
                sample = xp[:, f, XPW:XP].rearrange("p (b t) -> p b t", b=NSEQ)
                dst_s = xc[:, f, NPROMPT:T].rearrange("p (b t) -> p b t", b=NSEQ)
                dve.tensor_scalar(xc[:, f, 0:NPROMPT], xp[:, f, 0:NPROMPT], w[:, 4 * f:4 * f + 1], cb[:, f:f + 1],
                                  ALU.mult, ALU.add)
                ins = dve.tensor_scalar(dst_s, sample[:, :, 0:SLEN], w[:, 4 * f:4 * f + 1], cb[:, f:f + 1], ALU.mult, ALU.add)
                for t in range(1, CONV):
                    link(ins)
                    wt = w[:, 4 * f + t:4 * f + t + 1]
                    dve.scalar_tensor_tensor(xc[:, f, 0:NPROMPT], xp[:, f, t:t + NPROMPT], wt, xc[:, f, 0:NPROMPT],
                                             ALU.mult, ALU.add)
                    ins = dve.scalar_tensor_tensor(dst_s, sample[:, :, t:t + SLEN], wt, dst_s, ALU.mult, ALU.add)
                ins.then_inc(conv_done, 1)
            for i in range(TILES):
                r = rows(i)
                neg = cc("neg_a" if i < 4 else "neg_b", r)[:, 0:r]
                dve.wait_ge(pre_done, i + 1)
                if i >= 1:
                    dve.wait_ge(y_done, i)
                    dve.wait_ge(l_exp, i)
                dve.tensor_scalar(cum[0:r, 0, :], bank[3][0:r, 0:SH], -1.0, None, ALU.mult).then_inc(ncum_ready, 1)
                for g in range(2):
                    ins = dve.tensor_tensor(L[0:r, 4 * g:4 * g + 4, 0:r],
                                            bank[g][0:r, :].rearrange("p (h t) -> p h t", h=4)[:, :, 0:r], bc(neg, 1, 4), ALU.add)
                ins.then_inc(z_ready, 1)
                dti = dt[0:r, 0, SH * i:SH * i + SH]
                dve.tensor_tensor(Xd[0:r, :].rearrange("p (h q) -> p h q", h=SH), xtok3(i), bc(dti, 2, HD), ALU.mult)
                dve.wait_ge(wx_ready, i + 1)
                link(dve.tensor_tensor(cum[0:r, 2, :], cum[0:r, 1, :], dti, ALU.mult))
                if i >= 1:
                    dve.wait_ge(hloc_done, i)
                dve.tensor_tensor(XW[0:r, :].rearrange("p (h q) -> p h q", h=SH), xtok3(i), bc(cum[0:r, 2, :], 2, HD),
                                  ALU.mult).then_inc(xw_ready, 1)
                dve.wait_ge(l_exp, i + 1)
                for g in range(SG):
                    ins = dve.tensor_tensor(L[0:r, 4 * g:4 * g + 4, 0:r], L[0:r, 4 * g:4 * g + 4, 0:r],
                                            bc(bank[2][0:r, g * P:g * P + r], 1, 4), ALU.mult)
                ins.then_inc(m_ready, 1)
                if i == 4:
                    dve.wait_ge(xw_ready, i + 1)
                    for c in range(2):
                        dve.tensor_scalar(XWm[0:r, c % 2, :], XW[0:r, :], cc("col_b", r)[:, c:c + 1], None, ALU.mult
                                          ).then_inc(xwm_ready, 1)
                dve.wait_ge(y_done, i + 1)
                ds = pp("dskip")
                for j in range(4):
                    ins = dve.scalar_tensor_tensor(mix[:, 4 + j, cols(i)], xc[:, j, cols(i)], ds[:, j:j + 1],
                                                   bank[4][:, j * P:j * P + r], ALU.mult, ALU.add)
                ins.then_inc(y_copied, 1)
                for c in range(1 if i < 4 else SEGS):
                    last = r - 1 if i < 4 else seg_cols(c)[1] - 1
                    dve.wait_ge(hloc_done, i + c + 1)
                    src, dst = (H[:, i % 2, :], H[:, (i + 1) % 2, :]) if c == 0 else (Hsm[:, c - 1, :],) * 2
                    if c == 0 and i >= 1:
                        dve.wait_ge(h_updated, i)
                    dec = bc(ecb[:, :, last], 2, HD)
                    link(dve.tensor_tensor(dst.rearrange("p (h q) -> p h q", h=SH), src.rearrange("p (h q) -> p h q", h=SH),
                                           dec, ALU.mult))
                    dve.tensor_tensor(dst, dst, bank[5][:, :], ALU.add).then_inc(h_updated, 1)
                    if i == 4 and c + 2 < SEGS:
                        dve.tensor_scalar(XWm[0:r, c % 2, :], XW[0:r, :], cc("col_b", r)[:, c + 2:c + 3], None, ALU.mult
                                          ).then_inc(xwm_ready, 1)
            dve.wait_ge(y_copied, TILES)
            for j in range(4):
                dve.tensor_tensor(mix[:, 4 + j, :], mix[:, 4 + j, :], sz[:, j, :], ALU.mult).then_inc(yz_ready, 1)
            dve.wait_ge(yz_ready, 4)
            norm(1)
            for k in range(KT):
                n = N_FEAT + k
                dve.wait_ge(proj_done, n + 1)
                for x in range(2):
                    ins = dve.tensor_tensor(h[:, k, x * HALF:(x + 1) * HALF], h[:, k, x * HALF:(x + 1) * HALF],
                                            bank[2 * (n % 2) + x][:, 0:HALF], ALU.add)
                ins.then_inc(proj_dve, 1)
            dve.wait_ge(proj_dve, KT)
            norm(2)
            def top16(out, idx, src, r, n, rep_x):
                vals = rep[0:r, rep_x, 0:n]
                link(dve.max(out[:, 0:8], src))
                dve.max_index(idx[:, 0:8], out[:, 0:8], src)
                link(dve.match_replace(vals, out[:, 0:8], src, -3.0e38))
                link(dve.max(out[:, 8:16], vals))
                dve.max_index(idx[:, 8:16], out[:, 8:16], vals)

            for i in range(TILES):
                r = rows(i)
                dve.wait_ge(score_copied, 4 * (i + 1))
                for x in range(2 * PH):
                    half, hh = x // PH, x % PH
                    top16(v16[0:r, half, hh, :], i16[0:r, half, hh, :], s12[0:r, x, :], r, NK, x % 2)
                for hh in range(PH):
                    cnd = cand[0:r, :].rearrange("p (a b) -> p a b", a=TOPK)
                    link(dve.tensor_tensor(cnd, bc(v16[0:r, 0, hh, :], 2, TOPK), bc(v16[0:r, 1, hh, :], 1, TOPK), ALU.add))
                    top16(v16[0:r, 2, hh, :], i16[0:r, 2, hh, :], cand[0:r, :], r, TOPK * TOPK, hh % 2)
                dve.tensor_copy(f16[0:r, 0:2, :, :], i16[0:r, 0:2, :, :]).then_inc(top_sorted, 1)
                dve.wait_ge(top_sorted, i + 1)
                if i >= 1:
                    dve.wait_ge(e_turned, i)
                dve.tensor_tensor(e12[0:r, 2, :, :], v16[0:r, 2, :, :], bc(v16[0:r, 2, :, 0], 2, TOPK), ALU.subtract
                                  ).then_inc(sm_arg, 1)
                dve.tensor_scalar(j16[0:r, 0, :, :], i16[0:r, 2, :, :], 4, None, ALU.logical_shift_right)
                link(dve.tensor_scalar(j16[0:r, 1, :, :], i16[0:r, 2, :, :], TOPK - 1, None, ALU.bitwise_and))
                link(dve.tensor_copy(f16[0:r, 2:4, :, :], j16[0:r, :, :, :]))
                pk = pick[0:r, :, :, :].rearrange("p h k j -> p (h k) j")
                for x in range(2):
                    rank = f16[0:r, 2 + x, :, :].rearrange("p h k -> p (h k)")
                    link(dve.tensor_tensor(pk, bc(rank, 2, TOPK), bc(cc("iota16", r), 1, PH * TOPK), ALU.is_equal))
                    for hh in range(PH):
                        ins = dve.tensor_tensor(pick[0:r, hh, :, :], pick[0:r, hh, :, :], bc(f16[0:r, x, hh, :], 1, TOPK), ALU.mult)
                    link(ins)
                    link(dve.tensor_reduce(e12[0:r, x, :, :].rearrange("p h k -> p (h k)"), pk, AX.X, ALU.add))
                dve.wait_ge(sm_exp, i + 1)
                link(dve.tensor_reduce(den[0:r, 0, :], e12[0:r, 2, :, :], AX.X, ALU.add))
                link(dve.reciprocal(den[0:r, 1, :], den[0:r, 0, :]))
                dve.tensor_tensor(e12[0:r, 2, :, :], e12[0:r, 2, :, :], bc(den[0:r, 1, :], 2, TOPK), ALU.mult
                                  ).then_inc(e_ready, 1)
            dve.wait_ge(e_copied, TILES)

            def one_hots(b, x, first=False):
                if not first:
                    dve.wait_ge(gate_done, (b - 1) * (TB // 4))
                for t in range(TB):
                    at = b * TB + t
                    dve.tensor_scalar(oneB[:, x, t, :], cc("iota"), e2T[:, bass.ds(at, 1)], None, ALU.is_equal)
                    ins = dve.tensor_scalar(oneA[:, x, t, :], cc("iota"), e1T[:, bass.ds(at, 1)], gT[:, bass.ds(at, 1)],
                                            ALU.is_equal, ALU.mult)
                ins.then_inc(one_hot_ready, 1)

            one_hots(0, 0, first=True)
            one_hots(1, 1, first=True)
            with dve.Fori(1, NBLK // 2) as pair:
                b = pair * 2
                one_hots(b, 0)
                one_hots(b + 1, 1)
            one_hots(NBLK - 1, 0)

            def gate(g, par, j):
                if j == 0:
                    dve.wait_ge(g_loaded[par], 16 * (g // 2 + 1) if isinstance(g, int) else 8 * (g - par) + 16)
                dve.wait_ge(gelu_ready, g * GRP + j + 1)
                dve.tensor_tensor(W[:, par, j, :], W[:, par, j, :], G[:, par, :, j], ALU.mult).then_inc(w_ready, 1)

            def add_out(g, k):
                dve.wait_ge(acc_done, g * KT + k + 1)
                for y in range(2):
                    ins = dve.tensor_tensor(h[:, k, y * HALF:(y + 1) * HALF], h[:, k, y * HALF:(y + 1) * HALF],
                                            bank[4 + 2 * (k % 2) + y][:, 0:HALF], ALU.add)
                ins.then_inc(acc_added, 1)

            wait_gates_stored(dve)
            for j in range(GRP):
                gate(0, 0, j)
            for j in range(GRP):
                gate(1, 1, j)
                add_out(0, j)
            with dve.Fori(1, NGRP // 2) as pair:
                g = pair * 2
                for y in range(2):
                    for j in range(GRP):
                        gate(g + y, y, j)
                        add_out(g + (y - 1), j)
            for k in range(KT):
                add_out(NGRP - 1, k)
            dve.wait_ge(acc_added, NGRP * KT)
            norm(3)

        @block.gpsimd
        def _(pool):
            pool.wait_ge(proj_act, 4)
            for u in range(2 * TILES):
                i, p = u // 2, u % 2
                e = E[:, u % 2, 0:rows(i) * C].rearrange("p (t c s) -> p t c s", t=C, s=C)
                pool.wait_ge(e_exp, u + 1)
                pool.tensor_tensor(e, e, bc(qT[:, p, cols(i)].rearrange("p (c t) -> p t c", t=C), 3, C), ALU.mult
                                   ).then_inc(e_q, 1)
            pool.wait_ge(khat_ready, 1)
            for i in range(TILES):
                r, nch = rows(i), (P // C if i < 4 else SEGS)
                if i >= 2:
                    pool.wait_ge(local_done, (P // C) * (i - 1))
                pool.tensor_tensor(khm[i % 2][0:r, 0:nch, :], bc(khat[0:r, i, :], 1, nch),
                                   bc(cc("col_a" if i < 4 else "col_b", r), 2, GH * DK), ALU.mult).then_inc(khm_ready, 1)
            for i in range(TILES):
                r = rows(i)
                pool.wait_ge(ecb_ready, i + 1)
                if i >= 1:
                    pool.wait_ge(y_done, i)
                pool.wait_ge(xc_ready, CT)
                for g in range(SG):
                    ins = pool.tensor_tensor(Ct[:, 4 * g:4 * g + 4, 0:r], ecb[:, 4 * g:4 * g + 4, 0:r],
                                             bc(xc[:, 6 + g, cols(i)], 1, 4), ALU.mult)
                ins.then_inc(ct_ready, 1)


def feature_tiles(w):
    n = w.shape[1] // P
    return w.reshape(KT, P, n, P).transpose(2, 1, 0, 3).reshape(n, P, D)


def kernel(x_prompt, x_sample, state_gla, state_ssm, state_conv, meta_tokens, norm1_w, w_in, w_gk2, b_gk2, gla_norm_w,
           conv_w, conv_b, dt_bias, a_log, d_skip, ssd_norm_w, w_out, norm2_w, peer_wq, peer_k1, peer_k2, peer_u, peer_v,
           final_norm_w):
    import concourse.bacc as bacc
    from concourse.bass_utils import run_bass_kernel_spmd

    x = np.concatenate([np.asarray(meta_tokens), np.asarray(x_prompt)[0], np.asarray(x_sample).reshape(NSEQ * SLEN, D)])
    w = np.asarray(w_in)[0]
    at = np.cumsum([0, GH * DK, GH * DK, GH * DV, GH * DV, RANK, SH * HD, CONVD, SH])
    q, k, v, g, f, z, xbc, dtw = (w[:, at[i]:at[i + 1]] for i in range(8))
    per_feature = lambda a: np.asarray(a).reshape(-1, P).T
    params = {
        "norm1": per_feature(norm1_w), "norm2": per_feature(norm2_w), "final": per_feature(final_norm_w),
        "gla_w": per_feature(gla_norm_w), "ssd_w": per_feature(ssd_norm_w),
        "conv_w": np.asarray(conv_w)[0].reshape(CONV, CT, P).transpose(2, 1, 0).reshape(P, CT * CONV),
        "conv_b": per_feature(conv_b), "dskip": per_feature(np.repeat(np.asarray(d_skip)[0], HD)),
        "a_log": np.tile(np.asarray(a_log), (P, 1)),
    }
    ins = {
        "xT": x.reshape(T, KT, P).transpose(2, 1, 0),
        "const": constants(),
        "param": np.concatenate([params[n] for n, _ in PARAM_PARTS], axis=1),
        "rows": np.concatenate([np.asarray(b_gk2), np.asarray(dt_bias)], axis=1),
        "wsmall": np.concatenate([f, dtw], axis=1).reshape(KT, P, RANK + SH).transpose(1, 0, 2),
        "w_gk2": np.asarray(w_gk2)[0],
        "wv": v.reshape(KT, P, GH * DV).transpose(1, 0, 2),
        "wproj": np.concatenate([feature_tiles(np.concatenate([q, k, g, z, xbc], axis=1)),
                                 feature_tiles(np.asarray(w_out)[0]), feature_tiles(np.asarray(peer_wq)[0])]),
        "keys": np.concatenate([np.asarray(peer_k1)[0].T, np.asarray(peer_k2)[0].T]),
        "s_gla": np.asarray(state_gla)[0].reshape(NSEQ, NP, 2, DK, DV).transpose(2, 3, 0, 1, 4).reshape(P, NSEQ, NP, DV),
        "s_ssm": np.asarray(state_ssm)[0].transpose(3, 0, 1, 2).reshape(DS, NSEQ, SH * HD),
        "s_conv": np.asarray(state_conv)[0].reshape(NSEQ, CONV - 1, CT, P).transpose(3, 2, 0, 1),
        "u": np.asarray(peer_u)[0].reshape(NK, NK, KT, P).transpose(1, 3, 2, 0).reshape(NK, P, D),
        "v": np.asarray(peer_v)[0].reshape(NK, NGRP, GRP, D),
    }
    outs = {
        "yT": (P, KT, T), "gla_p": (P, NP, DV), "gla_s": (P, NSEQ, NP, DV), "ssm_p": (P, SH * HD),
        "ssm_s": (P, NSEQ, SH * HD), "conv_p": (P, CT, CONV - 1), "conv_s": (P, CT, NSEQ, CONV - 1),
    }
    nc = bacc.Bacc("TRN2", target_bir_lowering=False, num_devices=1)
    arrays, di, do = {}, {}, {}
    for name, a in ins.items():
        arrays[f"in_{name}"] = np.ascontiguousarray(a)
        di[name] = nc.dram_tensor(f"in_{name}", a.shape, F32, kind="ExternalInput").ap()
    for name, shape in outs.items():
        do[name] = nc.dram_tensor(f"out_{name}", shape, F32, kind="ExternalOutput").ap()
    build(nc, di, do)
    r = run_bass_kernel_spmd(nc, [arrays], core_ids=[0]).results[0]
    r = {name: np.asarray(r[f"out_{name}"]) for name in outs}
    y = r["yT"].transpose(2, 1, 0).reshape(T, D)
    heads = lambda a: a.reshape(2, DK, -1, NP, DV).transpose(2, 3, 0, 1, 4).reshape(1, -1, GH, DK, DV)
    ssm = lambda a: a.reshape(DS, -1, SH, HD).transpose(1, 2, 3, 0)[None]
    conv = lambda a: a.reshape(P, CT, -1, CONV - 1).transpose(2, 3, 1, 0).reshape(1, -1, CONV - 1, CONVD)
    return (y[META:NPROMPT][None], y[NPROMPT:].reshape(NSEQ, SLEN, D),
            heads(r["gla_p"]), ssm(r["ssm_p"]), conv(r["conv_p"]),
            heads(r["gla_s"]), ssm(r["ssm_s"]), conv(r["conv_s"]))
```

```python
from contextlib import ExitStack

import numpy as np
import concourse.bass as bass
from concourse import mybir

F32 = mybir.dt.float32
F32R = mybir.dt.float32r
U32 = mybir.dt.uint32
ALU = mybir.AluOpType
ACT = mybir.ActivationFunctionType
AX = mybir.AxisListType

P = 128
D = 1024
KT = D // P
META, SEQ = 16, 512
NPROMPT = META + SEQ
NSEQ, SLEN = 8, 8
T = NPROMPT + NSEQ * SLEN
HALF = T // 2
TILES = 5
EPS = 1e-6
GH, DK, DV = 4, 64, 128
NP = GH // 2
RANK = 16
C = 16
SH, HD, DS, SG = 8, 64, 128, 2
CONV, CONVD = 4, 1024
CT = CONVD // P
PH, NK, QD, TOPK = 8, 128, 128, 16
XPW = (CONV - 1) + NPROMPT
XPS = CONV - 1 + SLEN
XP = XPW + NSEQ * XPS
N_FEAT = 20
N_PROJ = N_FEAT + KT + PH
GRP = 8
NGRP = NK // GRP
TB = 16
NBLK = T // TB
NE = NK
ROUTE_QUADS = 3
SEGS = 1 + NSEQ
CHUNKS = (TILES - 1) * (P // C) + SEGS
PROMPT_CHUNKS = NPROMPT // C


def rows(i):
    return P if i < TILES - 1 else T - P * (TILES - 1)


def cols(i):
    return slice(P * i, P * i + rows(i))


def seg_cols(r):
    return (0, META) if r == 0 else (META + SLEN * (r - 1), META + SLEN * r)


CONST_PARTS = [("ident", P), ("ones", P), ("incl_a", P), ("incl_b", P), ("suf_a", P), ("suf_b", P),
               ("tincl_a", P), ("tsuf_a", P), ("neg_a", P), ("neg_b", P), ("col_a", P // C), ("col_b", SEGS),
               ("head2", 2), ("iota", NK), ("iota16", TOPK)]


def offsets(parts):
    out, at = {}, 0
    for name, n in parts:
        out[name] = (at, at + n)
        at += n
    return out, at


CONST_AT, CONST_N = offsets(CONST_PARTS)
PARAM_PARTS = [("norm1", KT), ("norm2", KT), ("final", KT), ("gla_w", 1), ("ssd_w", 4), ("conv_w", CT * CONV),
               ("conv_b", CT), ("dskip", 4), ("a_log", SH)]
PARAM_AT, PARAM_N = offsets(PARAM_PARTS)


def constants():
    r = np.arange(P)
    seg_b = np.where(r < META, 0, 1 + (r - META) // SLEN)
    chunk_a = r // C
    le, gt = r[:, None] <= r[None, :], r[:, None] > r[None, :]
    same_a, same_b = chunk_a[:, None] == chunk_a[None, :], seg_b[:, None] == seg_b[None, :]
    parts = {
        "ident": np.eye(P), "ones": np.ones((P, P)),
        "incl_a": le & same_a, "incl_b": le & same_b, "suf_a": gt & same_a, "suf_b": gt & same_b,
        "tincl_a": le, "tsuf_a": gt,
        "neg_a": np.where(le, 0.0, -1e30), "neg_b": np.where(le & same_b, 0.0, -1e30),
        "col_a": chunk_a[:, None] == np.arange(P // C)[None, :],
        "col_b": seg_b[:, None] == np.arange(SEGS)[None, :],
        "head2": (r // DK)[:, None] == np.arange(2)[None, :],
        "iota": np.tile(np.arange(NK), (P, 1)), "iota16": np.tile(np.arange(TOPK), (P, 1)),
    }
    return np.concatenate([np.asarray(parts[n], np.float32) for n, _ in CONST_PARTS], axis=1)


def bc(ap, axis, n):
    ap = ap.unsqueeze(axis)
    shape = list(ap.shape)
    shape[axis] = n
    return ap.broadcast_to(shape)


def build(nc, d, o):
    base = ExitStack()
    with base:
        def sem(name):
            return base.enter_context(nc.semaphore(name))

        def sb(stack, name, shape, dt=F32):
            return stack.enter_context(nc.sbuf_tensor(name, shape, dt))

        gates_dram = nc.dram_tensor("gates_scratch", (NGRP, P, T, GRP), F32, kind="Internal").ap()
        hid_dram = nc.dram_tensor("hidden_scratch", (NE, P, T), F32, kind="Internal").ap()

        h = sb(base, "h", [P, KT, T])
        xn = sb(base, "xn", [P, KT, T])
        ring = sb(base, "ring", [P, 4, D])
        cst = sb(base, "cst", [P, CONST_N])
        prm = sb(base, "prm", [P, PARAM_N])
        sq = sb(base, "sq", [P, 2, T])
        stat = sb(base, "stat", [P, 8, TILES])
        gstat = sb(base, "gstat", [P, 2, TILES * GH])

        def cc(name, r=P):
            a, b = CONST_AT[name]
            return cst[0:r, a:b]

        def pp(name):
            a, b = PARAM_AT[name]
            return prm[:, a:b]

        ident, ones = cc("ident"), cc("ones")
        bank = [base.enter_context(nc.psum_tensor(f"bank{n}", [P, 512], F32)) for n in range(8)]

        mix_stack = ExitStack()
        mix = sb(mix_stack, "mix", [P, 8, T])
        sg = sb(mix_stack, "sg", [P, 4, T])
        sz = sb(mix_stack, "sz", [P, 4, T])
        row = sb(mix_stack, "row", [1, GH * DK + SH])
        small = sb(mix_stack, "small", [P, KT, RANK + SH])
        wgk = sb(mix_stack, "wgk", [RANK, GH * DK])
        fl = sb(mix_stack, "fl", [RANK, T])
        dt = sb(mix_stack, "dt", [P, 4, TILES * SH])
        dta = sb(mix_stack, "dta", [P, TILES, SH])
        na = sb(mix_stack, "na", [P, SH])

        gla = ExitStack()
        qT = sb(gla, "qT", [P, NP, T])
        kT = sb(gla, "kT", [P, NP, T])
        bT = sb(gla, "bT", [P, NP, T])
        eb = sb(gla, "eb", [P, NP, T])
        qb = sb(gla, "qb", [P, NP, T])
        V = sb(gla, "V", [P, TILES, GH * DV])
        khat = sb(gla, "khat", [P, TILES, GH * DK])
        gk = sb(gla, "gk", [P, TILES, GH * DK])
        tmp = sb(gla, "tmp", [P, 2, TILES, GH * DK])
        E = sb(gla, "E", [P, 2, P // C * C * C])
        MT = sb(gla, "MT", [P, TILES, GH * P])
        tmpf = tmp[:, :, :, :].rearrange("p a b c -> p (a b c)")
        khm = [sb(gla, "khm", [P, SEGS, GH * DK])[:, :, :],
               tmpf[:, 0:SEGS * GH * DK].rearrange("p (c n) -> p c n", c=SEGS)]
        S = sb(gla, "S", [P, 2, NP, DV])
        Ssm = sb(gla, "Ssm", [P, NSEQ, NP, DV])
        gla.close()
        Ef = E[:, :, :].rearrange("p a b -> p (a b)")
        wv_sb = Ef[:, 0:KT * GH * DV].rearrange("p (k n) -> p k n", k=KT)
        gsq = Ef[:, 0:GH * T].rearrange("p (h t) -> p h t", h=GH)

        ssd = ExitStack()
        xp = sb(ssd, "xp", [P, CT, XP])
        xc = sb(ssd, "xc", [P, CT, T])
        xtok = sb(ssd, "xtok", [P, TILES, SH * HD])
        btok = sb(ssd, "btok", [P, TILES, SG * DS])
        ecb = sb(ssd, "ecb", [P, SH, P])
        L = sb(ssd, "L", [P, SH, P])
        Ct = sb(ssd, "Ct", [P, SH, P])
        Xd = sb(ssd, "Xd", [P, SH * HD])
        XW = sb(ssd, "XW", [P, SH * HD])
        XWm = sb(ssd, "XWm", [P, 2, SH * HD])
        cum = sb(ssd, "cum", [P, 3, SH])
        H = sb(ssd, "H", [P, 2, SH * HD])
        Hsm = sb(ssd, "Hsm", [P, NSEQ, SH * HD])
        ssd.close()
        mix_stack.close()

        rt = ExitStack()
        xh = sb(rt, "xh", [P, KT, T], F32R)
        xl = sb(rt, "xl", [P, KT, T], F32R)
        usp = sb(rt, "usp", [P, 2, 2, D], F32R)
        gl = sb(rt, "gl", [P, 4, T])
        e1T = sb(rt, "e1T", [P, T])
        e2T = sb(rt, "e2T", [P, T])
        gT = sb(rt, "gT", [P, T])
        gTh = sb(rt, "gTh", [P, T], F32R)
        gTl = sb(rt, "gTl", [P, T])
        rt1 = ExitStack()
        oneA = sb(rt1, "oneA", [P, 2, TB, 2, NK], F32R)
        oneB = sb(rt1, "oneB", [P, 2, TB, NK], F32R)
        stage = sb(rt1, "stage", [P, 2, NGRP, TB, GRP])
        rt1.close()
        rt2 = ExitStack()
        qh = sb(rt2, "qh", [P, PH, T])
        keys = sb(rt2, "keys", [P, NK])
        s12 = sb(rt2, "s12", [P, 2 * PH, NK])
        rep = sb(rt2, "rep", [P, 2, 2 * NK])
        v16 = sb(rt2, "v16", [P, 3, PH, TOPK])
        i16 = sb(rt2, "i16", [P, 3, PH, TOPK], U32)
        j16 = sb(rt2, "j16", [P, 2, PH, TOPK], U32)
        f16 = sb(rt2, "f16", [P, 4, PH, TOPK])
        cand = sb(rt2, "cand", [P, TOPK * TOPK])
        pick = sb(rt2, "pick", [P, PH, TOPK, TOPK])
        e12 = sb(rt2, "e12", [P, 3, PH, TOPK])
        den = sb(rt2, "den", [P, 2, PH])
        rt2.close()
        rt.close()

        ex = ExitStack()
        vsp = sb(ex, "vsp", [P, 2, 4, 2, D], F32R)
        W = sb(ex, "W", [P, 2, 4, 2, T], F32R)
        G = sb(ex, "G", [P, 2, T, GRP])
        ex.close()

        x_loaded, const_loaded, small_loaded, wv_loaded, sgla_loaded = map(
            sem, ["x_loaded", "const_loaded", "small_loaded", "wv_loaded", "sgla_loaded"])
        hist_loaded, hsm_loaded, keys_loaded = map(sem, ["hist_loaded", "hsm_loaded", "keys_loaded"])
        w_loaded = [sem(f"w_loaded{s}") for s in range(4)]
        u_loaded = [sem(f"u_loaded{s}") for s in range(4)]
        v_loaded = [sem(f"v_loaded{s}") for s in range(4)]
        hid_loaded = [sem(f"hid_loaded{s}") for s in range(8)]
        hid_stored = [sem(f"hid_stored{s}") for s in range(4)]
        g_loaded = [sem(f"g_loaded{s}") for s in range(2)]
        stored = sem("stored")
        proj_done, proj_act, proj_dve = map(sem, ["proj_done", "proj_act", "proj_dve"])
        sq_ready, sq_used, sum_done, var_ready, root_ready, rstd_ready, bc_done, normed = (
            sem(n) for n in
            ["sq_ready", "sq_used", "sum_done", "var_ready", "root_ready", "rstd_ready", "bc_done", "normed"])
        fl_done, fl_copied, dtl_done, dtl_copied, dt_step, dt_ready, a_exp = map(
            sem, ["fl_done", "fl_copied", "dtl_done", "dtl_copied", "dt_step", "dt_ready", "a_exp"])
        gk_done, gk_copied, gk_step, gk_ready, v_done, v_copied = map(
            sem, ["gk_done", "gk_copied", "gk_step", "gk_ready", "v_done", "v_copied"])
        b_done, b_copied, eb_ready, suf_done, suf_exp, ktok_done, khat_ready, qb_ready = map(
            sem, ["b_done", "b_copied", "eb_ready", "suf_done", "suf_exp", "ktok_done", "khat_ready", "qb_ready"])
        e_arg, e_exp, e_q, e_k, attn_used, attn_done, mt_ready, khm_ready = map(
            sem, ["e_arg", "e_exp", "e_q", "e_k", "attn_used", "attn_done", "mt_ready", "khm_ready"])
        s_zero, local_done, s_updated, inter_done, o_done, o_copied = map(
            sem, ["s_zero", "local_done", "s_updated", "inter_done", "o_done", "o_copied"])
        gsq_ready, gsum_done, gvar_ready, groot_ready, grstd_ready, gbc_done, g_normed, g_mixed = map(
            sem, ["gsq_ready", "gsum_done", "gvar_ready", "groot_ready", "grstd_ready", "gbc_done", "g_normed", "g_mixed"])
        xp_zero, conv_done, xc_ready, tr_done, tr_copied = map(
            sem, ["xp_zero", "conv_done", "xc_ready", "tr_done", "tr_copied"])
        pre_done, ecb_ready, wx_ready, ncum_ready, z_ready, l_exp, m_ready, ct_ready, xw_ready = map(
            sem, ["pre_done", "ecb_ready", "wx_ready", "ncum_ready", "z_ready", "l_exp", "m_ready", "ct_ready", "xw_ready"])
        y_done, y_copied, hloc_done, h_updated, xwm_ready, yz_ready = map(
            sem, ["y_done", "y_copied", "hloc_done", "h_updated", "xwm_ready", "yz_ready"])
        score_done, score_copied, top_sorted, sm_arg, sm_exp, pick_in, pick_mul, e_ready, e_turned, e_copied = map(
            sem, ["score_done", "score_copied", "top_sorted", "sm_arg", "sm_exp", "pick_in", "pick_mul", "e_ready", "e_turned", "e_copied"])
        one_hot_ready, gate_done, gate_copied = map(
            sem, ["one_hot_ready", "gate_done", "gate_copied"])
        gate_stored = [sem(f"gate_stored{x}") for x in range(2)]
        xh_ready, xl_ready, uhi_ready, ulo_ready, hid_done, gelu_ready = map(
            sem, ["xh_ready", "xl_ready", "uhi_ready", "ulo_ready", "hid_done", "gelu_ready"])
        vhi_ready, vlo_ready, gated, whi_ready, wlo_ready, acc_done, acc_added = map(
            sem, ["vhi_ready", "vlo_ready", "gated", "whi_ready", "wlo_ready", "acc_done", "acc_added"])
        chain, achain = sem("chain"), sem("achain")

        def proj_dst_is_dve(n):
            return N_FEAT <= n < N_FEAT + KT

        def wait_gates_stored(eng):
            eng.wait_ge(gate_stored[0], 16 * (NBLK - NBLK // 2))
            eng.wait_ge(gate_stored[1], 16 * (NBLK // 2))

        def xtok3(i):
            return xtok[0:rows(i), i, :].rearrange("p (h q) -> p h q", h=SH)

        def attn_matrix(dve, i):
            r, nch = rows(i), rows(i) // C
            dve.wait_ge(attn_used, 2 * i + 2)
            dve.tensor_tensor(MT[0:r, i, :].rearrange("p (h c t) -> p h c t", h=GH, t=C)[:, :, 0:nch, :],
                              bc(bank[i % 2][0:r, 0:GH * C].rearrange("p (h t) -> p h t", h=GH), 2, nch),
                              bc(cc("incl_a" if i < 4 else "incl_b", r)[:, 0:r].rearrange("p (c t) -> p c t", t=C), 1, GH),
                              ALU.mult).then_inc(mt_ready, 1)

        def wait_proj_evacuated(eng, n):
            m = n - 2
            if m < 0:
                return
            if proj_dst_is_dve(m):
                eng.wait_ge(proj_dve, m - N_FEAT + 1)
            else:
                eng.wait_ge(proj_act, m + 1 - (KT if m >= N_FEAT + KT else 0))

        norm_src = [(h, KT), (mix, 4), (h, KT), (h, KT)]
        norm_base = [0, KT, KT + 4, 2 * KT + 4]
        norm_par = ["norm1", "ssd_w", "norm2", "final"]

        block = base.enter_context(nc.Block())

        @block.sync
        def _(sp):
            for k in range(KT):
                sp.dma_start(h[:, k, :], d["xT"][:, k, :]).then_inc(x_loaded, 16)
            sp.dma_start(cst[:, :], d["const"]).then_inc(const_loaded, 16)
            sp.dma_start(prm[:, :], d["param"]).then_inc(const_loaded, 16)
            sp.dma_start(row[:, :], d["rows"]).then_inc(small_loaded, 16)
            sp.dma_start(small[:, :, :], d["wsmall"]).then_inc(small_loaded, 16)
            sp.dma_start(wgk[:, :], d["w_gk2"]).then_inc(small_loaded, 16)
            sp.dma_start(wv_sb, d["wv"]).then_inc(wv_loaded, 16)

            def load_w(n):
                if n >= 4:
                    sp.wait_ge(proj_done, n - 3)
                sp.dma_start(ring[:, n % 4, :], d["wproj"][n]).then_inc(w_loaded[n % 4], 16)

            for n in range(12):
                load_w(n)
            sp.dma_start(Ssm[:, :, :, :], d["s_gla"]).then_inc(sgla_loaded, 16)
            for n in range(12, N_FEAT):
                if n == 12:
                    sp.wait_ge(s_updated, PROMPT_CHUNKS)
                    sp.dma_start(o["gla_p"], S[:, PROMPT_CHUNKS % 2, :, :]).then_inc(stored, 16)
                    sp.wait_ge(s_updated, CHUNKS)
                    sp.dma_start(o["gla_s"], Ssm[:, :, :, :]).then_inc(stored, 16)
                    sp.wait_ge(stored, 32)
                    sp.wait_ge(g_mixed, 4)
                    for f in range(CT):
                        sp.dma_start(xp[:, f, XPW:XP].rearrange("p (b t) -> p b t", b=NSEQ)[:, :, 0:CONV - 1],
                                     d["s_conv"][:, f, :, :]).then_inc(hist_loaded, 16)
                    sp.dma_start(Hsm[:, :, :], d["s_ssm"]).then_inc(hsm_loaded, 16)
                load_w(n)
            for n in range(N_FEAT, N_FEAT + 4):
                load_w(n)
            sp.wait_ge(proj_act, N_FEAT)
            sp.wait_ge(hist_loaded, 16 * CT)
            sp.dma_start(o["conv_p"], xp[:, :, XPW - (CONV - 1):XPW]).then_inc(stored, 16)
            for f in range(CT):
                sp.dma_start(o["conv_s"][:, f, :, :],
                             xp[:, f, XPW:XP].rearrange("p (b t) -> p b t", b=NSEQ)[:, :, SLEN:XPS]).then_inc(stored, 16)
            sp.wait_ge(h_updated, TILES)
            sp.dma_start(o["ssm_p"], H[:, TILES % 2, :]).then_inc(stored, 16)
            sp.wait_ge(h_updated, TILES + NSEQ)
            sp.dma_start(o["ssm_s"], Hsm[:, :, :]).then_inc(stored, 16)
            sp.wait_ge(stored, 16 * (2 + 1 + CT + 2))
            for n in range(N_FEAT + 4, N_PROJ):
                load_w(n)
                if n == N_FEAT + KT + 4:
                    sp.wait_ge(proj_done, N_FEAT + KT)
                    sp.dma_start(keys[:, :], d["keys"]).then_inc(keys_loaded, 16)
            def load_u(n, j):
                sp.dma_start(ring[:, j, :], d["u"][bass.ds(n, 1), :, :].rearrange("a p n -> p (a n)")
                             ).then_inc(u_loaded[j], 16)

            def quad(q, last=False):
                for j in range(4):
                    n = q * 4 + j
                    if not last:
                        sp.wait_ge(ulo_ready, n + 1)
                        load_u(n + 4, j)
                    sp.wait_ge(gelu_ready, n + 1)
                    sp.dma_start(hid_dram[bass.ds(n, 1), :, :].rearrange("a p t -> p (a t)"), gl[:, j, :]
                                 ).then_inc(hid_stored[j], 16)

            def store_gates(b, x):
                sp.wait_ge(gate_copied, (b + 1) * (TB // 4))
                sp.dma_start(gates_dram[:, :, bass.ds(b * TB, TB), :].rearrange("g p t j -> p g (t j)"),
                             stage[:, x, :, :, :].rearrange("p g t j -> p g (t j)")).then_inc(gate_stored[x], 16)

            for j in range(4):
                sp.wait_ge(proj_done, N_PROJ - 3 + j)
                load_u(j, j)
            with sp.Fori(0, 18) as q:
                quad(q)
            with sp.Fori(0, 6) as it:
                for y in range(2):
                    quad(it * 2 + (18 + y))
                    for z in range(3):
                        store_gates(it * 6 + (3 * y + z), (y + z) % 2)
            store_gates(NBLK - 1, 0)
            quad(30)
            def load_v(m, g, y, j):
                sp.dma_start(ring[:, j, :], d["v"][:, bass.ds(g, 1), 4 * y + j, :].rearrange("p a n -> p (a n)")
                             ).then_inc(v_loaded[j], 16)

            for j in range(4):
                sp.wait_ge(ulo_ready, NE - 3 + j)
                load_v(0, 0, 0, j)
            quad(31, last=True)
            wait_gates_stored(sp)
            sp.wait_ge(xl_ready, KT)

            def load_group(g, par, first=False):
                if not first:
                    sp.wait_ge(gated, (g - 1) * GRP)
                sp.dma_start(G[:, par, :, :], gates_dram[bass.ds(g, 1), :, :, :].rearrange("a p t j -> p (a t) j")
                             ).then_inc(g_loaded[par], 16)
                for y in range(2):
                    for j in range(4):
                        n = g * GRP + (4 * y + j)
                        if not (first and g == 0):
                            sp.wait_ge(gated, n - 7)
                        sp.wait_ge(hid_stored[j], (g * 2 + (y + 1)) * 16)
                        sp.dma_start(xn[:, 4 * y + j, :], hid_dram[bass.ds(n, 1), :, :].rearrange("a p t -> p (a t)")
                                     ).then_inc(hid_loaded[4 * y + j], 16)
                        if not (first and g == 0 and y == 0):
                            sp.wait_ge(vlo_ready, n - 3)
                            load_v(g * 2 + y, g, y, j)

            load_group(0, 0, first=True)
            load_group(1, 1, first=True)
            with sp.Fori(1, NGRP // 2) as pair:
                g = pair * 2
                load_group(g, 0)
                load_group(g + 1, 1)
            for k in range(KT):
                sp.wait_ge(normed, norm_base[3] + k + 1)
                sp.dma_start(o["yT"][:, k, :], xn[:, k, :]).then_inc(stored, 16)
            sp.wait_ge(stored, 16 * (2 + 1 + CT + 2 + KT))

        @block.tensor
        def _(pe):
            def norm(m):
                _, n = norm_src[m]
                for k in range(n):
                    pe.wait_ge(sq_ready, norm_base[m] + k + 1)
                    for i in range(TILES):
                        mm = pe.matmul(bank[4][0:rows(i), i:i + 1], sq[:, k % 2, cols(i)], ones[:, 0:1],
                                       start=(k == 0 and i == 0), stop=(k == n - 1), skip_group_check=True)
                    mm.then_inc(sq_used, 1)
                pe.wait_ge(rstd_ready, m + 1)
                for i in range(TILES):
                    out = bank[6][:, cols(i)] if i < 4 else bank[7][:, 0:rows(i)]
                    mm = pe.matmul(out, stat[0:rows(i), 2 * m + 1, i:i + 1].broadcast_to([rows(i), P]),
                                   ident[0:rows(i), 0:rows(i)], start=True, stop=True)
                mm.then_inc(bc_done, 1)

            def project(n, src, src_ready=None):
                pe.wait_ge(w_loaded[n % 4], 16 * (n // 4 + 1))
                wait_proj_evacuated(pe, n)
                for x in range(2):
                    for k in range(KT):
                        mm = pe.matmul(bank[2 * (n % 2) + x][:, 0:HALF], ring[:, n % 4, k * P:(k + 1) * P],
                                       src[:, k, x * HALF:(x + 1) * HALF], start=(k == 0), stop=(k == KT - 1))
                mm.then_inc(proj_done, 1)

            pe.wait_ge(const_loaded, 32)
            norm(0)
            pe.wait_ge(normed, norm_base[0] + KT)
            pe.wait_ge(small_loaded, 48)
            for x in range(2):
                for k in range(KT):
                    mm = pe.matmul(bank[x][0:RANK, 0:HALF], small[:, k, 0:RANK], xn[:, k, x * HALF:(x + 1) * HALF],
                                   start=(k == 0), stop=(k == KT - 1))
            mm.then_inc(fl_done, 1)
            for i in range(TILES):
                out = bank[5][0:rows(i), SH * i:SH * i + SH]
                for k in range(KT):
                    pe.matmul(out, xn[:, k, cols(i)], small[:, k, RANK:RANK + SH], start=(k == 0), stop=False)
                mm = pe.matmul(out, ones[0:1, 0:rows(i)], row[0:1, GH * DK:GH * DK + SH], start=False, stop=True)
            mm.then_inc(dtl_done, 1)
            pe.wait_ge(fl_copied, 2)
            for i in range(TILES):
                out = bank[6 + i % 2][0:rows(i), 0:GH * DK]
                if i >= 2:
                    pe.wait_ge(gk_copied, i - 1)
                pe.matmul(out, fl[:, cols(i)], wgk[:, :], start=True, stop=False)
                pe.matmul(out, ones[0:1, 0:rows(i)], row[0:1, 0:GH * DK], start=False, stop=True).then_inc(gk_done, 1)
            pe.wait_ge(wv_loaded, 16)
            for i in range(TILES):
                if i >= 2:
                    pe.wait_ge(v_copied, i - 1)
                for k in range(KT):
                    mm = pe.matmul(bank[2 + i % 2][0:rows(i), :], xn[:, k, cols(i)], wv_sb[:, k, :],
                                   start=(k == 0), stop=(k == KT - 1))
                mm.then_inc(v_done, 1)
            pe.wait_ge(gk_ready, 1)
            pe.wait_ge(dtl_copied, 1)
            for p in range(NP):
                for i in range(TILES):
                    out = bank[4 + p][:, cols(i)] if i < 4 else bank[6][:, p * P:p * P + rows(i)]
                    mm = pe.matmul(out, gk[0:rows(i), i, p * P:(p + 1) * P],
                                   cc("incl_a" if i < 4 else "incl_b", rows(i))[:, 0:rows(i)], start=True, stop=True)
            mm.then_inc(b_done, 1)
            for i in range(TILES):
                out = [bank[7][:, 0:256], bank[7][:, 256:512], bank[0][:, 0:256], bank[0][:, 256:512],
                       bank[1][0:rows(4), 0:256]][i]
                mm = pe.matmul(out, cc("suf_a" if i < 4 else "suf_b", rows(i))[:, 0:rows(i)], gk[0:rows(i), i, :],
                               start=True, stop=True)
            mm.then_inc(suf_done, 1)
            pe.wait_ge(v_copied, TILES)
            pe.wait_ge(suf_exp, 3)
            for n in range(4):
                project(n, xn)
            pe.wait_ge(b_copied, 4)
            pe.wait_ge(proj_act, 4)
            for i in range(TILES):
                for p in range(NP):
                    mm = pe.transpose(bank[4 + i // 2][0:rows(i), (i % 2) * 256 + p * P:(i % 2) * 256 + (p + 1) * P],
                                      kT[:, p, cols(i)], ident)
            mm.then_inc(ktok_done, 1)
            for n in range(4, 12):
                project(n, xn)
            pe.wait_ge(proj_act, 12)
            for i in range(TILES):
                if i >= 2:
                    pe.wait_ge(mt_ready, i - 1)
                for p in range(NP):
                    u = 2 * i + p
                    pe.wait_ge(e_k, u + 1)
                    src = E[:, u % 2, 0:rows(i) * C].rearrange("p (t n) -> p t n", t=C)
                    for t in range(C):
                        out = bank[i % 2][0:rows(i), p * 2 * C + t:p * 2 * C + C + t + 1:C]
                        mm = pe.matmul(out, src[:, t, :], cc("head2"), start=True, stop=True)
                    mm.then_inc(attn_used, 1)
            pe.wait_ge(khat_ready, 1)
            n = 0
            for i in range(TILES):
                r = rows(i)
                ob = [bank[(2, 6)[i % 2] + x] for x in range(2)]
                pe.wait_ge(mt_ready, i + 1)
                pe.wait_ge(khm_ready, i + 1)
                if i >= 2:
                    pe.wait_ge(o_copied, i - 1)
                for hh in range(GH):
                    pe.matmul(ob[hh % 2][:, hh // 2 * P:hh // 2 * P + r], V[0:r, i, hh * DV:(hh + 1) * DV], MT[0:r, i, hh * P:hh * P + r],
                              start=(hh < 2), stop=True, skip_group_check=True)
                for c in range(P // C if i < 4 else SEGS):
                    a, b = (c * C, c * C + C) if i < 4 else seg_cols(c)
                    if n >= 2:
                        pe.wait_ge(s_updated, n - 1)
                    for hh in range(GH):
                        q = (hh % 2) * DK
                        mm = pe.matmul(bank[4 + n % 2][q:q + DK, (hh // 2) * P:(hh // 2) * P + DV],
                                       khm[i % 2][0:r, c, hh * DK:(hh + 1) * DK], V[0:r, i, hh * DV:(hh + 1) * DV],
                                       start=True, stop=True)
                    mm.then_inc(local_done, 1)
                    sample = i == 4 and c > 0
                    if sample:
                        pe.wait_ge(sgla_loaded, 16)
                    elif n == 0:
                        pe.wait_ge(s_zero, 1)
                    else:
                        pe.wait_ge(s_updated, n)
                    for hh in range(GH):
                        q = (hh % 2) * DK
                        src = Ssm[q:q + DK, c - 1, hh // 2, :] if sample else S[q:q + DK, n % 2, hh // 2, :]
                        mm = pe.matmul(ob[hh % 2][:, hh // 2 * P + a:hh // 2 * P + b], src, qb[q:q + DK, hh // 2, P * i + a:P * i + b],
                                       start=False, stop=True, skip_group_check=True)
                    mm.then_inc(inter_done, 1)
                    n += 1
            pe.wait_ge(gsq_ready, 1)
            pe.wait_ge(s_updated, CHUNKS)
            for i in range(TILES):
                for hh in range(GH):
                    mm = pe.matmul(bank[4][0:rows(i), i * GH + hh:i * GH + hh + 1], gsq[:, hh, cols(i)], ones[:, 0:1],
                                   start=True, stop=True)
            mm.then_inc(gsum_done, 1)
            pe.wait_ge(grstd_ready, 1)
            for hh in range(GH):
                for i in range(TILES):
                    out = bank[hh][:, cols(i)] if i < 4 else bank[5][:, hh * P:hh * P + rows(i)]
                    mm = pe.matmul(out, gstat[0:rows(i), 1, i * GH + hh:i * GH + hh + 1].broadcast_to([rows(i), P]),
                                   ident[0:rows(i), 0:rows(i)], start=True, stop=True)
            mm.then_inc(gbc_done, 1)
            pe.wait_ge(g_normed, 8)
            for n in range(12, N_FEAT):
                project(n, xn)
            pe.wait_ge(proj_act, N_FEAT)
            pe.wait_ge(xc_ready, 6)
            for i in range(TILES):
                if i >= 2:
                    pe.wait_ge(tr_copied, 2 * (i - 1))
                for f in range(6):
                    out = bank[4 + i % 2][0:rows(i), f * P:(f + 1) * P] if f < 4 else \
                        bank[6 + i % 2][0:rows(i), (f - 4) * P:(f - 3) * P]
                    mm = pe.transpose(out, xc[:, f, cols(i)], ident)
                mm.then_inc(tr_done, 1)
            pe.wait_ge(xc_ready, CT)
            pe.wait_ge(dt_ready, 1)
            pe.wait_ge(tr_copied, 2 * TILES)
            for i in range(TILES):
                r = rows(i)
                incl = cc("tincl_a" if i < 4 else "incl_b", r)[:, 0:r]
                suf = cc("tsuf_a" if i < 4 else "suf_b", r)[:, 0:r]
                if i >= 1:
                    pe.wait_ge(z_ready, i)
                    pe.wait_ge(ecb_ready, i)
                    pe.wait_ge(wx_ready, i)
                    pe.wait_ge(ncum_ready, i)
                    pe.wait_ge(m_ready, i)
                for hh in range(SH):
                    pe.matmul(bank[hh // 4][:, (hh % 4) * P:(hh % 4) * P + r],
                              dta[0:r, i, hh:hh + 1].broadcast_to([r, P]), incl, start=True, stop=True)
                pe.matmul(bank[3][0:r, 0:SH], incl, dta[0:r, i, :], start=True, stop=True)
                pe.matmul(bank[3][0:r, SH:2 * SH], suf, dta[0:r, i, :], start=True, stop=True)
                for g in range(SG):
                    mm = pe.matmul(bank[2][0:r, g * P:g * P + r], xc[:, 4 + g, cols(i)], xc[:, 6 + g, cols(i)],
                                   start=True, stop=True)
                mm.then_inc(pre_done, 1)
                pe.wait_ge(m_ready, i + 1)
                pe.wait_ge(ct_ready, i + 1)
                pe.wait_ge(xw_ready, i + 1)
                if i >= 1:
                    pe.wait_ge(y_copied, i)
                    pe.wait_ge(h_updated, i)
                else:
                    pe.wait_ge(s_zero, 2)
                if i == 4:
                    pe.wait_ge(hsm_loaded, 16)
                for hh in range(SH):
                    q = (hh % 2) * HD
                    out = bank[4][q:q + HD, (hh // 2) * P:(hh // 2) * P + r]
                    pe.matmul(out, Xd[0:r, hh * HD:(hh + 1) * HD], L[0:r, hh, 0:r], start=True, stop=(i == 4))
                    if i < 4:
                        mm = pe.matmul(out, H[:, i % 2, hh * HD:(hh + 1) * HD], Ct[:, hh, :], start=False, stop=True)
                    else:
                        for c in range(SEGS):
                            a, b = seg_cols(c)
                            src = H[:, i % 2, hh * HD:(hh + 1) * HD] if c == 0 else Hsm[:, c - 1, hh * HD:(hh + 1) * HD]
                            mm = pe.matmul(out[:, a:b], src, Ct[:, hh, a:b], start=False, stop=True,
                                           skip_group_check=True)
                mm.then_inc(y_done, 1)
                for c in range(1 if i < 4 else SEGS):
                    if i == 4:
                        pe.wait_ge(xwm_ready, c + 1)
                        if c >= 1:
                            pe.wait_ge(h_updated, i + c)
                    src = XW[0:r, :] if i < 4 else XWm[0:r, c % 2, :]
                    for g in range(SG):
                        mm = pe.matmul(bank[5][:, g * 256:(g + 1) * 256], btok[0:r, i, g * DS:(g + 1) * DS],
                                       src[:, g * 256:(g + 1) * 256], start=True, stop=True)
                    mm.then_inc(hloc_done, 1)
            pe.wait_ge(h_updated, TILES + NSEQ)
            norm(1)
            pe.wait_ge(normed, norm_base[1] + 4)
            for n in range(N_FEAT, N_FEAT + KT):
                project(n, mix)
            norm(2)
            pe.wait_ge(normed, norm_base[2] + KT)
            for n in range(N_FEAT + KT, N_PROJ):
                project(n, xn)
            pe.wait_ge(proj_act, N_PROJ - KT)
            pe.wait_ge(keys_loaded, 16)

            def turn_picks(i):
                pe.wait_ge(e_ready, i + 1)
                if i >= 1:
                    pe.wait_ge(e_copied, i)
                for x in range(3):
                    mm = pe.transpose(bank[4][:, x * P:x * P + rows(i)], e12[0:rows(i), x, :, :].rearrange("p h k -> p (h k)"),
                                      ident[0:rows(i), 0:rows(i)])
                mm.then_inc(e_turned, 1)

            def scores(i):
                if i >= 1:
                    pe.wait_ge(score_copied, 4 * i)
                    if i >= 2:
                        pe.wait_ge(e_copied, i - 1)
                for half in range(2):
                    for hh in range(PH):
                        q = half * 64
                        mm = pe.matmul(bank[4 + 2 * half + hh // 4][0:rows(i), (hh % 4) * NK:(hh % 4 + 1) * NK],
                                       qh[q:q + 64, hh, cols(i)], keys[q:q + 64, :], start=True, stop=True)
                mm.then_inc(score_done, 1)

            def quad(q, first=False):
                for j in range(4):
                    n = q * 4 + j
                    x = j % 2
                    pe.wait_ge(ulo_ready, n + 1)
                    if not (first and j < 2):
                        pe.wait_ge(gelu_ready, n - 1)
                    for k in range(KT):
                        hi, lo = (usp[:, x, z, k * P:(k + 1) * P] for z in range(2))
                        for w, src in ((hi, xh), (hi, xl), (lo, xh)):
                            for y in range(2):
                                mm = pe.matmul(bank[2 * x + y][:, 0:HALF], w, src[:, k, y * HALF:(y + 1) * HALF],
                                               start=(k == 0 and w is hi and src is xh), stop=(k == KT - 1 and w is lo))
                    mm.then_inc(hid_done, 1)

            def gate_block(b, x, first=False):
                pe.wait_ge(one_hot_ready, b + 1)
                for q in range(TB // 4):
                    if not first:
                        pe.wait_ge(gate_copied, b * (TB // 4) + q - 3)
                    for t in range(4):
                        for z in range(2):
                            mm = pe.matmul(bank[4 + q][:, t * NK:(t + 1) * NK], oneA[:, x, 4 * q + t, z, :],
                                           oneB[:, x, 4 * q + t, :], start=(z == 0), stop=(z == 1))
                    mm.then_inc(gate_done, 1)

            pe.wait_ge(xl_ready, KT)
            for i in range(TILES):
                scores(i)
                quad(ROUTE_QUADS * i, first=(i == 0))
                if i >= 1:
                    pe.wait_ge(score_copied, 4 * i + 4)
                    turn_picks(i - 1)
                with pe.Fori(ROUTE_QUADS * i + 1, ROUTE_QUADS * (i + 1)) as q:
                    quad(q)
            quad(15)
            turn_picks(TILES - 1)
            pe.wait_ge(e_copied, TILES)
            quad(16)
            quad(17)
            for y in range(2):
                quad(18 + y)
                for z in range(3):
                    gate_block(3 * y + z, (y + z) % 2, first=(y + z == 0))
            with pe.Fori(1, 6) as it:
                for y in range(2):
                    quad(it * 2 + (18 + y))
                    for z in range(3):
                        gate_block(it * 6 + (3 * y + z), (y + z) % 2)
            gate_block(NBLK - 1, 0)
            quad(30)
            quad(31)
            pe.wait_ge(gelu_ready, NE)
            pe.wait_ge(gate_copied, NBLK * (TB // 4))

            def second(m, par, first=False):
                pe.wait_ge(vlo_ready, m * 4 + 4)
                pe.wait_ge(wlo_ready, m * 4 + 4)
                for k in range(KT):
                    if not (first and k < 4):
                        pe.wait_ge(acc_added, m * KT + (k - 3))
                    for j in range(4):
                        hi, lo = (vsp[:, par, j, z, k * P:(k + 1) * P] for z in range(2))
                        for w, z in ((hi, 0), (hi, 1), (lo, 0)):
                            for y in range(2):
                                mm = pe.matmul(bank[2 * (k % 4) + y][:, 0:HALF], w, W[:, par, j, z, y * HALF:(y + 1) * HALF],
                                               start=(j == 0 and w is hi and z == 0), stop=(j == 3 and w is lo))
                    mm.then_inc(acc_done, 1)

            second(0, 0, first=True)
            second(1, 1)
            with pe.Fori(1, NE // 8) as pair:
                second(pair * 2, 0)
                second(pair * 2 + 1, 1)
            norm(3)

        @block.scalar
        def _(act):
            linked = [0]

            def link(ins):
                linked[0] += 1
                ins.then_inc(achain, 1)
                act.wait_ge(achain, linked[0])

            def norm(m):
                src, n = norm_src[m]
                off = 4 if m == 1 else 0
                for k in range(n):
                    if k >= 2:
                        act.wait_ge(sq_used, norm_base[m] + k - 1)
                    act.activation(sq[:, k % 2, :], src[:, off + k, :], ACT.Square).then_inc(sq_ready, 1)
                act.wait_ge(var_ready, m + 1)
                act.activation(stat[:, 2 * m, 0:TILES], stat[:, 2 * m, 0:TILES], ACT.Sqrt).then_inc(root_ready, 1)

            def from_pair(n, dst, func=ACT.Copy, scale=1.0):
                act.wait_ge(proj_done, n + 1)
                for x in range(2):
                    ins = act.activation(dst[:, x * HALF:(x + 1) * HALF], bank[2 * (n % 2) + x][:, 0:HALF], func, scale=scale)
                ins.then_inc(proj_act, 1)

            act.wait_ge(x_loaded, 16 * KT)
            norm(0)
            act.wait_ge(const_loaded, 32)
            act.activation(na[:, :], pp("a_log"), ACT.Exp).then_inc(a_exp, 1)
            act.wait_ge(fl_done, 1)
            for x in range(2):
                act.activation(fl[:, x * HALF:(x + 1) * HALF], bank[x][0:RANK, 0:HALF], ACT.Copy).then_inc(fl_copied, 1)
            act.wait_ge(dtl_copied, 1)
            link(act.activation(dt[:, 1, :], dt[:, 0, :], ACT.Abs))
            act.activation(dt[:, 1, :], dt[:, 1, :], ACT.Exp, scale=-1.0).then_inc(dt_step, 1)
            act.wait_ge(dt_step, 2)
            act.activation(dt[:, 3, :], dt[:, 2, :], ACT.Ln).then_inc(dt_step, 1)
            act.wait_ge(gk_copied, TILES)
            link(act.activation(tmp[:, 0, :, :], gk[:, :, :], ACT.Abs))
            act.activation(tmp[:, 0, :, :], tmp[:, 0, :, :], ACT.Exp, scale=-1.0).then_inc(gk_step, 1)
            act.wait_ge(gk_step, 3)
            act.activation(tmp[:, 1, :, :], tmp[:, 1, :, :], ACT.Ln).then_inc(gk_step, 1)
            for i in range(TILES):
                act.wait_ge(v_done, i + 1)
                act.activation(V[0:rows(i), i, :], bank[2 + i % 2][0:rows(i), :], ACT.Copy).then_inc(v_copied, 1)
            act.wait_ge(b_done, 1)
            for p in range(NP):
                act.activation(bT[:, p, 0:512], bank[4 + p][:, :], ACT.Copy).then_inc(b_copied, 1)
                act.activation(bT[:, p, 512:T], bank[6][:, p * P:p * P + rows(4)], ACT.Copy).then_inc(b_copied, 1)
            act.wait_ge(b_copied, 4)
            act.activation(eb[:, :, :], bT[:, :, :], ACT.Exp).then_inc(eb_ready, 1)
            act.wait_ge(suf_done, 1)
            act.activation(khat[:, 0:2, :], bank[7][:, :].rearrange("p (a b) -> p a b", a=2), ACT.Exp).then_inc(suf_exp, 1)
            act.activation(khat[:, 2:4, :], bank[0][:, :].rearrange("p (a b) -> p a b", a=2), ACT.Exp).then_inc(suf_exp, 1)
            act.activation(khat[0:rows(4), 4, :], bank[1][0:rows(4), 0:256], ACT.Exp).then_inc(suf_exp, 1)
            for n in range(4):
                from_pair(n, (qT if n < 2 else kT)[:, n % 2, :], scale=(DK ** -0.5 if n < 2 else 1.0))

            def decay(u):
                act.wait_ge(e_arg, u + 1)
                e = E[:, u % 2, 0:rows(u // 2) * C]
                act.activation(e, e, ACT.Exp).then_inc(e_exp, 1)

            for n in range(4, 12):
                from_pair(n, (sg if n < 8 else sz)[:, n % 4, :], ACT.Silu)
            for u in range(2 * TILES):
                decay(u)
            n = 0
            for i in range(TILES):
                n += P // C if i < 4 else SEGS
                act.wait_ge(inter_done, n)
                for x in range(2):
                    src = bank[(2, 6)[i % 2] + x][:, 0:2 * P].rearrange("p (h t) -> p h t", h=2)[:, :, 0:rows(i)]
                    ins = act.activation(mix[:, x:GH:2, cols(i)], src, ACT.Copy)
                ins.then_inc(o_copied, 1)
            act.wait_ge(o_copied, TILES)
            act.activation(gsq, mix[:, 0:GH, :], ACT.Square).then_inc(gsq_ready, 1)
            act.wait_ge(gvar_ready, 1)
            act.activation(gstat[:, 0, :], gstat[:, 0, :], ACT.Sqrt).then_inc(groot_ready, 1)
            act.wait_ge(g_mixed, 4)
            act.wait_ge(xp_zero, 1)
            act.wait_ge(stored, 32)
            for f in range(CT):
                n = 12 + f
                act.wait_ge(proj_done, n + 1)
                b0, b1 = bank[2 * (n % 2)], bank[2 * (n % 2) + 1]
                act.activation(xp[:, f, 3:3 + HALF], b0[:, 0:HALF], ACT.Copy)
                act.activation(xp[:, f, 3 + HALF:XPW], b1[:, 0:NPROMPT - HALF], ACT.Copy)
                act.activation(xp[:, f, XPW:XP].rearrange("p (b t) -> p b t", b=NSEQ)[:, :, CONV - 1:XPS],
                               b1[:, NPROMPT - HALF:HALF].rearrange("p (b t) -> p b t", b=NSEQ), ACT.Copy
                               ).then_inc(proj_act, 1)
            for f in range(CT):
                act.wait_ge(conv_done, f + 1)
                act.activation(xc[:, f, :], xc[:, f, :], ACT.Silu).then_inc(xc_ready, 1)
            for i in range(TILES):
                act.wait_ge(tr_done, i + 1)
                act.activation(xtok[0:rows(i), i, :], bank[4 + i % 2][0:rows(i), :], ACT.Copy).then_inc(tr_copied, 1)
                act.activation(btok[0:rows(i), i, :], bank[6 + i % 2][0:rows(i), 0:256], ACT.Copy).then_inc(tr_copied, 1)
            for i in range(TILES):
                r = rows(i)
                act.wait_ge(z_ready, i + 1)
                act.wait_ge(ncum_ready, i + 1)
                if i >= 1:
                    act.wait_ge(ct_ready, i)
                    act.wait_ge(h_updated, i)
                    act.wait_ge(xw_ready, i)
                for g in range(2):
                    ins = act.activation(ecb[:, 4 * g:4 * g + 4, 0:r],
                                         bank[g][:, :].rearrange("p (h t) -> p h t", h=4)[:, :, 0:r], ACT.Exp)
                ins.then_inc(ecb_ready, 1)
                act.activation(cum[0:r, 1, :], bank[3][0:r, SH:2 * SH], ACT.Exp).then_inc(wx_ready, 1)
                for hh in range(SH):
                    ins = act.activation(L[0:r, hh, 0:r], L[0:r, hh, 0:r], ACT.Exp, bias=cum[0:r, 0, hh:hh + 1])
                ins.then_inc(l_exp, 1)
            act.wait_ge(yz_ready, 4)
            norm(1)
            act.wait_ge(proj_dve, KT)
            norm(2)
            for k in range(KT):
                act.wait_ge(normed, norm_base[2] + k + 1)
                act.activation(xh[:, k, :], xn[:, k, :], ACT.Copy).then_inc(xh_ready, 1)
            for n in range(N_FEAT + KT, N_PROJ):
                from_pair(n, qh[:, n - N_FEAT - KT, :])

            def split_u(n, j, round_):
                act.wait_ge(u_loaded[j % 4], (round_ + j // 4 + 1) * 16)
                act.activation(usp[:, j % 2, 0, :], ring[:, j % 4, :], ACT.Copy).then_inc(uhi_ready, 1)

            def quad(q, first=False, last=False):
                for j in range(4):
                    n = q * 4 + j
                    act.wait_ge(hid_done, n + 1)
                    if not (last and j >= 2):
                        split_u(n + 2, j + 2, q)
                    if not first:
                        act.wait_ge(hid_stored[j], q * 16)
                    for y in range(2):
                        ins = act.activation(gl[:, j, y * HALF:(y + 1) * HALF], bank[2 * (j % 2) + y][:, 0:HALF],
                                             ACT.Gelu_apprx_tanh)
                    ins.then_inc(gelu_ready, 1)

            def copy_picks(i):
                act.wait_ge(e_turned, i + 1)
                for x, dst in enumerate((e1T, e2T, gT)):
                    ins = act.activation(dst[:, cols(i)], bank[4][:, x * P:x * P + rows(i)], ACT.Copy)
                ins.then_inc(e_copied, 1)

            split_u(0, 0, 0)
            split_u(1, 1, 0)
            for i in range(TILES):
                r = rows(i)
                act.wait_ge(score_done, i + 1)
                if i >= 1:
                    act.wait_ge(top_sorted, i)
                for x in range(4):
                    act.activation(s12[0:r, 4 * x:4 * x + 4, :], bank[4 + x][0:r, :].rearrange("p (h k) -> p h k", h=4),
                                   ACT.Copy).then_inc(score_copied, 1)
                quad(ROUTE_QUADS * i, first=(i == 0))
                if i >= 1:
                    copy_picks(i - 1)
                with act.Fori(ROUTE_QUADS * i + 1, ROUTE_QUADS * (i + 1)) as q:
                    quad(q)
                act.wait_ge(sm_arg, i + 1)
                act.activation(e12[0:r, 2, :, :], e12[0:r, 2, :, :], ACT.Exp).then_inc(sm_exp, 1)
            quad(15)
            copy_picks(TILES - 1)

            def gates_out(b, x, first=False):
                if not first:
                    act.wait_ge(gate_stored[x], (b - x) * 8)
                for q in range(TB // 4):
                    act.wait_ge(gate_done, b * (TB // 4) + q + 1)
                    act.activation(stage[:, x, :, 4 * q:4 * q + 4, :].rearrange("p g t j -> p t g j"),
                                   bank[4 + q][:, :].rearrange("p (t g j) -> p t g j", t=4, j=GRP), ACT.Copy
                                   ).then_inc(gate_copied, 1)

            quad(16)
            quad(17)
            for y in range(2):
                quad(18 + y)
                for z in range(3):
                    b = 3 * y + z
                    gates_out(b, b % 2, first=(b < 2))
            with act.Fori(1, 6) as it:
                for y in range(2):
                    quad(it * 2 + (18 + y))
                    for z in range(3):
                        gates_out(it * 6 + (3 * y + z), (y + z) % 2)
            gates_out(NBLK - 1, 0)
            quad(30)
            quad(31, last=True)

            def split_quad(m, par, first=False):
                if not first:
                    act.wait_ge(acc_done, (m - 1) * KT)
                for j in range(4):
                    act.wait_ge(v_loaded[j], (m + 1) * 16)
                    act.activation(vsp[:, par, j, 0, :], ring[:, j, :], ACT.Copy).then_inc(vhi_ready, 1)
                    act.wait_ge(gated, m * 4 + (j + 1))
                    act.activation(W[:, par, j, 0, :], sq[:, j % 2, :], ACT.Copy).then_inc(whi_ready, 1)

            split_quad(0, 0, first=True)
            for j in range(4):
                act.wait_ge(hid_stored[j], 16 * (NE // 4))
            split_quad(1, 1, first=True)
            with act.Fori(1, NE // 8) as pair:
                split_quad(pair * 2, 0)
                split_quad(pair * 2 + 1, 1)
            act.wait_ge(acc_added, NE // 4 * KT)
            norm(3)

        @block.vector
        def _(dve):
            linked = [0]

            def link(ins):
                linked[0] += 1
                ins.then_inc(chain, 1)
                dve.wait_ge(chain, linked[0])

            def norm(m):
                src, n = norm_src[m]
                off = 4 if m == 1 else 0
                dst = mix if m == 1 else xn
                link(dve.memset(stat[:, 2 * m, 0:TILES], 1.0))
                dve.wait_ge(sq_used, norm_base[m] + n)
                s = 1.0 / (n * P)
                dve.tensor_scalar(stat[:, 2 * m, 0:4], bank[4][:, 0:4], s, EPS, ALU.mult, ALU.add)
                dve.tensor_scalar(stat[0:rows(4), 2 * m, 4:5], bank[4][0:rows(4), 4:5], s, EPS, ALU.mult, ALU.add
                                  ).then_inc(var_ready, 1)
                dve.wait_ge(root_ready, m + 1)
                dve.reciprocal(stat[:, 2 * m + 1, 0:TILES], stat[:, 2 * m, 0:TILES]).then_inc(rstd_ready, 1)
                dve.wait_ge(bc_done, m + 1)
                w = pp(norm_par[m])
                for k in range(n):
                    dve.scalar_tensor_tensor(dst[:, off + k, 0:512], src[:, off + k, 0:512], w[:, k:k + 1], bank[6][:, :],
                                             ALU.mult, ALU.mult)
                    dve.scalar_tensor_tensor(dst[:, off + k, 512:T], src[:, off + k, 512:T], w[:, k:k + 1],
                                             bank[7][:, 0:T - 512], ALU.mult, ALU.mult).then_inc(normed, 1)

            dve.wait_ge(x_loaded, 16 * KT)
            dve.wait_ge(const_loaded, 32)
            dve.memset(S[:, 0, :, :], 0.0).then_inc(s_zero, 1)
            dve.memset(gk[:, TILES - 1, :], 0.0)
            link(dve.memset(dt[:, 0, :], 0.0))
            norm(0)
            dve.wait_ge(a_exp, 1)
            link(dve.tensor_scalar(na[:, :], na[:, :], -1.0, None, ALU.mult))
            dve.wait_ge(dtl_done, 1)
            dve.tensor_copy(dt[:, 0, 0:4 * SH], bank[5][:, 0:4 * SH])
            dve.tensor_copy(dt[0:rows(4), 0, 4 * SH:5 * SH], bank[5][0:rows(4), 4 * SH:5 * SH]).then_inc(dtl_copied, 1)
            dve.wait_ge(dt_step, 1)
            dve.tensor_scalar(dt[:, 2, :], dt[:, 1, :], 1.0, None, ALU.add).then_inc(dt_step, 1)
            dve.wait_ge(dt_step, 3)
            link(dve.scalar_tensor_tensor(dt[:, 1, :], dt[:, 2, :], -1.0, dt[:, 1, :], ALU.add, ALU.subtract))
            link(dve.tensor_tensor(dt[:, 3, :], dt[:, 3, :], dt[:, 1, :], ALU.subtract))
            link(dve.scalar_tensor_tensor(dt[:, 0, :], dt[:, 0, :], 0.0, dt[:, 3, :], ALU.max, ALU.add))
            dve.tensor_tensor(dta[:, :, :], dt[:, 0, :].rearrange("p (i h) -> p i h", h=SH), bc(na[:, :], 1, TILES),
                              ALU.mult).then_inc(dt_ready, 1)
            for i in range(TILES):
                dve.wait_ge(gk_done, i + 1)
                dve.tensor_copy(gk[0:rows(i), i, :], bank[6 + i % 2][0:rows(i), 0:GH * DK]).then_inc(gk_copied, 1)
            dve.wait_ge(gk_step, 1)
            dve.tensor_scalar(tmp[:, 1, :, :], tmp[:, 0, :, :], 1.0, None, ALU.add).then_inc(gk_step, 1)
            dve.wait_ge(gk_step, 2)
            dve.scalar_tensor_tensor(tmp[:, 0, :, :], tmp[:, 1, :, :], -1.0, tmp[:, 0, :, :], ALU.add, ALU.subtract
                                     ).then_inc(gk_step, 1)
            dve.wait_ge(gk_step, 4)
            link(dve.tensor_tensor(tmp[:, 1, :, :], tmp[:, 0, :, :], tmp[:, 1, :, :], ALU.subtract))
            link(dve.scalar_tensor_tensor(tmp[:, 1, :, :], gk[:, :, :], 0.0, tmp[:, 1, :, :], ALU.min, ALU.add))
            dve.tensor_scalar(gk[:, :, :], tmp[:, 1, :, :], 1.0 / 16.0, None, ALU.mult).then_inc(gk_ready, 1)
            dve.wait_ge(proj_act, 4)
            dve.wait_ge(eb_ready, 1)
            dve.tensor_tensor(qb[:, :, :], qT[:, :, :], eb[:, :, :], ALU.mult).then_inc(qb_ready, 1)

            def mult_k(u):
                i, p = u // 2, u % 2
                e = E[:, u % 2, 0:rows(i) * C].rearrange("p (t c s) -> p t c s", t=C, s=C)
                dve.wait_ge(e_q, u + 1)
                dve.tensor_tensor(e, e, bc(kT[:, p, cols(i)].rearrange("p (c s) -> p c s", s=C), 1, C), ALU.mult
                                  ).then_inc(e_k, 1)

            for u in range(2 * TILES):
                i, p = u // 2, u % 2
                e = E[:, u % 2, 0:rows(i) * C].rearrange("p (t c s) -> p t c s", t=C, s=C)
                target = bc(bT[:, p, cols(i)].rearrange("p (c t) -> p t c", t=C), 3, C)
                source = bc(bT[:, p, cols(i)].rearrange("p (c s) -> p c s", s=C), 1, C)
                if u >= 2:
                    dve.wait_ge(attn_used, u - 1)
                if u == 0:
                    dve.wait_ge(v_copied, TILES)
                link(dve.tensor_tensor(e, target, source, ALU.subtract))
                ef = E[:, u % 2, 0:rows(i) * C]
                dve.tensor_scalar(ef, ef, 0.0, None, ALU.min).then_inc(e_arg, 1)
                if u == 0:
                    dve.wait_ge(ktok_done, 1)
                    dve.wait_ge(suf_exp, 3)
                    for q in range(2):
                        dve.tensor_tensor(khat[:, 2 * q:2 * q + 2, :], khat[:, 2 * q:2 * q + 2, :],
                                          bank[4 + q][:, :].rearrange("p (a b) -> p a b", a=2), ALU.mult)
                    dve.tensor_tensor(khat[0:rows(4), 4, :], khat[0:rows(4), 4, :], bank[6][0:rows(4), 0:256], ALU.mult
                                      ).then_inc(khat_ready, 1)
                if u >= 1:
                    mult_k(u - 1)
                if u >= 3 and u % 2 == 1:
                    attn_matrix(dve, u // 2 - 1)
            mult_k(2 * TILES - 1)
            attn_matrix(dve, TILES - 1)
            n = 0
            for i in range(TILES):
                for c in range(P // C if i < 4 else SEGS):
                    a, b = (c * C, c * C + C) if i < 4 else seg_cols(c)
                    last = P * i + b - 1
                    sample = i == 4 and c > 0
                    dve.wait_ge(local_done, n + 1)
                    if sample:
                        dve.wait_ge(inter_done, n + 1)
                    elif n >= 1:
                        dve.wait_ge(inter_done, n)
                        dve.wait_ge(s_updated, n)
                    for p in range(NP):
                        src = Ssm[:, c - 1, p, :] if sample else S[:, n % 2, p, :]
                        dst = Ssm[:, c - 1, p, :] if sample else S[:, (n + 1) % 2, p, :]
                        ins = dve.scalar_tensor_tensor(dst, src, eb[:, p, last:last + 1], bank[4 + n % 2][:, p * P:p * P + DV],
                                                       ALU.mult, ALU.add)
                    ins.then_inc(s_updated, 1)
                    n += 1
            link(dve.memset(gstat[:, 0, :], 1.0))
            dve.wait_ge(gsum_done, 1)
            dve.tensor_scalar(gstat[:, 0, 0:4 * GH], bank[4][:, 0:4 * GH], 1.0 / DV, EPS, ALU.mult, ALU.add)
            dve.tensor_scalar(gstat[0:rows(4), 0, 4 * GH:], bank[4][0:rows(4), 4 * GH:5 * GH], 1.0 / DV, EPS, ALU.mult,
                              ALU.add).then_inc(gvar_ready, 1)
            dve.wait_ge(groot_ready, 1)
            dve.reciprocal(gstat[:, 1, :], gstat[:, 0, :]).then_inc(grstd_ready, 1)
            dve.wait_ge(gbc_done, 1)
            for hh in range(GH):
                dve.scalar_tensor_tensor(mix[:, hh, 0:512], mix[:, hh, 0:512], pp("gla_w"), bank[hh][:, :], ALU.mult,
                                         ALU.mult).then_inc(g_normed, 1)
                dve.scalar_tensor_tensor(mix[:, hh, 512:T], mix[:, hh, 512:T], pp("gla_w"), bank[5][:, hh * P:hh * P + rows(4)],
                                         ALU.mult, ALU.mult).then_inc(g_normed, 1)
                dve.wait_ge(g_normed, 2 * hh + 2)
                dve.tensor_tensor(mix[:, hh, :], mix[:, hh, :], sg[:, hh, :], ALU.mult).then_inc(g_mixed, 1)
            dve.wait_ge(stored, 32)
            dve.memset(xp[:, :, 0:CONV - 1], 0.0).then_inc(xp_zero, 1)
            dve.memset(H[:, 0, :], 0.0).then_inc(s_zero, 1)
            dve.wait_ge(hist_loaded, 16 * CT)
            w, cb = pp("conv_w"), pp("conv_b")
            for f in range(CT):
                dve.wait_ge(proj_act, 12 + f + 1)
                sample = xp[:, f, XPW:XP].rearrange("p (b t) -> p b t", b=NSEQ)
                dst_s = xc[:, f, NPROMPT:T].rearrange("p (b t) -> p b t", b=NSEQ)
                dve.tensor_scalar(xc[:, f, 0:NPROMPT], xp[:, f, 0:NPROMPT], w[:, 4 * f:4 * f + 1], cb[:, f:f + 1],
                                  ALU.mult, ALU.add)
                ins = dve.tensor_scalar(dst_s, sample[:, :, 0:SLEN], w[:, 4 * f:4 * f + 1], cb[:, f:f + 1], ALU.mult, ALU.add)
                for t in range(1, CONV):
                    link(ins)
                    wt = w[:, 4 * f + t:4 * f + t + 1]
                    dve.scalar_tensor_tensor(xc[:, f, 0:NPROMPT], xp[:, f, t:t + NPROMPT], wt, xc[:, f, 0:NPROMPT],
                                             ALU.mult, ALU.add)
                    ins = dve.scalar_tensor_tensor(dst_s, sample[:, :, t:t + SLEN], wt, dst_s, ALU.mult, ALU.add)
                ins.then_inc(conv_done, 1)
            for i in range(TILES):
                r = rows(i)
                neg = cc("neg_a" if i < 4 else "neg_b", r)[:, 0:r]
                dve.wait_ge(pre_done, i + 1)
                if i >= 1:
                    dve.wait_ge(y_done, i)
                    dve.wait_ge(l_exp, i)
                dve.tensor_scalar(cum[0:r, 0, :], bank[3][0:r, 0:SH], -1.0, None, ALU.mult).then_inc(ncum_ready, 1)
                for g in range(2):
                    ins = dve.tensor_tensor(L[0:r, 4 * g:4 * g + 4, 0:r],
                                            bank[g][0:r, :].rearrange("p (h t) -> p h t", h=4)[:, :, 0:r], bc(neg, 1, 4), ALU.add)
                ins.then_inc(z_ready, 1)
                dti = dt[0:r, 0, SH * i:SH * i + SH]
                dve.tensor_tensor(Xd[0:r, :].rearrange("p (h q) -> p h q", h=SH), xtok3(i), bc(dti, 2, HD), ALU.mult)
                dve.wait_ge(wx_ready, i + 1)
                link(dve.tensor_tensor(cum[0:r, 2, :], cum[0:r, 1, :], dti, ALU.mult))
                if i >= 1:
                    dve.wait_ge(hloc_done, i)
                dve.tensor_tensor(XW[0:r, :].rearrange("p (h q) -> p h q", h=SH), xtok3(i), bc(cum[0:r, 2, :], 2, HD),
                                  ALU.mult).then_inc(xw_ready, 1)
                dve.wait_ge(l_exp, i + 1)
                for g in range(SG):
                    ins = dve.tensor_tensor(L[0:r, 4 * g:4 * g + 4, 0:r], L[0:r, 4 * g:4 * g + 4, 0:r],
                                            bc(bank[2][0:r, g * P:g * P + r], 1, 4), ALU.mult)
                ins.then_inc(m_ready, 1)
                if i == 4:
                    dve.wait_ge(xw_ready, i + 1)
                    for c in range(2):
                        dve.tensor_scalar(XWm[0:r, c % 2, :], XW[0:r, :], cc("col_b", r)[:, c:c + 1], None, ALU.mult
                                          ).then_inc(xwm_ready, 1)
                dve.wait_ge(y_done, i + 1)
                ds = pp("dskip")
                for j in range(4):
                    ins = dve.scalar_tensor_tensor(mix[:, 4 + j, cols(i)], xc[:, j, cols(i)], ds[:, j:j + 1],
                                                   bank[4][:, j * P:j * P + r], ALU.mult, ALU.add)
                ins.then_inc(y_copied, 1)
                for c in range(1 if i < 4 else SEGS):
                    last = r - 1 if i < 4 else seg_cols(c)[1] - 1
                    dve.wait_ge(hloc_done, i + c + 1)
                    src, dst = (H[:, i % 2, :], H[:, (i + 1) % 2, :]) if c == 0 else (Hsm[:, c - 1, :],) * 2
                    if c == 0 and i >= 1:
                        dve.wait_ge(h_updated, i)
                    dec = bc(ecb[:, :, last], 2, HD)
                    link(dve.tensor_tensor(dst.rearrange("p (h q) -> p h q", h=SH), src.rearrange("p (h q) -> p h q", h=SH),
                                           dec, ALU.mult))
                    dve.tensor_tensor(dst, dst, bank[5][:, :], ALU.add).then_inc(h_updated, 1)
                    if i == 4 and c + 2 < SEGS:
                        dve.tensor_scalar(XWm[0:r, c % 2, :], XW[0:r, :], cc("col_b", r)[:, c + 2:c + 3], None, ALU.mult
                                          ).then_inc(xwm_ready, 1)
            dve.wait_ge(y_copied, TILES)
            for j in range(4):
                dve.tensor_tensor(mix[:, 4 + j, :], mix[:, 4 + j, :], sz[:, j, :], ALU.mult).then_inc(yz_ready, 1)
            dve.wait_ge(yz_ready, 4)
            norm(1)
            for k in range(KT):
                n = N_FEAT + k
                dve.wait_ge(proj_done, n + 1)
                for x in range(2):
                    ins = dve.tensor_tensor(h[:, k, x * HALF:(x + 1) * HALF], h[:, k, x * HALF:(x + 1) * HALF],
                                            bank[2 * (n % 2) + x][:, 0:HALF], ALU.add)
                ins.then_inc(proj_dve, 1)
            dve.wait_ge(proj_dve, KT)
            norm(2)
            def top16(out, idx, src, r, n, rep_x):
                vals = rep[0:r, rep_x, 0:n]
                link(dve.max(out[:, 0:8], src))
                dve.max_index(idx[:, 0:8], out[:, 0:8], src)
                link(dve.match_replace(vals, out[:, 0:8], src, -3.0e38))
                link(dve.max(out[:, 8:16], vals))
                dve.max_index(idx[:, 8:16], out[:, 8:16], vals)

            for i in range(TILES):
                r = rows(i)
                dve.wait_ge(score_copied, 4 * (i + 1))
                for x in range(2 * PH):
                    half, hh = x // PH, x % PH
                    top16(v16[0:r, half, hh, :], i16[0:r, half, hh, :], s12[0:r, x, :], r, NK, x % 2)
                for hh in range(PH):
                    cnd = cand[0:r, :].rearrange("p (a b) -> p a b", a=TOPK)
                    link(dve.tensor_tensor(cnd, bc(v16[0:r, 0, hh, :], 2, TOPK), bc(v16[0:r, 1, hh, :], 1, TOPK), ALU.add))
                    top16(v16[0:r, 2, hh, :], i16[0:r, 2, hh, :], cand[0:r, :], r, TOPK * TOPK, hh % 2)
                dve.tensor_copy(f16[0:r, 0:2, :, :], i16[0:r, 0:2, :, :]).then_inc(top_sorted, 1)
                dve.wait_ge(top_sorted, i + 1)
                if i >= 1:
                    dve.wait_ge(e_turned, i)
                dve.tensor_tensor(e12[0:r, 2, :, :], v16[0:r, 2, :, :], bc(v16[0:r, 2, :, 0], 2, TOPK), ALU.subtract
                                  ).then_inc(sm_arg, 1)
                dve.tensor_scalar(j16[0:r, 0, :, :], i16[0:r, 2, :, :], 4, None, ALU.logical_shift_right)
                link(dve.tensor_scalar(j16[0:r, 1, :, :], i16[0:r, 2, :, :], TOPK - 1, None, ALU.bitwise_and))
                link(dve.tensor_copy(f16[0:r, 2:4, :, :], j16[0:r, :, :, :]))
                pk = pick[0:r, :, :, :].rearrange("p h k j -> p (h k) j")
                for x in range(2):
                    rank = f16[0:r, 2 + x, :, :].rearrange("p h k -> p (h k)")
                    link(dve.tensor_tensor(pk, bc(rank, 2, TOPK), bc(cc("iota16", r), 1, PH * TOPK), ALU.is_equal))
                    for hh in range(PH):
                        ins = dve.tensor_tensor(pick[0:r, hh, :, :], pick[0:r, hh, :, :], bc(f16[0:r, x, hh, :], 1, TOPK), ALU.mult)
                    link(ins)
                    link(dve.tensor_reduce(e12[0:r, x, :, :].rearrange("p h k -> p (h k)"), pk, AX.X, ALU.add))
                dve.wait_ge(sm_exp, i + 1)
                link(dve.tensor_reduce(den[0:r, 0, :], e12[0:r, 2, :, :], AX.X, ALU.add))
                link(dve.reciprocal(den[0:r, 1, :], den[0:r, 0, :]))
                dve.tensor_tensor(e12[0:r, 2, :, :], e12[0:r, 2, :, :], bc(den[0:r, 1, :], 2, TOPK), ALU.mult
                                  ).then_inc(e_ready, 1)
            dve.wait_ge(e_copied, TILES)
            link(dve.tensor_copy(gTh[:, :], gT[:, :]))
            link(dve.tensor_tensor(gTl[:, :], gT[:, :], gTh[:, :].bitcast(F32), ALU.subtract))

            def one_hots(b, x, first=False):
                if not first:
                    dve.wait_ge(gate_done, (b - 1) * (TB // 4))
                for t in range(TB):
                    at = b * TB + t
                    e1, e2, g, g_lo = (a[:, bass.ds(at, 1)] for a in (e1T, e2T, gT, gTl))
                    dve.tensor_scalar(oneB[:, x, t, :], cc("iota"), e2, None, ALU.is_equal)
                    dve.tensor_scalar(oneA[:, x, t, 0, :], cc("iota"), e1, g, ALU.is_equal, ALU.mult)
                    ins = dve.tensor_scalar(oneA[:, x, t, 1, :], cc("iota"), e1, g_lo, ALU.is_equal, ALU.mult)
                ins.then_inc(one_hot_ready, 1)

            one_hots(0, 0, first=True)
            one_hots(1, 1, first=True)
            with dve.Fori(1, NBLK // 2) as pair:
                b = pair * 2
                one_hots(b, 0)
                one_hots(b + 1, 1)
            one_hots(NBLK - 1, 0)

            def gate(n, y, j, par, g_round, hid_round, first=False):
                if j == 0:
                    dve.wait_ge(g_loaded[par], (g_round + 1) * 16)
                dve.wait_ge(hid_loaded[4 * y + j], (hid_round + 1) * 16)
                if not (first and j < 2):
                    dve.wait_ge(wlo_ready, n - 1)
                dve.tensor_tensor(sq[:, j % 2, :], xn[:, 4 * y + j, :], G[:, par, :, 4 * y + j], ALU.mult
                                  ).then_inc(gated, 1)

            def add_out(m, k):
                dve.wait_ge(acc_done, m * KT + (k + 1))
                for y in range(2):
                    ins = dve.tensor_tensor(h[:, k, y * HALF:(y + 1) * HALF], h[:, k, y * HALF:(y + 1) * HALF],
                                            bank[2 * (k % 4) + y][:, 0:HALF], ALU.add)
                ins.then_inc(acc_added, 1)

            def two_groups(q, first=False):
                for mm in range(4):
                    m = q * 4 + mm
                    for j in range(4):
                        gate(m * 4 + j, mm % 2, j, mm // 2, q, q * 2 + mm // 2, first=(first and mm == 0))
                        if not (first and mm == 0):
                            add_out(m - 1, j)
                    if not (first and mm == 0):
                        for k in range(4, KT):
                            add_out(m - 1, k)

            two_groups(0, first=True)
            with dve.Fori(1, NGRP // 2) as q:
                two_groups(q)
            for k in range(KT):
                add_out(NE // 4 - 1, k)
            dve.wait_ge(acc_added, NE // 4 * KT)
            norm(3)

        @block.gpsimd
        def _(pool):
            pool.wait_ge(proj_act, 4)
            for u in range(2 * TILES):
                i, p = u // 2, u % 2
                e = E[:, u % 2, 0:rows(i) * C].rearrange("p (t c s) -> p t c s", t=C, s=C)
                pool.wait_ge(e_exp, u + 1)
                pool.tensor_tensor(e, e, bc(qT[:, p, cols(i)].rearrange("p (c t) -> p t c", t=C), 3, C), ALU.mult
                                   ).then_inc(e_q, 1)
            pool.wait_ge(khat_ready, 1)
            for i in range(TILES):
                r, nch = rows(i), (P // C if i < 4 else SEGS)
                if i >= 2:
                    pool.wait_ge(local_done, (P // C) * (i - 1))
                pool.tensor_tensor(khm[i % 2][0:r, 0:nch, :], bc(khat[0:r, i, :], 1, nch),
                                   bc(cc("col_a" if i < 4 else "col_b", r), 2, GH * DK), ALU.mult).then_inc(khm_ready, 1)
            for i in range(TILES):
                r = rows(i)
                pool.wait_ge(ecb_ready, i + 1)
                if i >= 1:
                    pool.wait_ge(y_done, i)
                pool.wait_ge(xc_ready, CT)
                for g in range(SG):
                    ins = pool.tensor_tensor(Ct[:, 4 * g:4 * g + 4, 0:r], ecb[:, 4 * g:4 * g + 4, 0:r],
                                             bc(xc[:, 6 + g, cols(i)], 1, 4), ALU.mult)
                ins.then_inc(ct_ready, 1)
            for k in range(KT):
                pool.wait_ge(xh_ready, k + 1)
                pool.tensor_tensor(xl[:, k, :], xn[:, k, :], xh[:, k, :].bitcast(F32), ALU.subtract).then_inc(xl_ready, 1)
            with pool.Fori(0, NE // 4) as q:
                for j in range(4):
                    pool.wait_ge(uhi_ready, q * 4 + (j + 1))
                    pool.tensor_tensor(usp[:, j % 2, 1, :], ring[:, j, :], usp[:, j % 2, 0, :].bitcast(F32), ALU.subtract
                                       ).then_inc(ulo_ready, 1)
            with pool.Fori(0, NE // 8) as pair:
                for par in range(2):
                    for j in range(4):
                        n = pair * 8 + (4 * par + j)
                        pool.wait_ge(vhi_ready, n + 1)
                        pool.tensor_tensor(vsp[:, par, j, 1, :], ring[:, j, :], vsp[:, par, j, 0, :].bitcast(F32),
                                           ALU.subtract).then_inc(vlo_ready, 1)
                        pool.wait_ge(whi_ready, n + 1)
                        pool.tensor_tensor(W[:, par, j, 1, :], sq[:, j % 2, :], W[:, par, j, 0, :].bitcast(F32),
                                           ALU.subtract).then_inc(wlo_ready, 1)


def feature_tiles(w):
    n = w.shape[1] // P
    return w.reshape(KT, P, n, P).transpose(2, 1, 0, 3).reshape(n, P, D)


def kernel(x_prompt, x_sample, state_gla, state_ssm, state_conv, meta_tokens, norm1_w, w_in, w_gk2, b_gk2, gla_norm_w,
           conv_w, conv_b, dt_bias, a_log, d_skip, ssd_norm_w, w_out, norm2_w, peer_wq, peer_k1, peer_k2, peer_u, peer_v,
           final_norm_w):
    import concourse.bacc as bacc
    from concourse.bass_utils import run_bass_kernel_spmd

    x = np.concatenate([np.asarray(meta_tokens), np.asarray(x_prompt)[0], np.asarray(x_sample).reshape(NSEQ * SLEN, D)])
    w = np.asarray(w_in)[0]
    at = np.cumsum([0, GH * DK, GH * DK, GH * DV, GH * DV, RANK, SH * HD, CONVD, SH])
    q, k, v, g, f, z, xbc, dtw = (w[:, at[i]:at[i + 1]] for i in range(8))
    per_feature = lambda a: np.asarray(a).reshape(-1, P).T
    params = {
        "norm1": per_feature(norm1_w), "norm2": per_feature(norm2_w), "final": per_feature(final_norm_w),
        "gla_w": per_feature(gla_norm_w), "ssd_w": per_feature(ssd_norm_w),
        "conv_w": np.asarray(conv_w)[0].reshape(CONV, CT, P).transpose(2, 1, 0).reshape(P, CT * CONV),
        "conv_b": per_feature(conv_b), "dskip": per_feature(np.repeat(np.asarray(d_skip)[0], HD)),
        "a_log": np.tile(np.asarray(a_log), (P, 1)),
    }
    ins = {
        "xT": x.reshape(T, KT, P).transpose(2, 1, 0),
        "const": constants(),
        "param": np.concatenate([params[n] for n, _ in PARAM_PARTS], axis=1),
        "rows": np.concatenate([np.asarray(b_gk2), np.asarray(dt_bias)], axis=1),
        "wsmall": np.concatenate([f, dtw], axis=1).reshape(KT, P, RANK + SH).transpose(1, 0, 2),
        "w_gk2": np.asarray(w_gk2)[0],
        "wv": v.reshape(KT, P, GH * DV).transpose(1, 0, 2),
        "wproj": np.concatenate([feature_tiles(np.concatenate([q, k, g, z, xbc], axis=1)),
                                 feature_tiles(np.asarray(w_out)[0]), feature_tiles(np.asarray(peer_wq)[0])]),
        "keys": np.concatenate([np.asarray(peer_k1)[0].T, np.asarray(peer_k2)[0].T]),
        "s_gla": np.asarray(state_gla)[0].reshape(NSEQ, NP, 2, DK, DV).transpose(2, 3, 0, 1, 4).reshape(P, NSEQ, NP, DV),
        "s_ssm": np.asarray(state_ssm)[0].transpose(3, 0, 1, 2).reshape(DS, NSEQ, SH * HD),
        "s_conv": np.asarray(state_conv)[0].reshape(NSEQ, CONV - 1, CT, P).transpose(3, 2, 0, 1),
        "u": np.asarray(peer_u)[0].reshape(NK, NK, KT, P).transpose(1, 3, 2, 0).reshape(NK, P, D),
        "v": np.asarray(peer_v)[0].reshape(NK, NGRP, GRP, D),
    }
    outs = {
        "yT": (P, KT, T), "gla_p": (P, NP, DV), "gla_s": (P, NSEQ, NP, DV), "ssm_p": (P, SH * HD),
        "ssm_s": (P, NSEQ, SH * HD), "conv_p": (P, CT, CONV - 1), "conv_s": (P, CT, NSEQ, CONV - 1),
    }
    nc = bacc.Bacc("TRN2", target_bir_lowering=False, num_devices=1)
    arrays, di, do = {}, {}, {}
    for name, a in ins.items():
        arrays[f"in_{name}"] = np.ascontiguousarray(a)
        di[name] = nc.dram_tensor(f"in_{name}", a.shape, F32, kind="ExternalInput").ap()
    for name, shape in outs.items():
        do[name] = nc.dram_tensor(f"out_{name}", shape, F32, kind="ExternalOutput").ap()
    build(nc, di, do)
    r = run_bass_kernel_spmd(nc, [arrays], core_ids=[0]).results[0]
    r = {name: np.asarray(r[f"out_{name}"]) for name in outs}
    y = r["yT"].transpose(2, 1, 0).reshape(T, D)
    heads = lambda a: a.reshape(2, DK, -1, NP, DV).transpose(2, 3, 0, 1, 4).reshape(1, -1, GH, DK, DV)
    ssm = lambda a: a.reshape(DS, -1, SH, HD).transpose(1, 2, 3, 0)[None]
    conv = lambda a: a.reshape(P, CT, -1, CONV - 1).transpose(2, 3, 1, 0).reshape(1, -1, CONV - 1, CONVD)
    return (y[META:NPROMPT][None], y[NPROMPT:].reshape(NSEQ, SLEN, D),
            heads(r["gla_p"]), ssm(r["ssm_p"]), conv(r["conv_p"]),
            heads(r["gla_s"]), ssm(r["ssm_s"]), conv(r["conv_s"]))
```

```python
from contextlib import ExitStack

import numpy as np
import concourse.bass as bass
from concourse import mybir

F32 = mybir.dt.float32
F32R = mybir.dt.float32r
BF16 = mybir.dt.bfloat16
U32 = mybir.dt.uint32
ALU = mybir.AluOpType
ACT = mybir.ActivationFunctionType
AX = mybir.AxisListType

P = 128
D = 1024
KT = D // P
META, SEQ = 16, 512
NPROMPT = META + SEQ
NSEQ, SLEN = 8, 8
T = NPROMPT + NSEQ * SLEN
HALF = T // 2
TILES = 5
EPS = 1e-6
GH, DK, DV = 4, 64, 128
NP = GH // 2
RANK = 16
DT_ROW = 32
C = 16
SH, HD, DS, SG = 8, 64, 128, 2
CONV, CONVD = 4, 1024
CT = CONVD // P
PH, NK, QD, TOPK = 8, 128, 128, 16
N_FEAT = 20
N_PROJ = N_FEAT + KT + PH
GRP = 8
NGRP = NK // GRP
TB = 16
TP = T - META
PHALF = TP // 2
NBLK = TP // TB
NE = NK
ROUTE_QUADS = 3
SEGS = 1 + NSEQ
CHUNKS = (TILES - 1) * (P // C) + SEGS
PROMPT_CHUNKS = NPROMPT // C


def rows(i):
    return P if i < TILES - 1 else T - P * (TILES - 1)


def cols(i):
    return slice(P * i, P * i + rows(i))


def peer_rows(i):
    return min(P, TP - P * i)


def peer_cols(i):
    return slice(P * i, P * i + peer_rows(i))


def seg_cols(r):
    return (0, META) if r == 0 else (META + SLEN * (r - 1), META + SLEN * r)


CONST_PARTS = [("ident", P), ("ones", P), ("incl_a", P), ("incl_b", P), ("suf_a", P), ("suf_b", P),
               ("tincl_a", P), ("tsuf_a", P), ("neg_a", P), ("neg_b", P), ("col_a", P // C), ("col_b", SEGS),
               ("head2", 2), ("iota", NK), ("iota16", TOPK), ("eps", 1)]


def offsets(parts):
    out, at = {}, 0
    for name, n in parts:
        out[name] = (at, at + n)
        at += n
    return out, at


CONST_AT, CONST_N = offsets(CONST_PARTS)
PARAM_PARTS = [("norm1", KT), ("norm2", KT), ("final", KT), ("gla_w", 1), ("ssd_w", 4), ("conv_w", CT * CONV),
               ("conv_b", CT), ("dskip", 4), ("a_log", SH), ("dt_bias", SH)]
PARAM_AT, PARAM_N = offsets(PARAM_PARTS)


def constants():
    r = np.arange(P)
    seg_b = np.where(r < META, 0, 1 + (r - META) // SLEN)
    chunk_a = r // C
    le, gt = r[:, None] <= r[None, :], r[:, None] > r[None, :]
    same_a, same_b = chunk_a[:, None] == chunk_a[None, :], seg_b[:, None] == seg_b[None, :]
    parts = {
        "ident": np.eye(P), "ones": np.ones((P, P)),
        "incl_a": le & same_a, "incl_b": le & same_b, "suf_a": gt & same_a, "suf_b": gt & same_b,
        "tincl_a": le, "tsuf_a": gt,
        "neg_a": np.where(le, 0.0, -1e30), "neg_b": np.where(le & same_b, 0.0, -1e30),
        "col_a": chunk_a[:, None] == np.arange(P // C)[None, :],
        "col_b": seg_b[:, None] == np.arange(SEGS)[None, :],
        "head2": (r // DK)[:, None] == np.arange(2)[None, :],
        "iota": np.tile(np.arange(NK), (P, 1)), "iota16": np.tile(np.arange(TOPK), (P, 1)),
        "eps": np.full((P, 1), EPS),
    }
    return np.concatenate([np.asarray(parts[n], np.float32) for n, _ in CONST_PARTS], axis=1)


def bc(ap, axis, n):
    ap = ap.unsqueeze(axis)
    shape = list(ap.shape)
    shape[axis] = n
    return ap.broadcast_to(shape)


def build(nc, d, o):
    base = ExitStack()
    with base:
        def sem(name):
            return base.enter_context(nc.semaphore(name))

        def sb(stack, name, shape, dt=F32):
            return stack.enter_context(nc.sbuf_tensor(name, shape, dt))

        gates_dram = nc.dram_tensor("gates_scratch", (NGRP, P, TP, GRP), F32, kind="Internal").ap()
        hid_dram = nc.dram_tensor("hidden_scratch", (NE, P, TP), F32, kind="Internal").ap()

        h = sb(base, "h", [P, KT, T])
        xc = h
        xn = sb(base, "xn", [P, KT, T])
        ring = sb(base, "ring", [P, 4, D])
        cst = sb(base, "cst", [P, CONST_N])
        prm = sb(base, "prm", [P, PARAM_N])
        sq = sb(base, "sq", [P, 2, T])
        gstat = sb(base, "gstat", [P, 2, TILES * GH])

        def cc(name, r=P):
            a, b = CONST_AT[name]
            return cst[0:r, a:b]

        def pp(name):
            a, b = PARAM_AT[name]
            return prm[:, a:b]

        ident, ones = cc("ident"), cc("ones")
        bank = [base.enter_context(nc.psum_tensor(f"bank{n}", [P, 512], F32)) for n in range(8)]

        mix_stack = ExitStack()
        mix = sb(mix_stack, "mix", [P, 8, T])
        sg = sb(mix_stack, "sg", [P, 4, T])
        sz = sb(mix_stack, "sz", [P, 4, T])
        row = sb(mix_stack, "row", [1, GH * DK])
        small = sb(mix_stack, "small", [P, KT, DT_ROW + SH])
        wgk = sb(mix_stack, "wgk", [RANK, GH * DK])
        fl = sb(mix_stack, "fl", [DT_ROW + SH, T])
        dt = sb(mix_stack, "dt", [P, 4, TILES * SH])
        dta = sb(mix_stack, "dta", [P, TILES, SH])
        na = sb(mix_stack, "na", [P, SH])

        hist = sb(mix_stack, "hist", [P, CT, NSEQ, CONV - 1])
        tails = sb(mix_stack, "tails", [P, CT, 1 + NSEQ, CONV - 1])

        gla = ExitStack()
        E = sb(gla, "E", [P, 2, C * P])
        khm0 = sb(gla, "khm0", [P, SEGS * GH * DK])
        qT = sb(gla, "qT", [P, NP, T])
        kT = sb(gla, "kT", [P, NP, T])
        bT = sb(gla, "bT", [P, NP, T])
        eb = sb(gla, "eb", [P, NP, T])
        qz = sb(gla, "qz", [P, NP, 2, T])
        V = sb(gla, "V", [P, TILES, GH * DV])
        khat = sb(gla, "khat", [P, TILES, GH * DK])
        tmp = sb(gla, "tmp", [P, 2, TILES, GH * DK])
        MT = sb(gla, "MT", [P, TILES, GH * P])
        S = sb(gla, "S", [P, 2, NP, DV])
        Ssm = sb(gla, "Ssm", [P, NSEQ, NP, DV])
        gla.close()
        gk = qz[:, :, :, :].rearrange("p a b t -> p (a b t)")[:, 0:TILES * GH * DK].rearrange(
            "p (i n) -> p i n", i=TILES)
        tmpf = tmp[:, :, :, :].rearrange("p a b c -> p (a b c)")
        khm = [khm0[:, :].rearrange("p (c n) -> p c n", c=SEGS),
               tmpf[:, 0:SEGS * GH * DK].rearrange("p (c n) -> p c n", c=SEGS)]
        E_unit = [E[:, 0, :], E[:, 1, :], khm0[:, 0:C * P]]
        Ef = E[:, :, :].rearrange("p a b -> p (a b)")
        wv_sb = Ef[:, 0:KT * GH * DV].rearrange("p (k n) -> p k n", k=KT)
        gsq = Ef[:, 0:GH * T].rearrange("p (h t) -> p h t", h=GH)

        ssd = ExitStack()
        sb(ssd, "E_place", [P, 2, C * P])
        xtok = sb(ssd, "xtok", [P, TILES, SH * HD])
        btok = sb(ssd, "btok", [P, TILES, SG * DS])
        ecb = sb(ssd, "ecb", [P, 2, SH, P])
        L = sb(ssd, "L", [P, 2, SH, P])
        Ct = sb(ssd, "Ct", [P, 2, SH, P])
        Xd = sb(ssd, "Xd", [P, 2, SH * HD])
        XW = sb(ssd, "XW", [P, 2, SH * HD])
        XWm = sb(ssd, "XWm", [P, 2, SH * HD])
        cum = sb(ssd, "cum", [P, 2, 3, SH])
        H = sb(ssd, "H", [P, 2, SH * HD])
        Hsm = sb(ssd, "Hsm", [P, NSEQ, SH * HD])
        ssd.close()
        mix_stack.close()

        rt = ExitStack()
        xh = sb(rt, "xh", [P, KT, TP], F32R)
        xl = sb(rt, "xl", [P, KT, TP], F32R)
        usp = sb(rt, "usp", [P, 2, 2, D], F32R)
        gl = sb(rt, "gl", [P, 4, TP])
        e1T = sb(rt, "e1T", [P, TP])
        e2T = sb(rt, "e2T", [P, TP])
        gT = sb(rt, "gT", [P, TP])
        gparts = sb(rt, "gparts", [P, 3, TP], BF16)
        rt1 = ExitStack()
        hotA = sb(rt1, "hotA", [P, 2, TB, NK], BF16)
        oneA = sb(rt1, "oneA", [P, 2, 3, TB, NK], BF16)
        oneB = sb(rt1, "oneB", [P, 2, TB, NK], BF16)
        stage = sb(rt1, "stage", [P, 2, NGRP, TB, GRP])
        rt1.close()
        rt2 = ExitStack()
        qh = sb(rt2, "qh", [P, PH, TP])
        keys = sb(rt2, "keys", [P, NK])
        s12 = sb(rt2, "s12", [P, 2 * PH, NK])
        rep = sb(rt2, "rep", [P, 2, 2 * NK])
        v16 = sb(rt2, "v16", [P, 3, PH, TOPK])
        i16 = sb(rt2, "i16", [P, 3, PH, TOPK], U32)
        j16 = sb(rt2, "j16", [P, 2, PH, TOPK], U32)
        f16 = sb(rt2, "f16", [P, 4, PH, TOPK])
        cand = sb(rt2, "cand", [P, TOPK * TOPK])
        pick = sb(rt2, "pick", [P, PH, TOPK, TOPK])
        e12 = sb(rt2, "e12", [P, 3, PH, TOPK])
        den = sb(rt2, "den", [P, 2, PH])
        rt2.close()
        rt.close()

        ex = ExitStack()
        W1 = sb(ex, "W1", [P, 4, 2, TP], F32R)
        vsp1 = sb(ex, "vsp1", [P, 4, 2, D], F32R)
        G1 = sb(ex, "G1", [P, TP, GRP])
        G0 = sb(ex, "G0", [P, TP, GRP])
        vsp0 = sb(ex, "vsp0", [P, 4, 2, D], F32R)
        W0 = sb(ex, "W0", [P, 4, 2, TP], F32R)
        W, vsp, G = [W0, W1], [vsp0, vsp1], [G0, G1]
        ex.close()

        x_loaded = [sem(f"x_loaded{k}") for k in range(KT)]
        const_loaded, small_loaded, wv_loaded, sgla_loaded = map(
            sem, ["const_loaded", "small_loaded", "wv_loaded", "sgla_loaded"])
        hist_loaded, hsm_loaded, keys_loaded = map(sem, ["hist_loaded", "hsm_loaded", "keys_loaded"])
        w_loaded = [sem(f"w_loaded{s}") for s in range(4)]
        u_loaded = [sem(f"u_loaded{s}") for s in range(4)]
        v_loaded = [sem(f"v_loaded{s}") for s in range(4)]
        hid_loaded = [sem(f"hid_loaded{s}") for s in range(8)]
        hid_stored = [sem(f"hid_stored{s}") for s in range(4)]
        g_loaded = [sem(f"g_loaded{s}") for s in range(2)]
        stored = sem("stored")
        MIXERS_STORED = 16 * (2 + 1 + CT + 2)
        proj_done, proj_act, proj_dve = map(sem, ["proj_done", "proj_act", "proj_dve"])
        sq_ready, sq_used, root_ready, normed = map(sem, ["sq_ready", "sq_used", "root_ready", "normed"])
        fl_done, fl_copied, dtl_done, dtl_copied, dt_step, dt_ready, a_exp = map(
            sem, ["fl_done", "fl_copied", "dtl_done", "dtl_copied", "dt_step", "dt_ready", "a_exp"])
        gk_done, gk_copied, gk_step, gk_ready, v_done, v_copied = map(
            sem, ["gk_done", "gk_copied", "gk_step", "gk_ready", "v_done", "v_copied"])
        b_done, b_copied, eb_ready, suf_done, suf_exp, ktok_done, khat_ready, qb_ready = map(
            sem, ["b_done", "b_copied", "eb_ready", "suf_done", "suf_exp", "ktok_done", "khat_ready", "qb_ready"])
        e_arg, e_exp, e_q, e_k, attn_used, mt_ready, khm_ready = map(
            sem, ["e_arg", "e_exp", "e_q", "e_k", "attn_used", "mt_ready", "khm_ready"])
        s_zero, local_done, s_updated, inter_done, o_copied = map(
            sem, ["s_zero", "local_done", "s_updated", "inter_done", "o_copied"])
        gsq_ready, gsum_done, gvar_ready, groot_ready, grstd_ready, gbc_done, g_normed, g_mixed = map(
            sem, ["gsq_ready", "gsum_done", "gvar_ready", "groot_ready", "grstd_ready", "gbc_done", "g_normed", "g_mixed"])
        x_reloaded, conv_link, conv_done, xc_ready, tr_done, tr_copied = map(
            sem, ["x_reloaded", "conv_link", "conv_done", "xc_ready", "tr_done", "tr_copied"])
        pre_done, ecb_ready, wx_ready, ncum_ready, z_ready, l_exp, m_ready, ct_ready, xw_ready = map(
            sem, ["pre_done", "ecb_ready", "wx_ready", "ncum_ready", "z_ready", "l_exp", "m_ready", "ct_ready", "xw_ready"])
        y_done, y_copied, hloc_done, h_updated, xwm_ready, yz_ready = map(
            sem, ["y_done", "y_copied", "hloc_done", "h_updated", "xwm_ready", "yz_ready"])
        score_done, score_copied, top_sorted, sm_arg, sm_exp, e_ready, e_turned, e_copied = map(
            sem, ["score_done", "score_copied", "top_sorted", "sm_arg", "sm_exp", "e_ready", "e_turned", "e_copied"])
        third_ready = sem("third_ready")
        one_hot_step, one_hot_ready, gate_done, gate_copied = map(
            sem, ["one_hot_step", "one_hot_ready", "gate_done", "gate_copied"])
        gate_stored = [sem(f"gate_stored{x}") for x in range(2)]
        qhi_ready, qlo_ready = sem("qhi_ready"), sem("qlo_ready")
        xh_ready, xl_ready, uhi_ready, ulo_ready, hid_done, gelu_ready = map(
            sem, ["xh_ready", "xl_ready", "uhi_ready", "ulo_ready", "hid_done", "gelu_ready"])
        vhi_ready, vlo_ready, gated, whi_ready, wlo_ready, acc_done, acc_added = map(
            sem, ["vhi_ready", "vlo_ready", "gated", "whi_ready", "wlo_ready", "acc_done", "acc_added"])
        chain, achain = sem("chain"), sem("achain")

        def proj_dst_is_dve(n):
            return N_FEAT <= n < N_FEAT + KT

        def wait_gates_stored(eng):
            eng.wait_ge(gate_stored[0], 16 * (NBLK - NBLK // 2))
            eng.wait_ge(gate_stored[1], 16 * (NBLK // 2))

        def xtok3(i):
            return xtok[0:rows(i), i, :].rearrange("p (h q) -> p h q", h=SH)

        def attn_matrix(dve, i):
            r, nch = rows(i), rows(i) // C
            dve.wait_ge(attn_used, 2 * i + 2)
            dve.tensor_tensor(MT[0:r, i, :].rearrange("p (h c t) -> p h c t", h=GH, t=C)[:, :, 0:nch, :],
                              bc(bank[4 + i % 2][0:r, 0:GH * C].rearrange("p (h t) -> p h t", h=GH), 2, nch),
                              bc(cc("incl_a" if i < 4 else "incl_b", r)[:, 0:r].rearrange("p (c t) -> p c t", t=C), 1, GH),
                              ALU.mult).then_inc(mt_ready, 1)

        def wait_proj_evacuated(eng, n):
            m = n - 2
            if m < 0:
                return
            if proj_dst_is_dve(m):
                eng.wait_ge(proj_dve, m - N_FEAT + 1)
            else:
                eng.wait_ge(proj_act, m + 1 - (KT if m >= N_FEAT + KT else 0))

        ssd_banks, CUM_AT = [(0, 1, 2), (3, 6, 7)], SG * P

        def state_bank(i, c):
            return 5 if i < 4 else 6 + c % 2

        norm_src = [(h, KT), (mix, 4), (h, KT), (h, KT)]
        norm_base = [0, KT, KT + 4, 2 * KT + 4]
        norm_par = ["norm1", "ssd_w", "norm2", "final"]

        block = base.enter_context(nc.Block())

        @block.sync
        def _(sp):
            for k in range(KT):
                sp.dma_start(h[:, k, :], d["xT"][:, k, :]).then_inc(x_loaded[k], 16)
            sp.dma_start(cst[:, :], d["const"]).then_inc(const_loaded, 16)
            sp.dma_start(prm[:, :], d["param"]).then_inc(const_loaded, 16)
            sp.dma_start(row[:, :], d["rows"]).then_inc(small_loaded, 16)
            sp.dma_start(small[:, :, :], d["wsmall"]).then_inc(small_loaded, 16)
            sp.dma_start(wgk[:, :], d["w_gk2"]).then_inc(small_loaded, 16)
            sp.dma_start(wv_sb, d["wv"]).then_inc(wv_loaded, 16)

            def load_w(n):
                if n >= 4:
                    sp.wait_ge(proj_done, n - 3)
                sp.dma_start(ring[:, n % 4, :], d["wproj"][n]).then_inc(w_loaded[n % 4], 16)

            sp.dma_start(hist[:, :, :, :].rearrange("p f b t -> p (f b t)"), d["s_conv"].rearrange("p f b t -> p (f b t)")
                         ).then_inc(hist_loaded, 16)
            for n in range(12):
                load_w(n)
            sp.dma_start(Ssm[:, :, :, :], d["s_gla"]).then_inc(sgla_loaded, 16)
            for n in range(12, N_FEAT + 4):
                load_w(n)
            sp.wait_ge(s_updated, PROMPT_CHUNKS)
            sp.dma_start(o["gla_p"], S[:, PROMPT_CHUNKS % 2, :, :]).then_inc(stored, 16)
            sp.wait_ge(s_updated, CHUNKS)
            sp.dma_start(Hsm[:, :, :], d["s_ssm"]).then_inc(hsm_loaded, 16)
            sp.dma_start(o["gla_s"], Ssm[:, :, :, :]).then_inc(stored, 16)
            sp.wait_ge(xc_ready, CT)
            sp.dma_start(o["conv_p"], tails[:, :, 0, :]).then_inc(stored, 16)
            for f in range(CT):
                sp.dma_start(o["conv_s"][:, f, :, :], tails[:, f, 1:1 + NSEQ, :]).then_inc(stored, 16)
            sp.wait_ge(y_copied, TILES)
            for k in range(KT):
                sp.dma_start(h[:, k, :], d["xT"][:, k, :]).then_inc(x_reloaded, 16)
            for n in range(N_FEAT + 4, N_FEAT + KT + 4):
                load_w(n)
            sp.wait_ge(h_updated, TILES)
            sp.dma_start(o["ssm_p"], H[:, TILES % 2, :]).then_inc(stored, 16)
            sp.wait_ge(h_updated, TILES + NSEQ)
            sp.dma_start(o["ssm_s"], Hsm[:, :, :]).then_inc(stored, 16)
            sp.wait_ge(stored, MIXERS_STORED)
            sp.wait_ge(proj_done, N_FEAT + KT)
            sp.dma_start(keys[:, :], d["keys"]).then_inc(keys_loaded, 16)
            for n in range(N_FEAT + KT + 4, N_PROJ):
                load_w(n)
            def load_u(n, j):
                sp.dma_start(ring[:, j, :], d["u"][bass.ds(n, 1), :, :].rearrange("a p n -> p (a n)")
                             ).then_inc(u_loaded[j], 16)

            def quad(q, b=None, x=0):
                for j in range(4):
                    n = q * 4 + j
                    sp.wait_ge(ulo_ready, n + 1)
                    load_u(n + 4, j)
                    sp.wait_ge(gelu_ready, n + 1)
                    sp.dma_start(hid_dram[bass.ds(n, 1), :, :].rearrange("a p t -> p (a t)"), gl[:, j, :]
                                 ).then_inc(hid_stored[j], 16)
                    if b is not None and j < 3:
                        store_gates(b + j, (x + j) % 2)

            def store_gates(b, x):
                sp.wait_ge(gate_copied, (b + 1) * (TB // 4))
                sp.dma_start(gates_dram[:, :, bass.ds(b * TB, TB), :].rearrange("g p t j -> p g (t j)"),
                             stage[:, x, :, :, :].rearrange("p g t j -> p g (t j)")).then_inc(gate_stored[x], 16)

            for j in range(4):
                sp.wait_ge(proj_done, N_PROJ - 3 + j)
                load_u(j, j)
            with sp.Fori(0, 18) as q:
                quad(q)
            with sp.Fori(0, 6) as it:
                for y in range(2):
                    quad(it * 2 + (18 + y), it * 6 + 3 * y, y)
            wait_gates_stored(sp)
            sp.wait_ge(xl_ready, KT)

            def load_gates(g, par):
                sp.dma_start(G[par][:, :, :], gates_dram[bass.ds(g, 1), :, :, :].rearrange("a p t j -> p (a t) j")
                             ).then_inc(g_loaded[par], 16)

            def load_hid(n, slot):
                sp.dma_start(xn[:, slot, 0:TP], hid_dram[bass.ds(n, 1), :, :].rearrange("a p t -> p (a t)")
                             ).then_inc(hid_loaded[slot], 16)

            def load_v(g, y, j):
                sp.dma_start(ring[:, j, :], d["v"][:, bass.ds(g, 1), 4 * y + j, :].rearrange("p a n -> p (a n)")
                             ).then_inc(v_loaded[j], 16)

            load_gates(0, 0)
            for n in range(GRP):
                if n % 4 == 0:
                    for j in range(4):
                        sp.wait_ge(hid_stored[j], 16 * (n // 4 + 1))
                load_hid(n, n)
            quad(30)
            for j in range(4):
                sp.wait_ge(ulo_ready, NE - 3 + j)
                load_v(0, 0, j)
                sp.wait_ge(gelu_ready, NE - 3 + j)
                sp.dma_start(hid_dram[NE - 4 + j, :, :], gl[:, j, :]).then_inc(hid_stored[j], 16)
            for j in range(4):
                sp.wait_ge(hid_stored[j], 16 * (NE // 4))
            load_gates(1, 1)
            for j in range(4):
                sp.wait_ge(vlo_ready, j + 1)
                load_v(0, 1, j)

            def load_group(g, par, first=False):
                if not first:
                    sp.wait_ge(gated, (g - 1) * GRP)
                    load_gates(g, par)
                for y in range(2):
                    for j in range(4):
                        n = g * GRP + (4 * y + j)
                        sp.wait_ge(gated, n - 7)
                        load_hid(n, 4 * y + j)
                        sp.wait_ge(vlo_ready, n - 3)
                        load_v(g, y, j)

            load_group(1, 1, first=True)
            with sp.Fori(1, NGRP // 2) as pair:
                g = pair * 2
                load_group(g, 0)
                load_group(g + 1, 1)
            for k in range(KT):
                sp.wait_ge(normed, norm_base[3] + k + 1)
                sp.dma_start(o["yT"][:, k, :], xn[:, k, :]).then_inc(stored, 16)
            sp.wait_ge(stored, MIXERS_STORED + 16 * KT)

        @block.tensor
        def _(pe):
            def norm_sum(m, k):
                pe.wait_ge(sq_ready, norm_base[m] + k + 1)
                for y in range(2):
                    mm = pe.matmul(bank[4 + y][:, 0:HALF], ones, sq[:, k % 2, y * HALF:(y + 1) * HALF],
                                   start=(k == 0), stop=(k == norm_src[m][1] - 1))
                mm.then_inc(sq_used, 1)

            def project(n, src, first=0, count=2 * KT, norm=None, at=0, half=HALF):
                if first == 0:
                    pe.wait_ge(w_loaded[n % 4], 16 * (n // 4 + 1))
                    wait_proj_evacuated(pe, n)
                for m in range(first, first + count):
                    x, k = m // KT, m % KT
                    if norm is not None and x == 0:
                        pe.wait_ge(normed, norm_base[norm] + k + 1)
                    mm = pe.matmul(bank[2 * (n % 2) + x][:, 0:half], ring[:, n % 4, k * P:(k + 1) * P],
                                   src[:, k, at + x * half:at + (x + 1) * half], start=(k == 0), stop=(k == KT - 1))
                if first + count == 2 * KT:
                    mm.then_inc(proj_done, 1)

            pe.wait_ge(const_loaded, 32)
            for k in range(KT):
                norm_sum(0, k)
            pe.wait_ge(small_loaded, 48)
            for x in range(2):
                for k in range(KT):
                    if x == 0:
                        pe.wait_ge(normed, norm_base[0] + k + 1)
                    mm = pe.matmul(bank[x][0:DT_ROW + SH, 0:HALF], small[:, k, :], xn[:, k, x * HALF:(x + 1) * HALF],
                                   start=(k == 0), stop=(k == KT - 1))
            mm.then_inc(fl_done, 1)
            pe.wait_ge(fl_copied, 2)
            for i in range(TILES):
                mm = pe.matmul(bank[5][0:rows(i), SH * i:SH * i + SH], fl[DT_ROW:DT_ROW + SH, cols(i)],
                               ident[DT_ROW:DT_ROW + SH, DT_ROW:DT_ROW + SH], start=True, stop=True)
            mm.then_inc(dtl_done, 1)
            for i in range(TILES):
                out = bank[6 + i % 2][0:rows(i), 0:GH * DK]
                if i >= 2:
                    pe.wait_ge(gk_copied, i - 1)
                pe.matmul(out, fl[0:RANK, cols(i)], wgk[:, :], start=True, stop=False)
                pe.matmul(out, ones[0:1, 0:rows(i)], row[0:1, :], start=False, stop=True).then_inc(gk_done, 1)
            pe.wait_ge(wv_loaded, 16)
            for i in range(TILES):
                if i >= 2:
                    pe.wait_ge(v_copied, i - 1)
                for k in range(KT):
                    mm = pe.matmul(bank[2 + i % 2][0:rows(i), :], xn[:, k, cols(i)], wv_sb[:, k, :],
                                   start=(k == 0), stop=(k == KT - 1))
                mm.then_inc(v_done, 1)
            pe.wait_ge(gk_ready, 1)
            pe.wait_ge(dtl_copied, 1)
            for p in range(NP):
                for i in range(TILES):
                    out = bank[4 + p][:, cols(i)] if i < 4 else bank[6][:, p * P:p * P + rows(i)]
                    mm = pe.matmul(out, gk[0:rows(i), i, p * P:(p + 1) * P],
                                   cc("incl_a" if i < 4 else "incl_b", rows(i))[:, 0:rows(i)], start=True, stop=True)
            mm.then_inc(b_done, 1)
            for i in range(TILES):
                out = [bank[7][:, 0:256], bank[7][:, 256:512], bank[0][:, 0:256], bank[0][:, 256:512],
                       bank[1][0:rows(4), 0:256]][i]
                mm = pe.matmul(out, cc("suf_a" if i < 4 else "suf_b", rows(i))[:, 0:rows(i)], gk[0:rows(i), i, :],
                               start=True, stop=True)
            mm.then_inc(suf_done, 1)
            pe.wait_ge(v_copied, TILES)
            pe.wait_ge(suf_exp, 3)
            for n in range(4):
                project(n, xn)
            pe.wait_ge(b_copied, 4)
            pe.wait_ge(proj_act, 4)
            for i in range(TILES):
                for p in range(NP):
                    mm = pe.transpose(bank[4 + i // 2][0:rows(i), (i % 2) * 256 + p * P:(i % 2) * 256 + (p + 1) * P],
                                      kT[:, p, cols(i)], ident)
            mm.then_inc(ktok_done, 1)
            def attn(u, n=None):
                i, p = u // 2, u % 2
                if p == 0 and i >= 2:
                    pe.wait_ge(mt_ready, i - 1)
                pe.wait_ge(e_k, u + 1)
                src = E_unit[u % 3][:, 0:rows(i) * C].rearrange("p (t n) -> p t n", t=C)
                for t in range(C):
                    if n is not None:
                        project(n, xn, first=t, count=1)
                    out = bank[4 + i % 2][0:rows(i), p * 2 * C + t:p * 2 * C + C + t + 1:C]
                    mm = pe.matmul(out, src[:, t, :], cc("head2"), start=True, stop=True)
                mm.then_inc(attn_used, 1)

            project(4, xn)
            project(5, xn)
            for u in range(2 * TILES):
                attn(u, 6 + u if u < 9 else None)
            pe.wait_ge(khat_ready, 1)
            n = 0
            for i in range(TILES):
                r = rows(i)
                ob = bank[6 + i % 2][:, :].rearrange("p (h t) -> p h t", h=GH)
                pe.wait_ge(mt_ready, max(i + 1, 4))
                pe.wait_ge(khm_ready, i + 1)
                if i >= 2:
                    pe.wait_ge(o_copied, i - 1)
                for hh in range(GH):
                    pe.matmul(ob[:, hh, 0:r], V[0:r, i, hh * DV:(hh + 1) * DV], MT[0:r, i, hh * P:hh * P + r],
                              start=(hh == 0), stop=True, skip_group_check=True)
                for c in range(P // C if i < 4 else SEGS):
                    a, b = (c * C, c * C + C) if i < 4 else seg_cols(c)
                    if n == 1:
                        pe.wait_ge(mt_ready, TILES)
                    if n >= 2:
                        pe.wait_ge(s_updated, n - 1)
                    for hh in range(GH):
                        q = (hh % 2) * DK
                        mm = pe.matmul(bank[5 - n % 2][q:q + DK, (hh // 2) * P:(hh // 2) * P + DV],
                                       khm[i % 2][0:r, c, hh * DK:(hh + 1) * DK], V[0:r, i, hh * DV:(hh + 1) * DV],
                                       start=True, stop=True)
                    mm.then_inc(local_done, 1)
                    if n < 8 * TILES:
                        project(15 + n // 8, xn, first=n % 8 * 2, count=2)
                    sample = i == 4 and c > 0
                    if sample:
                        pe.wait_ge(sgla_loaded, 16)
                    elif n == 0:
                        pe.wait_ge(s_zero, 1)
                        pe.wait_ge(qb_ready, 1)
                    else:
                        pe.wait_ge(s_updated, n)
                    for p in range(NP):
                        src = Ssm[:, c - 1, p, :] if sample else S[:, n % 2, p, :]
                        mm = pe.matmul(ob[:, 2 * p:2 * p + 2, a:b], src, qz[:, p, :, P * i + a:P * i + b],
                                       start=False, stop=True, skip_group_check=True)
                    mm.then_inc(inter_done, 1)
                    n += 1
            pe.wait_ge(gsq_ready, 1)
            pe.wait_ge(s_updated, CHUNKS)
            for i in range(TILES):
                for hh in range(GH):
                    mm = pe.matmul(bank[4][0:rows(i), i * GH + hh:i * GH + hh + 1], gsq[:, hh, cols(i)], ones[:, 0:1],
                                   start=True, stop=True)
            mm.then_inc(gsum_done, 1)
            pe.wait_ge(grstd_ready, 1)
            pe.wait_ge(proj_act, N_FEAT)
            for hh in range(GH):
                for i in range(TILES):
                    out = bank[hh][:, cols(i)] if i < 4 else bank[5][:, hh * P:hh * P + rows(i)]
                    mm = pe.matmul(out, gstat[0:rows(i), 1, i * GH + hh:i * GH + hh + 1].broadcast_to([rows(i), P]),
                                   ident[0:rows(i), 0:rows(i)], start=True, stop=True)
            mm.then_inc(gbc_done, 1)
            pe.wait_ge(o_copied, TILES)
            pe.wait_ge(xc_ready, 6)
            for i in range(TILES):
                if i >= 1:
                    pe.wait_ge(tr_copied, 2 * i)
                for f in range(6):
                    out = bank[6][0:rows(i), f * P:(f + 1) * P] if f < 4 else bank[7][0:rows(i), (f - 4) * P:(f - 3) * P]
                    mm = pe.transpose(out, xc[:, f, cols(i)], ident)
                mm.then_inc(tr_done, 1)
            pe.wait_ge(g_normed, 8)
            pe.wait_ge(xc_ready, CT)
            pe.wait_ge(dt_ready, 1)
            pe.wait_ge(tr_copied, 2 * TILES)

            def pre(i):
                r = rows(i)
                incl = cc("tincl_a" if i < 4 else "incl_b", r)[:, 0:r]
                suf = cc("tsuf_a" if i < 4 else "suf_b", r)[:, 0:r]
                b = ssd_banks[i % 2]
                if i >= 2:
                    pe.wait_ge(ecb_ready, i - 1)
                    pe.wait_ge(wx_ready, i - 1)
                    pe.wait_ge(m_ready, i - 1)
                for hh in range(SH):
                    pe.matmul(bank[b[hh // 4]][:, (hh % 4) * P:(hh % 4) * P + r],
                              dta[0:r, i, hh:hh + 1].broadcast_to([r, P]), incl, start=True, stop=True)
                for g in range(SG):
                    pe.matmul(bank[b[2]][0:r, g * P:g * P + r], xc[:, 4 + g, cols(i)], xc[:, 6 + g, cols(i)],
                              start=True, stop=True)
                pe.matmul(bank[b[2]][0:r, CUM_AT:CUM_AT + SH], incl, dta[0:r, i, :], start=True, stop=True)
                pe.matmul(bank[b[2]][0:r, CUM_AT + SH:CUM_AT + 2 * SH], suf, dta[0:r, i, :], start=True, stop=True
                          ).then_inc(pre_done, 1)

            def to_state(i, c):
                r = rows(i)
                if i == 4:
                    pe.wait_ge(xwm_ready, c + 1)
                    if c >= 2:
                        pe.wait_ge(h_updated, i + c - 1)
                src = XW[0:r, i % 2, :] if i < 4 else XWm[0:r, c % 2, :]
                for g in range(SG):
                    mm = pe.matmul(bank[state_bank(i, c)][:, g * 256:(g + 1) * 256], btok[0:r, i, g * DS:(g + 1) * DS],
                                   src[:, g * 256:(g + 1) * 256], start=True, stop=True)
                mm.then_inc(hloc_done, 1)

            pre(0)
            for i in range(TILES):
                r = rows(i)
                if i < 4:
                    pre(i + 1)
                pe.wait_ge(m_ready, i + 1)
                pe.wait_ge(ct_ready, i + 1)
                pe.wait_ge(xw_ready, i + 1)
                if i >= 1:
                    pe.wait_ge(y_copied, i)
                    pe.wait_ge(h_updated, i)
                else:
                    pe.wait_ge(s_zero, 2)
                if i == 4:
                    pe.wait_ge(hsm_loaded, 16)
                for hh in range(SH):
                    q = (hh % 2) * HD
                    out = bank[4][q:q + HD, (hh // 2) * P:(hh // 2) * P + r]
                    pe.matmul(out, Xd[0:r, i % 2, hh * HD:(hh + 1) * HD], L[0:r, i % 2, hh, 0:r], start=True, stop=(i == 4))
                    if i < 4:
                        mm = pe.matmul(out, H[:, i % 2, hh * HD:(hh + 1) * HD], Ct[:, i % 2, hh, :], start=False, stop=True)
                    else:
                        for c in range(SEGS):
                            a, b = seg_cols(c)
                            src = H[:, i % 2, hh * HD:(hh + 1) * HD] if c == 0 else Hsm[:, c - 1, hh * HD:(hh + 1) * HD]
                            mm = pe.matmul(out[:, a:b], src, Ct[:, i % 2, hh, a:b], start=False, stop=True,
                                           skip_group_check=True)
                mm.then_inc(y_done, 1)
                if i < 4:
                    to_state(i, 0)

            def project_out(n, ssd_part):
                if not ssd_part:
                    pe.wait_ge(w_loaded[n % 4], 16 * (n // 4 + 1))
                    wait_proj_evacuated(pe, n)
                for x in range(2):
                    for k in range(4 * ssd_part, 4 * ssd_part + 4):
                        mm = pe.matmul(bank[2 * (n % 2) + x][:, 0:HALF], ring[:, n % 4, k * P:(k + 1) * P],
                                       mix[:, k, x * HALF:(x + 1) * HALF], start=(k == 0), stop=(k == KT - 1))
                if ssd_part:
                    mm.then_inc(proj_done, 1)

            pe.wait_ge(g_mixed, GH)
            project_out(N_FEAT, 0)
            pe.wait_ge(y_copied, TILES)
            for k in range(4):
                norm_sum(1, k)
            project_out(N_FEAT + 1, 0)
            pe.wait_ge(normed, norm_base[1] + 4)
            for k in range(KT):
                if k >= 2:
                    norm_sum(2, k - 2)
                if k >= 2:
                    project_out(N_FEAT + k, 0)
                project_out(N_FEAT + k, 1)
                if k == 0:
                    to_state(4, 0)
                to_state(4, k + 1)
            norm_sum(2, KT - 2)
            norm_sum(2, KT - 1)
            def split_product(b, x):
                for k in range(KT):
                    hi, lo = (usp[:, x, z, k * P:(k + 1) * P] for z in range(2))
                    for w, src in ((hi, xh), (hi, xl), (lo, xh)):
                        for y in range(2):
                            mm = pe.matmul(bank[b + y][:, 0:PHALF], w, src[:, k, y * PHALF:(y + 1) * PHALF],
                                           start=(k == 0 and w is hi and src is xh), stop=(k == KT - 1 and w is lo))
                return mm

            project(N_FEAT + KT, xn, norm=2, at=META, half=PHALF)
            pe.wait_ge(xl_ready, KT)
            for n in range(N_FEAT + KT + 1, N_PROJ):
                pe.wait_ge(qlo_ready, n - N_FEAT - KT)
                wait_proj_evacuated(pe, n)
                split_product(2 * (n % 2), n % 2).then_inc(proj_done, 1)
            pe.wait_ge(proj_act, N_PROJ - KT)
            pe.wait_ge(keys_loaded, 16)

            def turn_picks(i):
                pe.wait_ge(e_ready, i + 1)
                if i >= 1:
                    pe.wait_ge(e_copied, i)
                for x in range(3):
                    mm = pe.transpose(bank[4][:, x * P:x * P + peer_rows(i)], e12[0:peer_rows(i), x, :, :].rearrange("p h k -> p (h k)"),
                                      ident[0:peer_rows(i), 0:peer_rows(i)])
                mm.then_inc(e_turned, 1)

            def scores(i):
                if i >= 1:
                    pe.wait_ge(score_copied, 4 * i)
                    if i >= 2:
                        pe.wait_ge(e_copied, i - 1)
                for half in range(2):
                    for hh in range(PH):
                        q = half * 64
                        mm = pe.matmul(bank[4 + 2 * half + hh // 4][0:peer_rows(i), (hh % 4) * NK:(hh % 4 + 1) * NK],
                                       qh[q:q + 64, hh, peer_cols(i)], keys[q:q + 64, :], start=True, stop=True)
                mm.then_inc(score_done, 1)

            def quad(q, first=False, b=None, x=0):
                par = x
                for j in range(4):
                    n = q * 4 + j
                    x = j % 2
                    pe.wait_ge(ulo_ready, n + 1)
                    if not (first and j < 2):
                        pe.wait_ge(gelu_ready, n - 1)
                    mm = split_product(2 * x, x)
                    mm.then_inc(hid_done, 1)
                    if b is not None and j < 3:
                        gate_block(b + j, (par + j) % 2, first=(isinstance(b, int) and b + j == 0))

            def gate_block(b, x, first=False):
                pe.wait_ge(one_hot_ready, b + 1)
                pe.wait_ge(third_ready, b + 1)
                for q in range(TB // 4):
                    if not first:
                        pe.wait_ge(gate_copied, b * (TB // 4) + q - 3)
                    for t in range(4):
                        for z in range(3):
                            mm = pe.matmul(bank[4 + q][:, t * NK:(t + 1) * NK], oneA[:, x, z, 4 * q + t, :],
                                           oneB[:, x, 4 * q + t, :], start=(z == 0), stop=(z == 2))
                    mm.then_inc(gate_done, 1)

            for i in range(TILES):
                scores(i)
                quad(ROUTE_QUADS * i, first=(i == 0))
                if i >= 1:
                    pe.wait_ge(score_copied, 4 * i + 4)
                    turn_picks(i - 1)
                with pe.Fori(ROUTE_QUADS * i + 1, ROUTE_QUADS * (i + 1)) as q:
                    quad(q)
            quad(15)
            turn_picks(TILES - 1)
            pe.wait_ge(e_copied, TILES)
            quad(16)
            quad(17)
            for y in range(2):
                quad(18 + y, b=3 * y, x=y)
            with pe.Fori(1, 6) as it:
                for y in range(2):
                    quad(it * 2 + (18 + y), b=it * 6 + 3 * y, x=y)
            quad(30)
            quad(31)
            pe.wait_ge(gate_copied, NBLK * (TB // 4))

            last_sums = {5: (0, 1), 6: (2, 3), 7: (4, 5, 6, 7)}

            def second(m, par, first=False, last=False):
                pe.wait_ge(vlo_ready, m * 4 + 4)
                pe.wait_ge(wlo_ready, m * 4 + 4)
                for k in range(KT):
                    if not (first and k < 4):
                        pe.wait_ge(acc_added, m * KT + (k - 3))
                    elif k == 2:
                        pe.wait_ge(gelu_ready, NE)
                    for j in range(4):
                        hi, lo = (vsp[par][:, j, z, k * P:(k + 1) * P] for z in range(2))
                        for w, z in ((hi, 0), (hi, 1), (lo, 0)):
                            for y in range(2):
                                mm = pe.matmul(bank[2 * ((k + 2) % 4) + y][:, 0:PHALF], w, W[par][:, j, z, y * PHALF:(y + 1) * PHALF],
                                               start=(j == 0 and w is hi and z == 0), stop=(j == 3 and w is lo))
                    mm.then_inc(acc_done, 1)
                    if last and k == 5:
                        pe.wait_ge(acc_added, m * KT + 5)
                    if last and k in last_sums:
                        for t in last_sums[k]:
                            norm_sum(3, t)

            second(0, 0, first=True)
            second(1, 1)
            with pe.Fori(1, NE // 8 - 1) as pair:
                second(pair * 2, 0)
                second(pair * 2 + 1, 1)
            second(NE // 4 - 2, 0)
            second(NE // 4 - 1, 1, last=True)

        @block.scalar
        def _(act):
            linked = [0]

            def link(ins):
                linked[0] += 1
                ins.then_inc(achain, 1)
                act.wait_ge(achain, linked[0])

            def norm(m, ready):
                src, n = norm_src[m]
                off = 4 if m == 1 else 0
                for k in range(n):
                    ready(k)
                    if k >= 2:
                        act.wait_ge(sq_used, norm_base[m] + k - 1)
                    act.activation(sq[:, k % 2, :], src[:, off + k, :], ACT.Square).then_inc(sq_ready, 1)
                act.wait_ge(sq_used, norm_base[m] + n)
                for y in range(2):
                    act.activation(sq[:, 0, y * HALF:(y + 1) * HALF], bank[4 + y][:, 0:HALF], ACT.Sqrt,
                                   scale=1.0 / (n * P), bias=cc("eps")).then_inc(root_ready, 1)

            def from_pair(n, dst, func=ACT.Copy, scale=1.0, half=HALF):
                act.wait_ge(proj_done, n + 1)
                for x in range(2):
                    ins = act.activation(dst[:, x * half:(x + 1) * half], bank[2 * (n % 2) + x][:, 0:half], func, scale=scale)
                ins.then_inc(proj_act, 1)

            act.wait_ge(const_loaded, 32)
            norm(0, lambda k: act.wait_ge(x_loaded[k], 16))
            act.activation(na[:, :], pp("a_log"), ACT.Exp).then_inc(a_exp, 1)
            act.wait_ge(fl_done, 1)
            for x in range(2):
                act.activation(fl[:, x * HALF:(x + 1) * HALF], bank[x][0:DT_ROW + SH, 0:HALF], ACT.Copy).then_inc(fl_copied, 1)
            act.wait_ge(dtl_copied, 1)
            link(act.activation(dt[:, 1, :], dt[:, 0, :], ACT.Abs))
            act.activation(dt[:, 1, :], dt[:, 1, :], ACT.Exp, scale=-1.0).then_inc(dt_step, 1)
            act.wait_ge(dt_step, 2)
            act.activation(dt[:, 3, :], dt[:, 2, :], ACT.Ln).then_inc(dt_step, 1)
            act.wait_ge(gk_copied, TILES)
            link(act.activation(tmp[:, 0, :, :], gk[:, :, :], ACT.Abs))
            act.activation(tmp[:, 0, :, :], tmp[:, 0, :, :], ACT.Exp, scale=-1.0).then_inc(gk_step, 1)
            act.wait_ge(gk_step, 3)
            act.activation(tmp[:, 1, :, :], tmp[:, 1, :, :], ACT.Ln).then_inc(gk_step, 1)
            for i in range(TILES):
                act.wait_ge(v_done, i + 1)
                act.activation(V[0:rows(i), i, :], bank[2 + i % 2][0:rows(i), :], ACT.Copy).then_inc(v_copied, 1)
            act.wait_ge(b_done, 1)
            for p in range(NP):
                act.activation(bT[:, p, 0:512], bank[4 + p][:, :], ACT.Copy).then_inc(b_copied, 1)
                act.activation(bT[:, p, 512:T], bank[6][:, p * P:p * P + rows(4)], ACT.Copy).then_inc(b_copied, 1)
            act.wait_ge(b_copied, 4)
            act.activation(eb[:, :, :], bT[:, :, :], ACT.Exp).then_inc(eb_ready, 1)
            act.wait_ge(suf_done, 1)
            act.activation(khat[:, 0:2, :], bank[7][:, :].rearrange("p (a b) -> p a b", a=2), ACT.Exp).then_inc(suf_exp, 1)
            act.activation(khat[:, 2:4, :], bank[0][:, :].rearrange("p (a b) -> p a b", a=2), ACT.Exp).then_inc(suf_exp, 1)
            act.activation(khat[0:rows(4), 4, :], bank[1][0:rows(4), 0:256], ACT.Exp).then_inc(suf_exp, 1)

            def decay(u):
                act.wait_ge(e_arg, u + 1)
                e = E_unit[u % 3][:, 0:rows(u // 2) * C]
                act.activation(e, e, ACT.Exp).then_inc(e_exp, 1)

            for n in range(15):
                if n < 4:
                    from_pair(n, (qT if n < 2 else kT)[:, n % 2, :], scale=(DK ** -0.5 if n < 2 else 1.0))
                elif n < 12:
                    from_pair(n, (sg if n < 8 else sz)[:, n % 4, :], ACT.Silu)
                else:
                    from_pair(n, h[:, n - 12, :])
                if n < 3:
                    decay(n)
                elif 5 <= n < 12:
                    decay(n - 2)

            def conv_out(f):
                act.wait_ge(conv_done, f + 1)
                act.activation(tails[:, f, 0, :], h[:, f, NPROMPT - (CONV - 1):NPROMPT], ACT.Copy)
                seqs = h[:, f, NPROMPT:T].rearrange("p (b t) -> p b t", b=NSEQ)
                link(act.activation(tails[:, f, 1:1 + NSEQ, :], seqs[:, :, SLEN - (CONV - 1):SLEN], ACT.Copy))
                act.activation(xc[:, f, :], sq[:, f % 2, :], ACT.Silu).then_inc(xc_ready, 1)

            n = 0
            before = [(0,), (2,), (4,), (5,), (6,)]
            after = [(1,), (3,), (), ()]
            for i in range(TILES):
                n += P // C if i < 4 else SEGS
                for f in before[i]:
                    conv_out(f)
                from_pair(15 + i, h[:, 3 + i, :])
                act.wait_ge(inter_done, n)
                act.activation(mix[:, 0:GH, cols(i)],
                               bank[6 + i % 2][:, :].rearrange("p (h t) -> p h t", h=GH)[:, :, 0:rows(i)], ACT.Copy
                               ).then_inc(o_copied, 1)
                if i < 4:
                    for f in after[i]:
                        conv_out(f)
            act.wait_ge(o_copied, TILES)
            act.activation(gsq, mix[:, 0:GH, :], ACT.Square).then_inc(gsq_ready, 1)
            act.wait_ge(gvar_ready, 1)
            act.activation(gstat[:, 0, :], gstat[:, 0, :], ACT.Sqrt).then_inc(groot_ready, 1)
            conv_out(7)
            for i in range(TILES):
                act.wait_ge(tr_done, i + 1)
                act.activation(xtok[0:rows(i), i, :], bank[6][0:rows(i), :], ACT.Copy).then_inc(tr_copied, 1)
                act.activation(btok[0:rows(i), i, :], bank[7][0:rows(i), 0:256], ACT.Copy).then_inc(tr_copied, 1)
            for i in range(TILES):
                r = rows(i)
                b = ssd_banks[i % 2]
                act.wait_ge(z_ready, i + 1)
                act.wait_ge(ncum_ready, i + 1)
                if i >= 2:
                    act.wait_ge(ct_ready, i - 1)
                    act.wait_ge(h_updated, i - 1)
                    act.wait_ge(xw_ready, i - 1)
                for g in range(2):
                    ins = act.activation(ecb[:, i % 2, 4 * g:4 * g + 4, 0:r],
                                         bank[b[g]][:, :].rearrange("p (h t) -> p h t", h=4)[:, :, 0:r], ACT.Exp)
                ins.then_inc(ecb_ready, 1)
                act.activation(cum[0:r, i % 2, 1, :], bank[b[2]][0:r, CUM_AT + SH:CUM_AT + 2 * SH], ACT.Exp).then_inc(wx_ready, 1)
                for hh in range(SH):
                    ins = act.activation(L[0:r, i % 2, hh, 0:r], L[0:r, i % 2, hh, 0:r], ACT.Exp,
                                         bias=cum[0:r, i % 2, 0, hh:hh + 1])
                ins.then_inc(l_exp, 1)
            norm(1, lambda k: act.wait_ge(yz_ready, k + 1))
            norm(2, lambda k: act.wait_ge(proj_dve, k + 1))
            for k in range(KT):
                act.wait_ge(normed, norm_base[2] + k + 1)
                act.activation(xh[:, k, :], xn[:, k, META:T], ACT.Copy).then_inc(xh_ready, 1)
            act.wait_ge(stored, MIXERS_STORED)
            for n in range(N_FEAT + KT, N_PROJ):
                if n + 1 < N_PROJ:
                    if n > N_FEAT + KT + 1:
                        act.wait_ge(proj_done, n)
                    act.wait_ge(w_loaded[(n + 1) % 4], 16 * ((n + 1) // 4 + 1))
                    act.activation(usp[:, (n + 1) % 2, 0, :], ring[:, (n + 1) % 4, :], ACT.Copy).then_inc(qhi_ready, 1)
                from_pair(n, qh[:, n - N_FEAT - KT, :], half=PHALF)

            def split_u(n, j, round_):
                act.wait_ge(u_loaded[j % 4], (round_ + j // 4 + 1) * 16)
                act.activation(usp[:, j % 2, 0, :], ring[:, j % 4, :], ACT.Copy).then_inc(uhi_ready, 1)

            def quad(q, first=False, b=None, x=0):
                for j in range(4):
                    n = q * 4 + j
                    act.wait_ge(hid_done, n + 1)
                    split_u(n + 2, j + 2, q)
                    if not first:
                        act.wait_ge(hid_stored[j], q * 16)
                    for y in range(2):
                        ins = act.activation(gl[:, j, y * PHALF:(y + 1) * PHALF], bank[2 * (j % 2) + y][:, 0:PHALF],
                                             ACT.Gelu_apprx_tanh)
                    ins.then_inc(gelu_ready, 1)
                    if b is not None and j < 3:
                        gates_out(b + j, (x + j) % 2, first=(isinstance(b, int) and b + j < 2))

            def copy_picks(i):
                act.wait_ge(e_turned, i + 1)
                for x, dst in enumerate((e1T, e2T, gT)):
                    ins = act.activation(dst[:, peer_cols(i)], bank[4][:, x * P:x * P + peer_rows(i)], ACT.Copy)
                ins.then_inc(e_copied, 1)

            split_u(0, 0, 0)
            split_u(1, 1, 0)
            for i in range(TILES):
                r = peer_rows(i)
                act.wait_ge(score_done, i + 1)
                if i >= 1:
                    act.wait_ge(top_sorted, i)
                for x in range(4):
                    act.activation(s12[0:r, 4 * x:4 * x + 4, :], bank[4 + x][0:r, :].rearrange("p (h k) -> p h k", h=4),
                                   ACT.Copy).then_inc(score_copied, 1)
                quad(ROUTE_QUADS * i, first=(i == 0))
                if i >= 1:
                    copy_picks(i - 1)
                with act.Fori(ROUTE_QUADS * i + 1, ROUTE_QUADS * (i + 1)) as q:
                    quad(q)
                act.wait_ge(sm_arg, i + 1)
                act.activation(e12[0:r, 2, :, :], e12[0:r, 2, :, :], ACT.Exp).then_inc(sm_exp, 1)
            quad(15)
            copy_picks(TILES - 1)

            def gates_out(b, x, first=False):
                if not first:
                    act.wait_ge(gate_stored[x], (b - x) * 8)
                for q in range(TB // 4):
                    act.wait_ge(gate_done, b * (TB // 4) + q + 1)
                    act.activation(stage[:, x, :, 4 * q:4 * q + 4, :].rearrange("p g t j -> p t g j"),
                                   bank[4 + q][:, :].rearrange("p (t g j) -> p t g j", t=4, j=GRP), ACT.Copy
                                   ).then_inc(gate_copied, 1)

            quad(16)
            quad(17)
            for y in range(2):
                quad(18 + y, b=3 * y, x=y)
            with act.Fori(1, 6) as it:
                for y in range(2):
                    quad(it * 2 + (18 + y), b=it * 6 + 3 * y, x=y)
            quad(30)

            def split_v(m, par, j):
                act.wait_ge(v_loaded[j], (m + 1) * 16)
                act.activation(vsp[par][:, j, 0, :], ring[:, j, :], ACT.Copy).then_inc(vhi_ready, 1)
                act.wait_ge(gated, m * 4 + (j + 1))
                act.activation(W[par][:, j, 0, :], sq[:, j % 2, 0:TP], ACT.Copy).then_inc(whi_ready, 1)

            def split_quad(m, par, first=False):
                if not first:
                    act.wait_ge(acc_done, (m - 1) * KT)
                for j in range(4):
                    split_v(m, par, j)

            for j in range(4):
                n = NE - 4 + j
                if j == 3:
                    split_v(0, 0, j)
                act.wait_ge(hid_done, n + 1)
                if j < 2:
                    split_u(n + 2, j + 2, NE // 4 - 1)
                act.wait_ge(hid_stored[j], 16 * (NE // 4 - 1))
                for y in range(2):
                    ins = act.activation(gl[:, j, y * PHALF:(y + 1) * PHALF], bank[2 * (j % 2) + y][:, 0:PHALF],
                                         ACT.Gelu_apprx_tanh)
                ins.then_inc(gelu_ready, 1)
                if j < 3:
                    split_v(0, 0, j)
            for j in range(4):
                act.wait_ge(hid_stored[j], 16 * (NE // 4))
            split_quad(1, 1, first=True)
            with act.Fori(1, NE // 8) as pair:
                split_quad(pair * 2, 0)
                split_quad(pair * 2 + 1, 1)
            norm(3, lambda k: act.wait_ge(acc_added, NE // 4 * KT - KT + k + 1))

        @block.vector
        def _(dve):
            linked = [0]

            def link(ins):
                linked[0] += 1
                ins.then_inc(chain, 1)
                dve.wait_ge(chain, linked[0])

            def norm(m):
                src, n = norm_src[m]
                off = 4 if m == 1 else 0
                dst = mix if m == 1 else xn
                for y in range(2):
                    dve.wait_ge(root_ready, 2 * m + y + 1)
                    rstd = sq[:, 0, y * HALF:(y + 1) * HALF]
                    link(dve.reciprocal(rstd, rstd))
                w = pp(norm_par[m])
                for k in range(n):
                    dve.scalar_tensor_tensor(dst[:, off + k, :], src[:, off + k, :], w[:, k:k + 1], sq[:, 0, :],
                                             ALU.mult, ALU.mult).then_inc(normed, 1)

            dve.wait_ge(const_loaded, 32)
            dve.memset(S[:, 0, :, :], 0.0).then_inc(s_zero, 1)
            dve.memset(gk[:, TILES - 1, :], 0.0)
            link(dve.memset(dt[:, 0, :], 0.0))
            norm(0)
            dve.wait_ge(a_exp, 1)
            link(dve.tensor_scalar(na[:, :], na[:, :], -1.0, None, ALU.mult))
            dve.wait_ge(dtl_done, 1)
            dve.tensor_tensor(dt[:, 0, 0:4 * SH].rearrange("p (i h) -> p i h", h=SH),
                              bank[5][:, 0:4 * SH].rearrange("p (i h) -> p i h", h=SH), bc(pp("dt_bias"), 1, 4), ALU.add)
            dve.tensor_tensor(dt[0:rows(4), 0, 4 * SH:5 * SH], bank[5][0:rows(4), 4 * SH:5 * SH], pp("dt_bias")[0:rows(4), :],
                              ALU.add).then_inc(dtl_copied, 1)
            dve.wait_ge(dt_step, 1)
            dve.tensor_scalar(dt[:, 2, :], dt[:, 1, :], 1.0, None, ALU.add).then_inc(dt_step, 1)
            dve.wait_ge(dt_step, 3)
            link(dve.scalar_tensor_tensor(dt[:, 1, :], dt[:, 2, :], -1.0, dt[:, 1, :], ALU.add, ALU.subtract))
            link(dve.tensor_tensor(dt[:, 3, :], dt[:, 3, :], dt[:, 1, :], ALU.subtract))
            link(dve.scalar_tensor_tensor(dt[:, 0, :], dt[:, 0, :], 0.0, dt[:, 3, :], ALU.max, ALU.add))
            dve.tensor_tensor(dta[:, :, :], dt[:, 0, :].rearrange("p (i h) -> p i h", h=SH), bc(na[:, :], 1, TILES),
                              ALU.mult).then_inc(dt_ready, 1)
            for i in range(TILES):
                dve.wait_ge(gk_done, i + 1)
                dve.tensor_copy(gk[0:rows(i), i, :], bank[6 + i % 2][0:rows(i), 0:GH * DK]).then_inc(gk_copied, 1)
            dve.wait_ge(gk_step, 1)
            dve.tensor_scalar(tmp[:, 1, :, :], tmp[:, 0, :, :], 1.0, None, ALU.add).then_inc(gk_step, 1)
            dve.wait_ge(gk_step, 2)
            dve.scalar_tensor_tensor(tmp[:, 0, :, :], tmp[:, 1, :, :], -1.0, tmp[:, 0, :, :], ALU.add, ALU.subtract
                                     ).then_inc(gk_step, 1)
            dve.wait_ge(gk_step, 4)
            link(dve.tensor_tensor(tmp[:, 1, :, :], tmp[:, 0, :, :], tmp[:, 1, :, :], ALU.subtract))
            link(dve.scalar_tensor_tensor(tmp[:, 1, :, :], gk[:, :, :], 0.0, tmp[:, 1, :, :], ALU.min, ALU.add))
            dve.tensor_scalar(gk[:, :, :], tmp[:, 1, :, :], 1.0 / 16.0, None, ALU.mult).then_inc(gk_ready, 1)
            dve.wait_ge(b_copied, 4)
            dve.wait_ge(v_copied, TILES)

            def decay_arg(u):
                i, p = u // 2, u % 2
                ef = E_unit[u % 3][:, 0:rows(i) * C]
                e = ef.rearrange("p (t c s) -> p t c s", t=C, s=C)
                target = bc(bT[:, p, cols(i)].rearrange("p (c t) -> p t c", t=C), 3, C)
                source = bc(bT[:, p, cols(i)].rearrange("p (c s) -> p c s", s=C), 1, C)
                if u >= 3:
                    dve.wait_ge(attn_used, u - 2)
                link(dve.tensor_tensor(e, target, source, ALU.subtract))
                dve.tensor_scalar(ef, ef, 0.0, None, ALU.min).then_inc(e_arg, 1)

            def mult_k(u):
                i, p = u // 2, u % 2
                e = E_unit[u % 3][:, 0:rows(i) * C].rearrange("p (t c s) -> p t c s", t=C, s=C)
                dve.wait_ge(e_q, u + 1)
                dve.tensor_tensor(e, e, bc(kT[:, p, cols(i)].rearrange("p (c s) -> p c s", s=C), 1, C), ALU.mult
                                  ).then_inc(e_k, 1)

            for u in range(3):
                decay_arg(u)
            dve.wait_ge(suf_done, 1)
            dve.memset(qz[0:DK, :, 1, :], 0.0)
            dve.memset(qz[DK:P, :, 0, :], 0.0)
            dve.wait_ge(proj_act, 2)
            dve.wait_ge(eb_ready, 1)
            dve.tensor_tensor(qz[0:DK, :, 0, :], qT[0:DK, :, :], eb[0:DK, :, :], ALU.mult)
            dve.tensor_tensor(qz[DK:P, :, 1, :], qT[DK:P, :, :], eb[DK:P, :, :], ALU.mult).then_inc(qb_ready, 1)
            dve.wait_ge(proj_act, 4)
            dve.wait_ge(ktok_done, 1)
            dve.wait_ge(suf_exp, 3)
            for q in range(2):
                dve.tensor_tensor(khat[:, 2 * q:2 * q + 2, :], khat[:, 2 * q:2 * q + 2, :],
                                  bank[4 + q][:, :].rearrange("p (a b) -> p a b", a=2), ALU.mult)
            dve.tensor_tensor(khat[0:rows(4), 4, :], khat[0:rows(4), 4, :], bank[6][0:rows(4), 0:256], ALU.mult
                              ).then_inc(khat_ready, 1)
            mult_k(0)
            for u in range(2 * TILES):
                if u + 1 < 2 * TILES:
                    mult_k(u + 1)
                if u + 3 < 2 * TILES:
                    decay_arg(u + 3)
                if u % 2 == 1:
                    attn_matrix(dve, u // 2)
            w, cb = pp("conv_w"), pp("conv_b")

            def conv_step(f, step):
                acc = sq[:, f % 2, :]
                seqs = lambda a: a[:, NPROMPT:T].rearrange("p (b t) -> p b t", b=NSEQ)
                src, acc_s, src_s = h[:, f, :], seqs(acc), seqs(h[:, f, :])
                if step == 0:
                    dve.wait_ge(proj_act, 12 + f + 1)
                    if f >= 2:
                        dve.wait_ge(xc_ready, f - 1)
                    ins = dve.tensor_scalar(acc, src, w[:, CONV * (f + 1) - 1:CONV * (f + 1)], cb[:, f:f + 1], ALU.mult, ALU.add)
                    ins.then_inc(conv_link, 1)
                    return
                t, back = step - 1, CONV - step
                wt = w[:, CONV * f + t:CONV * f + t + 1]
                dve.wait_ge(conv_link, 3 * f + step)
                dve.scalar_tensor_tensor(acc[:, back:NPROMPT], src[:, 0:NPROMPT - back], wt, acc[:, back:NPROMPT],
                                         ALU.mult, ALU.add)
                dve.scalar_tensor_tensor(acc_s[:, :, back:SLEN], src_s[:, :, 0:SLEN - back], wt, acc_s[:, :, back:SLEN],
                                         ALU.mult, ALU.add)
                ins = dve.scalar_tensor_tensor(acc_s[:, :, 0:back], hist[:, f, :, t:CONV - 1], wt, acc_s[:, :, 0:back],
                                               ALU.mult, ALU.add)
                ins.then_inc(conv_done if step == CONV - 1 else conv_link, 1)

            conv_at = [1, 5, 9, 13, 18, 26, 34]
            dve.wait_ge(hist_loaded, 16)
            n = 0
            for i in range(TILES):
                for c in range(P // C if i < 4 else SEGS):
                    a, b = (c * C, c * C + C) if i < 4 else seg_cols(c)
                    last = P * i + b - 1
                    sample = i == 4 and c > 0
                    for f, at in enumerate(conv_at):
                        if at <= n < at + CONV:
                            conv_step(f, n - at)
                    dve.wait_ge(local_done, n + 1)
                    if sample:
                        dve.wait_ge(inter_done, n + 1)
                    elif n >= 1:
                        dve.wait_ge(inter_done, n)
                        dve.wait_ge(s_updated, n)
                    for p in range(NP):
                        src = Ssm[:, c - 1, p, :] if sample else S[:, n % 2, p, :]
                        dst = Ssm[:, c - 1, p, :] if sample else S[:, (n + 1) % 2, p, :]
                        ins = dve.scalar_tensor_tensor(dst, src, eb[:, p, last:last + 1], bank[5 - n % 2][:, p * P:p * P + DV],
                                                       ALU.mult, ALU.add)
                    ins.then_inc(s_updated, 1)
                    n += 1
            for step in range(CONV):
                conv_step(CT - 1, step)
            link(dve.memset(gstat[:, 0, :], 1.0))
            dve.wait_ge(gsum_done, 1)
            dve.tensor_scalar(gstat[:, 0, 0:4 * GH], bank[4][:, 0:4 * GH], 1.0 / DV, EPS, ALU.mult, ALU.add)
            dve.tensor_scalar(gstat[0:rows(4), 0, 4 * GH:], bank[4][0:rows(4), 4 * GH:5 * GH], 1.0 / DV, EPS, ALU.mult,
                              ALU.add).then_inc(gvar_ready, 1)
            dve.wait_ge(groot_ready, 1)
            dve.reciprocal(gstat[:, 1, :], gstat[:, 0, :]).then_inc(grstd_ready, 1)
            dve.wait_ge(gbc_done, 1)
            for hh in range(GH):
                dve.scalar_tensor_tensor(mix[:, hh, 0:512], mix[:, hh, 0:512], pp("gla_w"), bank[hh][:, :], ALU.mult,
                                         ALU.mult).then_inc(g_normed, 1)
                dve.scalar_tensor_tensor(mix[:, hh, 512:T], mix[:, hh, 512:T], pp("gla_w"), bank[5][:, hh * P:hh * P + rows(4)],
                                         ALU.mult, ALU.mult).then_inc(g_normed, 1)
                dve.wait_ge(g_normed, 2 * hh + 2)
                dve.tensor_tensor(mix[:, hh, :], mix[:, hh, :], sg[:, hh, :], ALU.mult).then_inc(g_mixed, 1)
            dve.memset(H[:, 0, :], 0.0).then_inc(s_zero, 1)

            def decays(i):
                r = rows(i)
                neg = cc("neg_a" if i < 4 else "neg_b", r)[:, 0:r]
                b = ssd_banks[i % 2]
                dve.wait_ge(pre_done, i + 1)
                if i >= 2:
                    dve.wait_ge(y_done, i - 1)
                    dve.wait_ge(l_exp, i - 1)
                dve.tensor_scalar(cum[0:r, i % 2, 0, :], bank[b[2]][0:r, CUM_AT:CUM_AT + SH], -1.0, None, ALU.mult
                                  ).then_inc(ncum_ready, 1)
                for g in range(2):
                    ins = dve.tensor_tensor(L[0:r, i % 2, 4 * g:4 * g + 4, 0:r],
                                            bank[b[g]][0:r, :].rearrange("p (h t) -> p h t", h=4)[:, :, 0:r], bc(neg, 1, 4),
                                            ALU.add)
                ins.then_inc(z_ready, 1)

            def weighted_x(i):
                r = rows(i)
                dti = dt[0:r, 0, SH * i:SH * i + SH]
                dve.tensor_tensor(Xd[0:r, i % 2, :].rearrange("p (h q) -> p h q", h=SH), xtok3(i), bc(dti, 2, HD), ALU.mult)
                dve.wait_ge(wx_ready, i + 1)
                link(dve.tensor_tensor(cum[0:r, i % 2, 2, :], cum[0:r, i % 2, 1, :], dti, ALU.mult))
                if i >= 2:
                    dve.wait_ge(hloc_done, i - 1)
                dve.tensor_tensor(XW[0:r, i % 2, :].rearrange("p (h q) -> p h q", h=SH), xtok3(i),
                                  bc(cum[0:r, i % 2, 2, :], 2, HD), ALU.mult).then_inc(xw_ready, 1)

            def mixing(i):
                r = rows(i)
                dve.wait_ge(l_exp, i + 1)
                for g in range(SG):
                    ins = dve.tensor_tensor(L[0:r, i % 2, 4 * g:4 * g + 4, 0:r], L[0:r, i % 2, 4 * g:4 * g + 4, 0:r],
                                            bc(bank[ssd_banks[i % 2][2]][0:r, g * P:g * P + r], 1, 4), ALU.mult)
                ins.then_inc(m_ready, 1)

            def segment_rows(c):
                r = rows(4)
                dve.tensor_scalar(XWm[0:r, c % 2, :], XW[0:r, 0, :], cc("col_b", r)[:, c:c + 1], None, ALU.mult
                                  ).then_inc(xwm_ready, 1)

            def new_state(i, c):
                last = rows(i) - 1 if i < 4 else seg_cols(c)[1] - 1
                dve.wait_ge(hloc_done, i + c + 1)
                src, dst = (H[:, i % 2, :], H[:, (i + 1) % 2, :]) if c == 0 else (Hsm[:, c - 1, :],) * 2
                if c == 0 and i >= 1:
                    dve.wait_ge(h_updated, i)
                dec = bc(ecb[:, i % 2, :, last], 2, HD)
                link(dve.tensor_tensor(dst.rearrange("p (h q) -> p h q", h=SH), src.rearrange("p (h q) -> p h q", h=SH),
                                       dec, ALU.mult))
                dve.tensor_tensor(dst, dst, bank[state_bank(i, c)][:, :], ALU.add).then_inc(h_updated, 1)

            decays(0)
            weighted_x(0)
            for i in range(TILES):
                r = rows(i)
                if i < 4:
                    decays(i + 1)
                mixing(i)
                if i < 4:
                    weighted_x(i + 1)
                dve.wait_ge(y_done, i + 1)
                ds = pp("dskip")
                for j in range(4):
                    ins = dve.scalar_tensor_tensor(mix[:, 4 + j, cols(i)], xc[:, j, cols(i)], ds[:, j:j + 1],
                                                   bank[4][:, j * P:j * P + r], ALU.mult, ALU.add)
                ins.then_inc(y_copied, 1)
                if i < 4:
                    new_state(i, 0)
            dve.wait_ge(y_copied, TILES)
            for j in range(4):
                dve.tensor_tensor(mix[:, 4 + j, :], mix[:, 4 + j, :], sz[:, j, :], ALU.mult).then_inc(yz_ready, 1)
            dve.wait_ge(xw_ready, TILES)
            segment_rows(0)
            segment_rows(1)
            dve.wait_ge(yz_ready, 4)
            norm(1)
            dve.wait_ge(x_reloaded, 16 * KT)
            for k in range(KT):
                n = N_FEAT + k
                dve.wait_ge(proj_done, n + 1)
                for x in range(2):
                    ins = dve.tensor_tensor(h[:, k, x * HALF:(x + 1) * HALF], h[:, k, x * HALF:(x + 1) * HALF],
                                            bank[2 * (n % 2) + x][:, 0:HALF], ALU.add)
                ins.then_inc(proj_dve, 1)
                new_state(4, k)
                if k + 2 < SEGS:
                    segment_rows(k + 2)
            new_state(4, SEGS - 1)
            dve.wait_ge(proj_dve, KT)
            norm(2)
            for k in range(1, KT, 2):
                dve.wait_ge(xh_ready, k + 1)
                dve.tensor_tensor(xl[:, k, :], xn[:, k, META:T], xh[:, k, :].bitcast(F32), ALU.subtract).then_inc(xl_ready, 1)
            def top16(out, idx, src, r, n, rep_x):
                vals = rep[0:r, rep_x, 0:n]
                link(dve.max(out[:, 0:8], src))
                dve.max_index(idx[:, 0:8], out[:, 0:8], src)
                link(dve.match_replace(vals, out[:, 0:8], src, -3.0e38))
                link(dve.max(out[:, 8:16], vals))
                dve.max_index(idx[:, 8:16], out[:, 8:16], vals)

            for i in range(TILES):
                r = peer_rows(i)
                dve.wait_ge(score_copied, 4 * (i + 1))
                for x in range(2 * PH):
                    half, hh = x // PH, x % PH
                    top16(v16[0:r, half, hh, :], i16[0:r, half, hh, :], s12[0:r, x, :], r, NK, x % 2)
                for hh in range(PH):
                    cnd = cand[0:r, :].rearrange("p (a b) -> p a b", a=TOPK)
                    link(dve.tensor_tensor(cnd, bc(v16[0:r, 0, hh, :], 2, TOPK), bc(v16[0:r, 1, hh, :], 1, TOPK), ALU.add))
                    top16(v16[0:r, 2, hh, :], i16[0:r, 2, hh, :], cand[0:r, :], r, TOPK * TOPK, hh % 2)
                dve.tensor_copy(f16[0:r, 0:2, :, :], i16[0:r, 0:2, :, :]).then_inc(top_sorted, 1)
                dve.wait_ge(top_sorted, i + 1)
                if i >= 1:
                    dve.wait_ge(e_turned, i)
                dve.tensor_tensor(e12[0:r, 2, :, :], v16[0:r, 2, :, :], bc(v16[0:r, 2, :, 0], 2, TOPK), ALU.subtract
                                  ).then_inc(sm_arg, 1)
                dve.tensor_scalar(j16[0:r, 0, :, :], i16[0:r, 2, :, :], 4, None, ALU.logical_shift_right)
                link(dve.tensor_scalar(j16[0:r, 1, :, :], i16[0:r, 2, :, :], TOPK - 1, None, ALU.bitwise_and))
                link(dve.tensor_copy(f16[0:r, 2:4, :, :], j16[0:r, :, :, :]))
                pk = pick[0:r, :, :, :].rearrange("p h k j -> p (h k) j")
                for x in range(2):
                    rank = f16[0:r, 2 + x, :, :].rearrange("p h k -> p (h k)")
                    link(dve.tensor_tensor(pk, bc(rank, 2, TOPK), bc(cc("iota16", r), 1, PH * TOPK), ALU.is_equal))
                    for hh in range(PH):
                        ins = dve.tensor_tensor(pick[0:r, hh, :, :], pick[0:r, hh, :, :], bc(f16[0:r, x, hh, :], 1, TOPK), ALU.mult)
                    link(ins)
                    link(dve.tensor_reduce(e12[0:r, x, :, :].rearrange("p h k -> p (h k)"), pk, AX.X, ALU.add))
                dve.wait_ge(sm_exp, i + 1)
                link(dve.tensor_reduce(den[0:r, 0, :], e12[0:r, 2, :, :], AX.X, ALU.add))
                link(dve.reciprocal(den[0:r, 1, :], den[0:r, 0, :]))
                dve.tensor_tensor(e12[0:r, 2, :, :], e12[0:r, 2, :, :], bc(den[0:r, 1, :], 2, TOPK), ALU.mult
                                  ).then_inc(e_ready, 1)
            dve.wait_ge(e_copied, TILES)
            for z in range(3):
                link(dve.tensor_copy(gparts[:, z, :], gT[:, :]))
                if z < 2:
                    link(dve.tensor_tensor(gT[:, :], gT[:, :], gparts[:, z, :], ALU.subtract))


            def one_hots(b, x, first=False):
                if not first:
                    dve.wait_ge(gate_done, (b - 1) * (TB // 4))
                e1, e2 = (bc(a[:, bass.ds(b * TB, TB)], 2, NK) for a in (e1T, e2T))
                index = bc(cc("iota"), 1, TB)
                dve.tensor_tensor(hotA[:, x, :, :], index, e1, ALU.is_equal).then_inc(one_hot_step, 1)
                dve.tensor_tensor(oneB[:, x, :, :], index, e2, ALU.is_equal)
                dve.wait_ge(one_hot_step, b + 1)
                for z in range(2):
                    ins = dve.tensor_tensor(oneA[:, x, z, :, :], hotA[:, x, :, :],
                                            bc(gparts[:, z, bass.ds(b * TB, TB)], 2, NK), ALU.mult)
                ins.then_inc(one_hot_ready, 1)

            one_hots(0, 0, first=True)
            one_hots(1, 1, first=True)
            with dve.Fori(1, NBLK // 2) as pair:
                b = pair * 2
                one_hots(b, 0)
                one_hots(b + 1, 1)

            def gate(n, y, j, par, g_round, hid_round, first=False):
                if j == 0:
                    dve.wait_ge(g_loaded[par], (g_round + 1) * 16)
                dve.wait_ge(hid_loaded[4 * y + j], (hid_round + 1) * 16)
                if not (first and j < 2):
                    dve.wait_ge(wlo_ready, n - 1)
                dve.tensor_tensor(sq[:, j % 2, 0:TP], xn[:, 4 * y + j, 0:TP], G[par][:, :, 4 * y + j], ALU.mult
                                  ).then_inc(gated, 1)

            def add_out(m, k):
                dve.wait_ge(acc_done, m * KT + (k + 1))
                for y in range(2):
                    ins = dve.tensor_tensor(h[:, k, META + y * PHALF:META + (y + 1) * PHALF], h[:, k, META + y * PHALF:META + (y + 1) * PHALF],
                                            bank[2 * ((k + 2) % 4) + y][:, 0:PHALF], ALU.add)
                ins.then_inc(acc_added, 1)

            def two_groups(q, first=False):
                for mm in range(4):
                    m = q * 4 + mm
                    for j in range(4):
                        gate(m * 4 + j, mm % 2, j, mm // 2, q, q * 2 + mm // 2, first=(first and mm == 0))
                        if not (first and mm == 0):
                            add_out(m - 1, j)
                        else:
                            dve.wait_ge(vhi_ready, j + 1)
                            dve.tensor_tensor(vsp0[:, j, 1, :], ring[:, j, :], vsp0[:, j, 0, :].bitcast(F32), ALU.subtract
                                              ).then_inc(vlo_ready, 1)
                    if not (first and mm == 0):
                        for k in range(4, KT):
                            add_out(m - 1, k)

            two_groups(0, first=True)
            with dve.Fori(1, NGRP // 2) as q:
                two_groups(q)
            for k in range(KT):
                add_out(NE // 4 - 1, k)
            dve.wait_ge(acc_added, NE // 4 * KT)
            norm(3)

        @block.gpsimd
        def _(pool):
            pool.wait_ge(proj_act, 2)
            for u in range(2 * TILES):
                i, p = u // 2, u % 2
                e = E_unit[u % 3][:, 0:rows(i) * C].rearrange("p (t c s) -> p t c s", t=C, s=C)
                pool.wait_ge(e_exp, u + 1)
                pool.tensor_tensor(e, e, bc(qT[:, p, cols(i)].rearrange("p (c t) -> p t c", t=C), 3, C), ALU.mult
                                   ).then_inc(e_q, 1)
            pool.wait_ge(khat_ready, 1)

            def chunk_rows(i):
                r, nch = rows(i), (P // C if i < 4 else SEGS)
                if i == 0:
                    pool.wait_ge(attn_used, 2 * TILES - 1)
                if i >= 2:
                    pool.wait_ge(local_done, (P // C) * (i - 1))
                pool.tensor_tensor(khm[i % 2][0:r, 0:nch, :], bc(khat[0:r, i, :], 1, nch),
                                   bc(cc("col_a" if i < 4 else "col_b", r), 2, GH * DK), ALU.mult).then_inc(khm_ready, 1)

            for i in range(TILES):
                chunk_rows(i)
            for i in range(TILES):
                r = rows(i)
                pool.wait_ge(ecb_ready, i + 1)
                if i >= 2:
                    pool.wait_ge(y_done, i - 1)
                pool.wait_ge(xc_ready, CT)
                for g in range(SG):
                    ins = pool.tensor_tensor(Ct[:, i % 2, 4 * g:4 * g + 4, 0:r], ecb[:, i % 2, 4 * g:4 * g + 4, 0:r],
                                             bc(xc[:, 6 + g, cols(i)], 1, 4), ALU.mult)
                ins.then_inc(ct_ready, 1)
            for k in range(0, KT, 2):
                pool.wait_ge(xh_ready, k + 1)
                pool.tensor_tensor(xl[:, k, :], xn[:, k, META:T], xh[:, k, :].bitcast(F32), ALU.subtract).then_inc(xl_ready, 1)
            for n in range(N_FEAT + KT + 1, N_PROJ):
                pool.wait_ge(qhi_ready, n - N_FEAT - KT)
                pool.tensor_tensor(usp[:, n % 2, 1, :], ring[:, n % 4, :], usp[:, n % 2, 0, :].bitcast(F32), ALU.subtract
                                   ).then_inc(qlo_ready, 1)

            def quad(q, b=None, x=0):
                for j in range(4):
                    pool.wait_ge(uhi_ready, q * 4 + (j + 1))
                    pool.tensor_tensor(usp[:, j % 2, 1, :], ring[:, j, :], usp[:, j % 2, 0, :].bitcast(F32), ALU.subtract
                                       ).then_inc(ulo_ready, 1)
                    if b is not None and j < 3:
                        y = (x + j) % 2
                        pool.wait_ge(one_hot_step, b + (j + 1))
                        pool.tensor_tensor(oneA[:, y, 2, :, :], hotA[:, y, :, :],
                                           bc(gparts[:, 2, bass.ds((b + j) * TB, TB)], 2, NK), ALU.mult
                                           ).then_inc(third_ready, 1)

            with pool.Fori(0, 18) as q:
                quad(q)
            with pool.Fori(0, 6) as it:
                for y in range(2):
                    quad(it * 2 + (18 + y), b=it * 6 + 3 * y, x=y)
            quad(30)
            quad(31)

            def split_rest(n, par, j, v=True):
                if v:
                    pool.wait_ge(vhi_ready, n + 1)
                    pool.tensor_tensor(vsp[par][:, j, 1, :], ring[:, j, :], vsp[par][:, j, 0, :].bitcast(F32),
                                       ALU.subtract).then_inc(vlo_ready, 1)
                pool.wait_ge(whi_ready, n + 1)
                pool.tensor_tensor(W[par][:, j, 1, :], sq[:, j % 2, 0:TP], W[par][:, j, 0, :].bitcast(F32),
                                   ALU.subtract).then_inc(wlo_ready, 1)

            for j in range(4):
                split_rest(j, 0, j, v=False)
            pool.wait_ge(vlo_ready, 4)
            for j in range(4):
                split_rest(4 + j, 1, j)
            with pool.Fori(1, NE // 8) as pair:
                for par in range(2):
                    for j in range(4):
                        split_rest(pair * 8 + (4 * par + j), par, j)


def feature_tiles(w):
    n = w.shape[1] // P
    return w.reshape(KT, P, n, P).transpose(2, 1, 0, 3).reshape(n, P, D)


def kernel(x_prompt, x_sample, state_gla, state_ssm, state_conv, meta_tokens, norm1_w, w_in, w_gk2, b_gk2, gla_norm_w,
           conv_w, conv_b, dt_bias, a_log, d_skip, ssd_norm_w, w_out, norm2_w, peer_wq, peer_k1, peer_k2, peer_u, peer_v,
           final_norm_w):
    import concourse.bacc as bacc
    from concourse.bass_utils import run_bass_kernel_spmd

    x = np.concatenate([np.asarray(meta_tokens), np.asarray(x_prompt)[0], np.asarray(x_sample).reshape(NSEQ * SLEN, D)])
    w = np.asarray(w_in)[0]
    at = np.cumsum([0, GH * DK, GH * DK, GH * DV, GH * DV, RANK, SH * HD, CONVD, SH])
    q, k, v, g, f, z, xbc, dtw = (w[:, at[i]:at[i + 1]] for i in range(8))
    per_feature = lambda a: np.asarray(a).reshape(-1, P).T
    params = {
        "norm1": per_feature(norm1_w), "norm2": per_feature(norm2_w), "final": per_feature(final_norm_w),
        "gla_w": per_feature(gla_norm_w), "ssd_w": per_feature(ssd_norm_w),
        "conv_w": np.asarray(conv_w)[0].reshape(CONV, CT, P).transpose(2, 1, 0).reshape(P, CT * CONV),
        "conv_b": per_feature(conv_b), "dskip": per_feature(np.repeat(np.asarray(d_skip)[0], HD)),
        "a_log": np.tile(np.asarray(a_log), (P, 1)), "dt_bias": np.tile(np.asarray(dt_bias), (P, 1)),
    }
    ins = {
        "xT": x.reshape(T, KT, P).transpose(2, 1, 0),
        "const": constants(),
        "param": np.concatenate([params[n] for n, _ in PARAM_PARTS], axis=1),
        "rows": np.asarray(b_gk2),
        "wsmall": np.concatenate([f, np.zeros((D, DT_ROW - RANK), np.float32), dtw], axis=1).reshape(KT, P, DT_ROW + SH).transpose(1, 0, 2),
        "w_gk2": np.asarray(w_gk2)[0],
        "wv": v.reshape(KT, P, GH * DV).transpose(1, 0, 2),
        "wproj": np.concatenate([feature_tiles(np.concatenate([q, k, g, z, xbc], axis=1)),
                                 feature_tiles(np.asarray(w_out)[0]), feature_tiles(np.asarray(peer_wq)[0])]),
        "keys": np.concatenate([np.asarray(peer_k1)[0].T, np.asarray(peer_k2)[0].T]),
        "s_gla": np.asarray(state_gla)[0].reshape(NSEQ, NP, 2, DK, DV).transpose(2, 3, 0, 1, 4).reshape(P, NSEQ, NP, DV),
        "s_ssm": np.asarray(state_ssm)[0].transpose(3, 0, 1, 2).reshape(DS, NSEQ, SH * HD),
        "s_conv": np.asarray(state_conv)[0].reshape(NSEQ, CONV - 1, CT, P).transpose(3, 2, 0, 1),
        "u": np.asarray(peer_u)[0].reshape(NK, NK, KT, P).transpose(1, 3, 2, 0).reshape(NK, P, D),
        "v": np.asarray(peer_v)[0].reshape(NK, NGRP, GRP, D),
    }
    outs = {
        "yT": (P, KT, T), "gla_p": (P, NP, DV), "gla_s": (P, NSEQ, NP, DV), "ssm_p": (P, SH * HD),
        "ssm_s": (P, NSEQ, SH * HD), "conv_p": (P, CT, CONV - 1), "conv_s": (P, CT, NSEQ, CONV - 1),
    }
    nc = bacc.Bacc("TRN2", target_bir_lowering=False, num_devices=1)
    arrays, di, do = {}, {}, {}
    for name, a in ins.items():
        arrays[f"in_{name}"] = np.ascontiguousarray(a)
        di[name] = nc.dram_tensor(f"in_{name}", a.shape, F32, kind="ExternalInput").ap()
    for name, shape in outs.items():
        do[name] = nc.dram_tensor(f"out_{name}", shape, F32, kind="ExternalOutput").ap()
    build(nc, di, do)
    r = run_bass_kernel_spmd(nc, [arrays], core_ids=[0]).results[0]
    r = {name: np.asarray(r[f"out_{name}"]) for name in outs}
    y = r["yT"].transpose(2, 1, 0).reshape(T, D)
    heads = lambda a: a.reshape(2, DK, -1, NP, DV).transpose(2, 3, 0, 1, 4).reshape(1, -1, GH, DK, DV)
    ssm = lambda a: a.reshape(DS, -1, SH, HD).transpose(1, 2, 3, 0)[None]
    conv = lambda a: a.reshape(P, CT, -1, CONV - 1).transpose(2, 3, 1, 0).reshape(1, -1, CONV - 1, CONVD)
    return (y[META:NPROMPT][None], y[NPROMPT:].reshape(NSEQ, SLEN, D),
            heads(r["gla_p"]), ssm(r["ssm_p"]), conv(r["conv_p"]),
            heads(r["gla_s"]), ssm(r["ssm_s"]), conv(r["conv_s"]))
```
